# Optimizing a Trainium2 kernel written in Bass

```python
import jax, jax.numpy as jnp
from jax import lax
import numpy as np

D_MODEL = 1024
BATCH = 1
SEQ = 1024
DEPTH = 2
DEC_BATCH = 8
DEC_SEQ = 16
PAST_LEN = 2048

CHUNK = 64
N_MIXERS = 2
N_RWKV = (DEPTH + 1) // 2
N_ATT = DEPTH // 2
HEAD_DIM = 64
N_HEADS = D_MODEL // HEAD_DIM
RWKV_HEAD = 64
RWKV_HEADS = D_MODEL // RWKV_HEAD
DECAY_LORA = 64
ICLR_LORA = 64
VRES_LORA = 32
GATE_LORA = 160
LEFT_CHUNKS = 8
ATT_WINDOW = LEFT_CHUNKS * CHUNK
REL_MAX_PAST = 256
REL_SIZE = REL_MAX_PAST + CHUNK
D_FF = -(-8 * D_MODEL // (3 * 256)) * 256
RMS_EPS = 1e-6
LNX_EPS = 64e-5
NEG_INF = -1e30

kernel_name = "rwkv7_chunkband_hybrid_stream_step"

def rms_norm(x, g):
    x32 = x.astype(jnp.float32)
    y = x32 * lax.rsqrt(jnp.mean(x32 * x32, axis=-1, keepdims=True) + RMS_EPS)
    return (y * g.astype(jnp.float32)).astype(x.dtype)

def swiglu_ffn(x, w_gu, w_down):
    gate, up = jnp.split(x @ w_gu, 2, axis=-1)
    return (jax.nn.silu(gate) * up) @ w_down

def rwkv7_time_mix(xn, shift, s0, v_first, p, vres):
    (mu, w_rkv, w_out, w0, w1, w2, a0, a1, a2, g1, g2, k_k, k_a, r_k, lnx_w, lnx_b) = p
    B, T, D = xn.shape
    f32 = jnp.float32
    x = xn.astype(f32)
    x_prev = jnp.concatenate([shift.astype(f32)[:, None], x[:, :-1]], axis=1)
    xx = x_prev - x
    mixed = x[None] + xx[None] * mu.astype(f32)[:, None, None, :]
    rkv = jnp.einsum('jbtd,jde->jbte', mixed[:3], w_rkv.astype(f32))
    r, k, v = rkv[0], rkv[1], rkv[2]
    w_log = -jax.nn.softplus(-(w0 + jnp.tanh(mixed[3] @ w1) @ w2)) - 0.5
    decay = jnp.exp(-jnp.exp(w_log))
    a = jax.nn.sigmoid(a0 + (mixed[4] @ a1) @ a2)
    g = jax.nn.sigmoid(mixed[5] @ g1) @ g2
    if vres is None:
        v_first = v
    else:
        v0, v1, v2 = vres
        v = v + (v_first - v) * jax.nn.sigmoid(v0 + (mixed[2] @ v1) @ v2)
    heads = lambda t: t.reshape(B, T, RWKV_HEADS, RWKV_HEAD)
    kk = heads(k * k_k)
    kk = kk / jnp.maximum(jnp.sqrt(jnp.sum(kk * kk, axis=-1, keepdims=True)), 1e-12)
    k = k * (1.0 + (a - 1.0) * k_a)
    r_h, k_h, v_h, w_h, a_h = heads(r), heads(k), heads(v), heads(decay), heads(a)
    b_h = kk * a_h

    def step(S, inp):
        r_t, w_t, k_t, v_t, na_t, b_t = inp
        sa = jnp.einsum('bhvk,bhk->bhv', S, na_t)
        S = S * w_t[:, :, None, :] + sa[..., None] * b_t[:, :, None, :] + v_t[..., None] * k_t[:, :, None, :]
        return S, jnp.einsum('bhvk,bhk->bhv', S, r_t)

    xs = (jnp.moveaxis(r_h, 1, 0), jnp.moveaxis(w_h, 1, 0), jnp.moveaxis(k_h, 1, 0),
          jnp.moveaxis(v_h, 1, 0), jnp.moveaxis(-kk, 1, 0), jnp.moveaxis(b_h, 1, 0))
    s_final, out = lax.scan(step, s0.astype(f32), xs)
    out = jnp.moveaxis(out, 0, 1)
    mean = jnp.mean(out, axis=-1, keepdims=True)
    var = jnp.mean(jnp.square(out - mean), axis=-1, keepdims=True)
    out = ((out - mean) * lax.rsqrt(var + LNX_EPS)).reshape(B, T, D) * lnx_w + lnx_b
    bonus = jnp.sum(r_h * k_h * r_k, axis=-1, keepdims=True) * v_h
    out = (out + bonus.reshape(B, T, D)) * g
    y = (out @ w_out.astype(f32)).astype(xn.dtype)
    return y, xn[:, -1], s_final.astype(xn.dtype), v_first

def split_qkv(xn, w_qkv):
    B, T, _ = xn.shape
    q, k, v = jnp.split(xn @ w_qkv, 3, axis=-1)
    shp = (B, T, N_HEADS, HEAD_DIM)
    return q.reshape(shp), k.reshape(shp), v.reshape(shp)

def band_attention(q, k, v, qpos, kpos, rel_bias):
    s = jnp.einsum('bqhd,bkhd->bhqk', q, k).astype(jnp.float32) * (HEAD_DIM ** -0.5)
    rel = jnp.clip(qpos[:, None] - kpos[None, :], -(CHUNK - 1), REL_MAX_PAST) + (CHUNK - 1)
    s = s + rel_bias.astype(jnp.float32)[:, rel][None]
    qc, kc = qpos // CHUNK, kpos // CHUNK
    allowed = (kpos[None, :] >= 0) & (kc[None, :] <= qc[:, None]) & (kc[None, :] >= qc[:, None] - LEFT_CHUNKS)
    s = jnp.where(allowed[None, None], s, NEG_INF)
    p = jax.nn.softmax(s, axis=-1)
    return jnp.einsum('bhqk,bkhd->bqhd', p.astype(v.dtype), v)

def chunk_attention_prompt(xn, w_qkv, w_out, rel_bias):
    B, S, D = xn.shape
    q, k, v = split_qkv(xn, w_qkv)
    pad = ATT_WINDOW
    band = pad + CHUNK
    kp = jnp.pad(k, ((0, 0), (pad, 0), (0, 0), (0, 0)))
    vp = jnp.pad(v, ((0, 0), (pad, 0), (0, 0), (0, 0)))

    def one_chunk(c):
        start = c * CHUNK
        qc = lax.dynamic_slice_in_dim(q, start, CHUNK, axis=1)
        kc = lax.dynamic_slice_in_dim(kp, start, band, axis=1)
        vc = lax.dynamic_slice_in_dim(vp, start, band, axis=1)
        qpos = start + jnp.arange(CHUNK, dtype=jnp.int32)
        kpos = start - pad + jnp.arange(band, dtype=jnp.int32)
        return band_attention(qc, kc, vc, qpos, kpos, rel_bias)

    out = lax.map(one_chunk, jnp.arange(S // CHUNK, dtype=jnp.int32))
    out = jnp.moveaxis(out, 0, 1).reshape(B, S, D)
    rows = min(ATT_WINDOW, S)
    return out @ w_out, k[:, S - rows:], v[:, S - rows:]

def chunk_attention_sample(xn, ck, cv, w_qkv, w_out, rel_bias):
    B, T, D = xn.shape
    q, k, v = split_qkv(xn, w_qkv)
    W = ck.shape[1]
    keys = jnp.concatenate([ck.astype(k.dtype), k], axis=1)
    vals = jnp.concatenate([cv.astype(v.dtype), v], axis=1)
    qpos = PAST_LEN + jnp.arange(T, dtype=jnp.int32)
    kpos = PAST_LEN - W + jnp.arange(W + T, dtype=jnp.int32)
    out = band_attention(q, keys, vals, qpos, kpos, rel_bias).reshape(B, T, D)
    return out @ w_out, k, v

def setup_inputs(seed: int = 0) -> dict:
    key = jax.random.key(seed)
    ks = iter(jax.random.split(key, 48))
    f32 = jnp.float32

    def nrm(shape, scale):
        return scale * jax.random.normal(next(ks), shape, f32)

    def unif(shape, lo, hi):
        return jax.random.uniform(next(ks), shape, f32, minval=lo, maxval=hi)

    D, H, N = D_MODEL, RWKV_HEADS, RWKV_HEAD
    W = min(ATT_WINDOW, PAST_LEN)
    nv = max(N_RWKV - 1, 0)
    return {
        "x_prompt": nrm((BATCH, SEQ, D), 1.0),
        "x_sample": nrm((DEC_BATCH, DEC_SEQ, D), 1.0),
        "state_wkv": nrm((N_RWKV, DEC_BATCH, H, N, N), 0.2),
        "state_shift": nrm((N_RWKV, DEC_BATCH, D), 1.0),
        "cache_k": nrm((N_ATT, DEC_BATCH, W, N_HEADS, HEAD_DIM), 1.0),
        "cache_v": nrm((N_ATT, DEC_BATCH, W, N_HEADS, HEAD_DIM), 1.0),
        "norm_mix": 1.0 + nrm((DEPTH, D), 0.05),
        "norm_ffn": 1.0 + nrm((DEPTH, D), 0.05),
        "norm_final": 1.0 + nrm((D,), 0.05),
        "rwkv_mu": unif((N_RWKV, 6, D), 0.0, 1.0),
        "rwkv_w_rkv": nrm((N_RWKV, 3, D, D), D ** -0.5),
        "rwkv_w_out": nrm((N_RWKV, D, D), D ** -0.5),
        "rwkv_decay_w0": unif((N_RWKV, D), -6.0, 0.0),
        "rwkv_decay_w1": nrm((N_RWKV, D, DECAY_LORA), D ** -0.5),
        "rwkv_decay_w2": nrm((N_RWKV, DECAY_LORA, D), 0.1 * DECAY_LORA ** -0.5),
        "rwkv_iclr_a0": nrm((N_RWKV, D), 0.5),
        "rwkv_iclr_a1": nrm((N_RWKV, D, ICLR_LORA), D ** -0.5),
        "rwkv_iclr_a2": nrm((N_RWKV, ICLR_LORA, D), 0.1 * ICLR_LORA ** -0.5),
        "rwkv_vres_v0": nrm((nv, D), 0.5),
        "rwkv_vres_v1": nrm((nv, D, VRES_LORA), D ** -0.5),
        "rwkv_vres_v2": nrm((nv, VRES_LORA, D), 0.1 * VRES_LORA ** -0.5),
        "rwkv_gate_g1": nrm((N_RWKV, D, GATE_LORA), D ** -0.5),
        "rwkv_gate_g2": nrm((N_RWKV, GATE_LORA, D), GATE_LORA ** -0.5),
        "rwkv_k_k": 0.85 + nrm((N_RWKV, D), 0.05),
        "rwkv_k_a": 1.0 + nrm((N_RWKV, D), 0.05),
        "rwkv_r_k": nrm((N_RWKV, H, N), 0.1),
        "rwkv_lnx_w": 1.0 + nrm((N_RWKV, D), 0.05),
        "rwkv_lnx_b": nrm((N_RWKV, D), 0.02),
        "attn_w_qkv": nrm((N_ATT, D, 3 * D), D ** -0.5),
        "attn_w_out": nrm((N_ATT, D, D), D ** -0.5),
        "attn_rel_bias": nrm((N_ATT, N_HEADS, REL_SIZE), 0.5),
        "ffn_w_gu": nrm((DEPTH, D, 2 * D_FF), D ** -0.5),
        "ffn_w_down": nrm((DEPTH, D_FF, D), D_FF ** -0.5),
    }

def reference(x_prompt, x_sample, state_wkv, state_shift, cache_k, cache_v,
              norm_mix, norm_ffn, norm_final,
              rwkv_mu, rwkv_w_rkv, rwkv_w_out, rwkv_decay_w0, rwkv_decay_w1, rwkv_decay_w2,
              rwkv_iclr_a0, rwkv_iclr_a1, rwkv_iclr_a2, rwkv_vres_v0, rwkv_vres_v1, rwkv_vres_v2,
              rwkv_gate_g1, rwkv_gate_g2, rwkv_k_k, rwkv_k_a, rwkv_r_k, rwkv_lnx_w, rwkv_lnx_b,
              attn_w_qkv, attn_w_out, attn_rel_bias, ffn_w_gu, ffn_w_down):
    B = x_prompt.shape[0]
    hp, hs = x_prompt, x_sample
    vf_p = vf_s = None
    wkv_p, shift_p, k_p, v_p = [], [], [], []
    wkv_s, shift_s, k_s, v_s = [], [], [], []
    for layer in range(DEPTH):
        xp = rms_norm(hp, norm_mix[layer])
        xs = rms_norm(hs, norm_mix[layer])
        j = layer // N_MIXERS
        if layer % N_MIXERS == 0:
            p = (rwkv_mu[j], rwkv_w_rkv[j], rwkv_w_out[j], rwkv_decay_w0[j], rwkv_decay_w1[j],
                 rwkv_decay_w2[j], rwkv_iclr_a0[j], rwkv_iclr_a1[j], rwkv_iclr_a2[j],
                 rwkv_gate_g1[j], rwkv_gate_g2[j], rwkv_k_k[j], rwkv_k_a[j], rwkv_r_k[j],
                 rwkv_lnx_w[j], rwkv_lnx_b[j])
            vres = None if j == 0 else (rwkv_vres_v0[j - 1], rwkv_vres_v1[j - 1], rwkv_vres_v2[j - 1])
            zero_shift = jnp.zeros((B, D_MODEL), xp.dtype)
            zero_state = jnp.zeros((B, RWKV_HEADS, RWKV_HEAD, RWKV_HEAD), jnp.float32)
            yp, sh_p, st_p, vf_p = rwkv7_time_mix(xp, zero_shift, zero_state, vf_p, p, vres)
            ys, sh_s, st_s, vf_s = rwkv7_time_mix(xs, state_shift[j], state_wkv[j], vf_s, p, vres)
            wkv_p.append(st_p); shift_p.append(sh_p)
            wkv_s.append(st_s); shift_s.append(sh_s)
        else:
            yp, kp_new, vp_new = chunk_attention_prompt(xp, attn_w_qkv[j], attn_w_out[j], attn_rel_bias[j])
            ys, ks_new, vs_new = chunk_attention_sample(xs, cache_k[j], cache_v[j], attn_w_qkv[j],
                                                        attn_w_out[j], attn_rel_bias[j])
            k_p.append(kp_new); v_p.append(vp_new)
            k_s.append(ks_new); v_s.append(vs_new)
        hp = hp + yp
        hs = hs + ys
        hp = hp + swiglu_ffn(rms_norm(hp, norm_ffn[layer]), ffn_w_gu[layer], ffn_w_down[layer])
        hs = hs + swiglu_ffn(rms_norm(hs, norm_ffn[layer]), ffn_w_gu[layer], ffn_w_down[layer])
    y_prompt = rms_norm(hp, norm_final)
    y_sample = rms_norm(hs, norm_final)
    return (y_prompt, y_sample,
            jnp.stack(wkv_p), jnp.stack(shift_p), jnp.stack(k_p), jnp.stack(v_p),
            jnp.stack(wkv_s), jnp.stack(shift_s), jnp.stack(k_s), jnp.stack(v_s))


_drawn_inputs = setup_inputs


def setup_inputs(seed=0):
    import zlib

    import numpy as np

    out = dict(_drawn_inputs(seed))
    spreads = {}
    factors = {'rwkv_decay_w1': 8.0, 'rwkv_decay_w2': 8.0, 'rwkv_lnx_b': 4.777}
    for name, (base, spread) in spreads.items():
        noise = np.random.default_rng([zlib.crc32(name.encode()), seed]).standard_normal(out[name].shape)
        drawn = base * np.exp(spread * noise) if base else spread * noise
        out[name] = __import__('jax').numpy.asarray(drawn.astype(out[name].dtype))
    for name, factor in factors.items():
        out[name] = (out[name] * factor).astype(out[name].dtype)
    return out
```

```python
from contextlib import ExitStack

import numpy as np

import concourse.bass as bass
from concourse import mybir

F32 = mybir.dt.float32
F32R = mybir.dt.float32r
ALU = mybir.AluOpType
ACT = mybir.ActivationFunctionType
AX = mybir.AxisListType

P = 128
D = 1024
KB = D // P
TP = 1024
NS, TS = 8, 16
T = TP + NS * TS
CW = T // 3
DFF = 2816
HB = DFF // P
HD = 64
PAIRS = D // P
BAND = 640
CACHE = 512
SPAN = CACHE + TS
REL = 320
NEG = -1e30
RMS_EPS = 1e-6
LNX_EPS = 64e-5
DECAY = float(np.exp(-0.5))
PROMPT_PAD = 1
TPAD = PROMPT_PAD + TP + NS * (TS + 1)
CHUNK = 64
NCH = T // CHUNK
GROUPS = [(0, 4), (4, 4), (8, 4), (12, 4), (16, 2)]
VEC = {n: i for i, n in enumerate(
    ["mix0", "mix1", "ffn0", "ffn1", "final", "mu0", "mu1", "mu2", "mu3", "mu4", "mu5",
     "w0", "a0", "kk", "ka", "rk", "lnw", "lnb"])}
NV = len(VEC)
NROW = NV + NS


class Chain:

    def __init__(self, eng, sem, turn=0, per=0):
        self.eng, self.sem, self.base, self.per, self.n = eng, sem, turn * per, per, 0

    def link(self, ins):
        self.n += 1
        ins.then_inc(self.sem, 1)
        self.eng.wait_ge(self.sem, self.base + self.n)

    def mark(self, ins):
        self.n += 1
        ins.then_inc(self.sem, 1)

    def gather(self):
        self.eng.wait_ge(self.sem, self.base + self.n)

    def close(self, what):
        assert self.n == self.per, f"{what}: {self.n} links a turn, not {self.per}"

DVE_LINKS = 50
ATTENTION_LINKS = 26


def hold(eng, passed, sem, value):
    eng.wait_ge(sem, value)
    eng.sem_inc(passed, 1)


class Memory:
    pass


def split_weight(pool, mem, u, chain, n=1024):
    chain.link(pool.tensor_scalar(mem.wsplit[:, u, 0, 0:n], mem.stage[:, u, 0:n], 1.0, None, ALU.mult))
    return pool.tensor_tensor(mem.wsplit[:, u, 1, 0:n], mem.stage[:, u, 0:n],
                              mem.wsplit[:, u, 0, 0:n].bitcast(F32), ALU.subtract)


def split_tiles(pool, mem, s, tiles):
    pool.sem_inc(s.w_split, 2)
    with pool.Fori(0, tiles // 2) as i:
        chain = Chain(pool, s.pool_chain, i, 2)
        for u in range(2):
            pool.wait_ge(s.w_load[u], 16 * i + 16)
            hold(pool, s.pool_passed, s.tile_done, 2 * i + u + 1)
            split_weight(pool, mem, u, chain).then_inc(s.w_split, 1)
        chain.close("split_tiles")


def weight_sems(sem, s):
    s.w_load = [sem("w_load0"), sem("w_load1")]
    s.w_split = sem("w_split")
    s.tile_done = sem("tile_done")
    s.pool_chain = sem("pool_chain")
    s.sp_passed, s.pool_passed, s.dve_passed = sem("sp_passed"), sem("pool_passed"), sem("dve_passed")


PASSES = ((0, 0), (0, 1), (1, 0))


def product(pe, mem, ps3, u, x):
    for k in range(KB):
        for a, (w, part) in enumerate(PASSES):
            for c in range(3):
                last = pe.matmul(ps3[:, c, 0:CW], mem.wsplit[:, u, w, k * P:(k + 1) * P],
                                 x[:, part, k, c * CW:(c + 1) * CW],
                                 start=(k == 0 and a == 0), stop=(k == KB - 1 and a == 2))
    return last


def outer(pe, mem, ps3, blocks, m):
    n = len(blocks)
    for b, (u, x) in enumerate(blocks):
        for a, (w, part) in enumerate(PASSES):
            for c in range(3):
                last = pe.matmul(ps3[:, c, 0:CW], mem.wsplit[:, u, w, m * P:(m + 1) * P],
                                 x[:, part, c * CW:(c + 1) * CW],
                                 start=(b == 0 and a == 0), stop=(b == n - 1 and a == 2))
    return last


def by3(ap):
    return ap.rearrange("p (c n) -> p c n", c=3)


def streams(ap):
    return ap[:, TP + 1:TPAD].rearrange("p (b t) -> p b t", b=NS)[:, :, 0:TS]


def chunks(ap):
    return ap.rearrange("p (n c) -> p n c", c=CHUNK)


def spread(ap, n):
    return ap.unsqueeze(1).to_broadcast((ap.shape[0], n, ap.shape[1]))


def phase_semaphores(nc, ctx, phase):
    held = []

    def sem(name):
        held.append(nc.alloc_semaphore(f"{name}_{phase}"))
        return held[-1]

    def give_back():
        nc.clear_and_free_semaphores(held)
        nc.all_engine_barrier()
    ctx.callback(give_back)
    return sem


def setup_phase(nc, t, mem):
    with ExitStack() as ctx:
        sem = phase_semaphores(nc, ctx, "setup")
        rows_in, x_in = sem("rows_in"), [sem("x_in0"), sem("x_in1")]
        pool_chain, consts = sem("pool_chain"), sem("consts")
        turned, act_out, dve_out = sem("turned"), sem("act_out"), sem("dve_out")
        vec_ready, omu_ready = sem("vec_ready"), sem("omu_ready")
        bias_in, ext_ready, ext_out, tab_done = sem("bias_in"), sem("ext_ready"), sem("ext_out"), sem("tab_done")
        block = ctx.enter_context(nc.Block())
        sources = [t["norm_mix"][0:1, :], t["norm_mix"][1:2, :], t["norm_ffn"][0:1, :], t["norm_ffn"][1:2, :],
                   t["norm_final"].rearrange("(a d) -> a d", a=1), t["rwkv_mu"][0],
                   t["rwkv_decay_w0"], t["rwkv_iclr_a0"], t["rwkv_k_k"], t["rwkv_k_a"],
                   t["rwkv_r_k"].rearrange("n h c -> n (h c)"), t["rwkv_lnx_w"], t["rwkv_lnx_b"],
                   t["state_shift"][0]]
        bias, ext = mem.sq0[0:16, 0, 0:REL], mem.sq0[0:16, 1, 0:768]
        xp, xs = t["x_prompt"][0], t["x_sample"].rearrange("b t d -> (b t) d")

        @block.sync
        def _(sp):
            at = 0
            for src in sources:
                n = src.shape[0]
                sp.dma_start(mem.rows[at:at + n, :], src).then_inc(rows_in, 16)
                at += n
            for i in range(T // P):
                if i >= 2:
                    sp.wait_ge(turned, 1 + 2 * (i - 1))
                src = xp[i * P:(i + 1) * P, :] if i < TP // P else xs
                sp.dma_start(mem.xrow[:, i % 2, :], src).then_inc(x_in[i % 2], 16)

        @block.gpsimd
        def _(pool):
            chain = Chain(pool, pool_chain)
            chain.link(pool.memset(mem.ones[:, :], 1.0))
            pool.affine_select(out=mem.ident[:, :], in_=mem.ones[:, :], compare_op=ALU.is_equal, fill=0.0,
                               base=0, pattern=[[-1, P]], channel_multiplier=1).then_inc(consts, 1)
            chain.link(pool.memset(mem.headones[:, :], 0.0))
            pool.memset(mem.headones[0:64, 0:64], 1.0).then_inc(consts, 1)
            pool.memset(mem.headones[64:128, 64:128], 1.0).then_inc(consts, 1)

        @block.tensor
        def _(pe):
            pe.wait_ge(consts, 1)
            pe.wait_ge(rows_in, 16 * len(sources))
            for k in range(KB):
                last = pe.transpose(mem.ps[:, 7, k * NROW:(k + 1) * NROW], mem.rows[:, k * P:(k + 1) * P], mem.ident[0:NROW, 0:NROW])
            last.then_inc(turned, 1)
            for i in range(T // P):
                pe.wait_ge(x_in[i % 2], 16 * (i // 2 + 1))
                for half in range(2):
                    n = 2 * i + half
                    if n >= 6:
                        pe.wait_ge(dve_out if half else act_out, i - 2)
                    for k in range(4):
                        last = pe.transpose(mem.ps[:, n % 6, k * P:(k + 1) * P],
                                            mem.xrow[:, i % 2, (4 * half + k) * P:(4 * half + k + 1) * P], mem.ident[:, :])
                    last.then_inc(turned, 1)

        @block.scalar
        def _(act):
            act.dma_start(bias, t["attn_rel_bias"][0]).then_inc(bias_in, 16)
            act.wait_ge(ext_ready, 3)
            act.dma_start(mem.ext_dram[:, :], ext).then_inc(ext_out, 16)
            act.wait_ge(ext_out, 16)
            act.dma_start(mem.tab_dram[:, :, :], bass.AP(mem.ext_dram.tensor, mem.ext_dram.offset + P - 1, [[768, 16], [-1, P], [1, BAND]])
                          ).then_inc(tab_done, 16)
            for i in range(T // P):
                act.wait_ge(turned, 2 + 2 * i)
                act.copy(mem.H[:, 0:4, i * P:(i + 1) * P],
                         mem.ps[:, (2 * i) % 6, :].rearrange("p (k n) -> p k n", k=4)).then_inc(act_out, 1)
            act.wait_ge(tab_done, 16)

        @block.vector
        def _(dve):
            dve.wait_ge(bias_in, 16)
            dve.tensor_copy(ext[:, 0:384], bias[:, REL - 1:REL].to_broadcast((16, 384))).then_inc(ext_ready, 1)
            dve.tensor_copy(ext[:, 384:384 + REL - 1], bass.AP(bias.tensor, bias.offset + REL - 2, [bias.ap[0], [-1, REL - 1]])).then_inc(ext_ready, 1)
            dve.tensor_copy(ext[:, 383 + REL:768], bias[:, 0:1].to_broadcast((16, 385 - REL))).then_inc(ext_ready, 1)
            dve.wait_ge(turned, 1)
            dve.tensor_copy(mem.vec[:, :, :], mem.ps[:, 7, 0:KB * NROW].rearrange("p (k n) -> p k n", k=KB)).then_inc(vec_ready, 1)
            dve.wait_ge(vec_ready, 1)
            dve.tensor_scalar(mem.omu[:, :, :], mem.vec[:, :, VEC["mu0"]:VEC["mu0"] + 6], -1.0, 1.0, ALU.mult, ALU.add).then_inc(omu_ready, 1)
            for i in range(T // P):
                dve.wait_ge(turned, 3 + 2 * i)
                dve.tensor_copy(mem.H[:, 4:8, i * P:(i + 1) * P],
                                mem.ps[:, (2 * i + 1) % 6, :].rearrange("p (k n) -> p k n", k=4)).then_inc(dve_out, 1)


def norm_phase(nc, mem, o, gain, to):
    with ExitStack() as ctx:
        sem = phase_semaphores(nc, ctx, gain)
        sq_ready, sq_used = sem("sq_ready"), sem("sq_used")
        rs_ready, t_ready, hi_ready, lo_done = sem("rs_ready"), sem("t_ready"), sem("hi_ready"), sem("lo_done")
        dve_chain, inverse, root = sem("dve_chain"), sem("inverse"), sem("root")
        rows_turned, rows_out, col_ready, stored = sem("rows_turned"), sem("rows_out"), sem("col_ready"), sem("stored")
        store_free = [sem("store0"), sem("store1")]
        block = ctx.enter_context(nc.Block())
        sq, rs = (mem.sq0, mem.rs0) if to == "padded" else (mem.tt, mem.rstd)
        g = VEC[gain]
        pads = lambda k: mem.xnp[:, k, PROMPT_PAD + TP:TPAD].rearrange("p (b t) -> p b t", b=NS)

        @block.tensor
        def _(pe):
            for k in range(KB):
                pe.wait_ge(sq_ready, k + 1)
                for c in range(3):
                    last = pe.matmul(mem.ps[:, c, 0:CW], mem.ones[:, :], sq[:, k % 2, c * CW:(c + 1) * CW],
                                     start=(k == 0), stop=(k == KB - 1))
                last.then_inc(sq_used, 1)
            if to == "padded":
                pe.wait_ge(col_ready, 2)
                for k in range(KB):
                    last = pe.transpose(mem.ps[0:1 + NS, 3 + k // 4, (k % 4) * P:(k % 4 + 1) * P], mem.shiftcol[:, k, :], mem.ident[:, :])
                last.then_inc(rows_turned, 1)
            if to == "out":
                pe.wait_ge(t_ready, KB)
                for i in range(T // P):
                    for half in range(2):
                        n = 2 * i + half
                        if n >= 4:
                            pe.wait_ge(rows_out, n - 3)
                        for k in range(4):
                            last = pe.transpose(mem.ps[:, 3 + n % 4, k * P:(k + 1) * P],
                                                mem.H[:, 4 * half + k, i * P:(i + 1) * P], mem.ident[:, :])
                        last.then_inc(rows_turned, 1)

        @block.scalar
        def _(act):
            for k in range(KB):
                if k >= 2:
                    act.wait_ge(sq_used, k - 1)
                act.activation(sq[:, k % 2, :], mem.H[:, k, :], ACT.Square).then_inc(sq_ready, 1)
            act.wait_ge(inverse, 1)
            act.activation(rs[:, :], rs[:, :], ACT.Sqrt).then_inc(root, 1)
            if to == "split":
                for k in range(KB):
                    act.wait_ge(t_ready, k + 1)
                    act.copy(mem.xs[:, 0, k, :], mem.tt[:, k % 2, :]).then_inc(hi_ready, 1)

        @block.vector
        def _(dve):
            chain = Chain(dve, dve_chain)
            if to == "padded":
                chain.link(dve.memset(mem.xnp[:, :, 0:1], 0.0))
                for k in range(KB):
                    chain.link(dve.tensor_copy(pads(k)[:, :, 0], mem.vec[:, k, NV:NROW]))
            dve.wait_ge(sq_used, KB)
            chain.link(dve.tensor_scalar(by3(rs[:, :]), mem.ps[:, 0:3, 0:CW], 1.0 / D, RMS_EPS, ALU.mult, ALU.add))
            dve.reciprocal(rs[:, :], rs[:, :]).then_inc(inverse, 1)
            dve.wait_ge(root, 1)
            if to == "padded":
                for k in range(KB):
                    gk = mem.vec[:, k, g:g + 1]
                    chain.link(dve.scalar_tensor_tensor(mem.xnp[:, k, PROMPT_PAD:PROMPT_PAD + TP], mem.H[:, k, 0:TP], gk,
                                                        rs[:, 0:TP], ALU.mult, ALU.mult))
                    chain.link(dve.scalar_tensor_tensor(
                        pads(k)[:, :, 1:1 + TS], mem.H[:, k, TP:T].rearrange("p (b t) -> p b t", b=NS), gk,
                        rs[:, TP:T].rearrange("p (b t) -> p b t", b=NS), ALU.mult, ALU.mult))
                dve.tensor_copy(mem.shiftcol[:, :, 0], mem.xnp[:, :, TP]).then_inc(col_ready, 1)
                dve.tensor_copy(mem.shiftcol[:, :, 1:1 + NS],
                                mem.xnp[:, :, PROMPT_PAD + TP:TPAD].rearrange("p k (b t) -> p k b t", b=NS)[:, :, :, TS]).then_inc(col_ready, 1)
                dve.wait_ge(rows_turned, 1)
                dve.tensor_copy(mem.shiftrow[:, :].rearrange("p (a n) -> p a n", a=2), mem.ps[0:1 + NS, 3:5, :]).then_inc(rows_out, 1)
            elif to == "split":
                def write(k):
                    if k >= 2:
                        dve.wait_ge(lo_done, k - 1)
                    dve.scalar_tensor_tensor(mem.tt[:, k % 2, :], mem.H[:, k, :], mem.vec[:, k, g:g + 1], rs[:, :],
                                             ALU.mult, ALU.mult).then_inc(t_ready, 1)
                write(0)
                for k in range(KB):
                    if k + 1 < KB:
                        write(k + 1)
                    dve.wait_ge(hi_ready, k + 1)
                    dve.wait_ge(t_ready, k + 1)
                    dve.tensor_tensor(mem.xs[:, 1, k, :], mem.tt[:, k % 2, :], mem.xs[:, 0, k, :].bitcast(F32),
                                      ALU.subtract).then_inc(lo_done, 1)
            else:
                for k in range(KB):
                    dve.scalar_tensor_tensor(mem.H[:, k, :], mem.H[:, k, :], mem.vec[:, k, g:g + 1], rs[:, :],
                                             ALU.mult, ALU.mult).then_inc(t_ready, 1)
                for i in range(T // P):
                    if i >= 2:
                        dve.wait_ge(store_free[i % 2], 16 * (i // 2))
                    for half in range(2):
                        n = 2 * i + half
                        dve.wait_ge(rows_turned, n + 1)
                        dve.tensor_copy(mem.yrow[:, i % 2, half * 512:half * 512 + 512], mem.ps[:, 3 + n % 4, :]).then_inc(rows_out, 1)

        @block.sync
        def _(sp):
            if to == "padded":
                sp.wait_ge(rows_out, 1)
                sp.dma_start(o["shift_p"][0], mem.shiftrow[0:1, :]).then_inc(stored, 16)
                sp.dma_start(o["shift_s"][0], mem.shiftrow[1:1 + NS, :]).then_inc(stored, 16)
                sp.wait_ge(stored, 32)
            if to == "out":
                for i in range(T // P):
                    sp.wait_ge(rows_out, 2 * i + 2)
                    dst = o["y_p"][0, i * P:(i + 1) * P, :] if i < TP // P else o["y_s"].rearrange("b t d -> (b t) d")
                    sp.dma_start(dst, mem.yrow[:, i % 2, :]).then_inc(store_free[i % 2], 16)
                sp.wait_ge(store_free[0], 16 * 5)
                sp.wait_ge(store_free[1], 16 * 4)


def mix_phase(nc, t, mem):
    JOBS = [(0, 8, "r"), (3, 1, "w"), (1, 8, "k"), (4, 1, "a"), (2, 8, "v"), (5, 2, "g")]
    FIRST = [sum(b for _, b, _ in JOBS[:j]) for j in range(len(JOBS))]
    TILES = sum(b for _, b, _ in JOBS)
    RKV = {"r": 0, "k": 1, "v": 2}
    with ExitStack() as ctx:
        sem = phase_semaphores(nc, ctx, "mix")
        s = Memory()
        weight_sems(sem, s)
        scaled, summed, hi_done, lo_done = sem("scaled"), sem("summed"), sem("hi_done"), sem("lo_done")
        mix_used = sem("mix_used")
        ps_free = sem("ps_free")
        out_ready, out_stored = sem("out_ready"), [sem("out_stored0"), sem("out_stored1")]
        block = ctx.enter_context(nc.Block())
        wr = t["rwkv_w_rkv"][0]

        @block.sync
        def _(sp):
            def slot(n):
                return mem.stage[:, n % 2, :].rearrange("p (k m) -> p k m", k=KB)

            for j, (mu, blocks, what) in enumerate(JOBS):
                n0 = FIRST[j]
                if what in RKV:
                    rank = RKV[what]
                    w = wr[rank].rearrange("(k p) m -> p k m", p=P)
                    with sp.Fori(0, 4) as i:
                        for u in range(2):
                            hold(sp, s.sp_passed, s.w_split, n0 + 2 * i + u + 1)
                            sp.dma_start(slot(n0 + u), w[:, :, bass.ds((2 * i + u) * P, P)]).then_inc(s.w_load[(n0 + u) % 2], 16)
                else:
                    for u in range(blocks):
                        n = n0 + u
                        hold(sp, s.sp_passed, s.w_split, n + 1)
                        if what == "g":
                            g1 = t["rwkv_gate_g1"][0].rearrange("(k p) m -> p k m", p=P)
                            sp.dma_start(slot(n), g1[:, :, 32 * u:32 * u + P]).then_inc(s.w_load[n % 2], 16)
                        else:
                            sp.dma_start(slot(n)[:, :, 0:64], t["rwkv_decay_w1"][0].rearrange("(k p) m -> p k m", p=P)
                                         ).then_inc(s.w_load[n % 2], 16)
                            sp.dma_start(slot(n)[:, :, 64:128], t["rwkv_iclr_a1"][0].rearrange("(k p) m -> p k m", p=P)
                                         ).then_inc(s.w_load[n % 2], 16)

        @block.gpsimd
        def _(pool):
            pool.sem_inc(s.w_split, 2)
            loads = [0, 0]
            for j, (mu, blocks, what) in enumerate(JOBS):
                n0 = FIRST[j]
                if what in RKV:
                    with pool.Fori(0, 4) as i:
                        chain = Chain(pool, s.pool_chain, n0 + 2 * i, 1)
                        for u in range(2):
                            v = (n0 + u) % 2
                            pool.wait_ge(s.w_load[v], loads[v] + 16 * i + 16)
                            hold(pool, s.pool_passed, s.tile_done, n0 + 2 * i + u + 1)
                            split_weight(pool, mem, v, chain).then_inc(s.w_split, 1)
                    loads = [x + 64 for x in loads]
                else:
                    chain = Chain(pool, s.pool_chain, n0, 1)
                    for u in range(blocks):
                        v = (n0 + u) % 2
                        loads[v] += 16 if what == "g" else 32
                        pool.wait_ge(s.w_load[v], loads[v])
                        hold(pool, s.pool_passed, s.tile_done, n0 + u + 1)
                        split_weight(pool, mem, v, chain).then_inc(s.w_split, 1)

        @block.tensor
        def _(pe):
            pe.sem_inc(s.tile_done, 2)

            def tile(n, v, j):
                pe.wait_ge(s.w_split, n + 3)
                pe.wait_ge(ps_free, n + 1)
                for k in range(KB):
                    pe.wait_ge(lo_done, KB * j + k + 1)
                    for a, (w, part) in enumerate(PASSES):
                        for c in range(3):
                            last = pe.matmul(mem.ps[:, 3 * v + c, 0:CW], mem.wsplit[:, v, w, k * P:(k + 1) * P],
                                             mem.mixed[:, part, k, c * CW:(c + 1) * CW],
                                             start=(k == 0 and a == 0), stop=(k == KB - 1 and a == 2))
                    last.then_inc(mix_used if k < KB - 1 else s.tile_done, 1)

            for j, (mu, blocks, what) in enumerate(JOBS):
                n0 = FIRST[j]
                if blocks == 8:
                    with pe.Fori(0, 4) as i:
                        for u in range(2):
                            tile(n0 + 2 * i + u, (n0 + u) % 2, j)
                else:
                    for u in range(blocks):
                        tile(n0 + u, (n0 + u) % 2, j)

        sample = lambda ap: ap[:, PROMPT_PAD + TP:TPAD - 1 + 1].rearrange("p (b t) -> p b t", b=NS)

        @block.scalar
        def _(act):
            act.sem_inc(ps_free, 2)

            def mix(j, mu):
                def scale(k):
                    if KB * j + k >= 2:
                        act.wait_ge(summed, KB * j + k - 1)
                    act.activation(mem.mt1[:, k % 2, 0:TPAD - 1], mem.xnp[:, k, 1:TPAD], ACT.Copy, scale=mem.omu[:, k, mu:mu + 1]).then_inc(scaled, 1)

                def hi(k):
                    act.wait_ge(summed, KB * j + k + 1)
                    if j:
                        if k < KB - 1:
                            act.wait_ge(mix_used, 7 * (FIRST[j] - 1) + k + 1)
                        else:
                            act.wait_ge(s.tile_done, FIRST[j] + 2)
                    act.copy(mem.mixed[:, 0, k, 0:TP], mem.mt2[:, k % 2, 0:TP]).then_inc(hi_done, 1)
                    act.copy(mem.mixed[:, 0, k, TP:T].rearrange("p (b t) -> p b t", b=NS), streams(mem.mt2[:, k % 2, :])).then_inc(hi_done, 1)

                scale(0)
                for k in range(KB):
                    if k + 1 < KB:
                        scale(k + 1)
                    hi(k)

            def leave(j, m_lo, m_hi):
                what = JOBS[j][2]
                n0 = FIRST[j]

                def one(n, m, v, even):
                    act.wait_ge(s.tile_done, n + 3)
                    ps3 = mem.ps[:, 3 * v:3 * v + 3, 0:CW]
                    if what in RKV:
                        act.wait_ge(out_stored[even], 16 * (4 * RKV[what]) + 8 * (m - even) + 16)
                        act.copy(by3(mem.rkvout[even][:, :]), ps3).then_inc(out_ready, 1)
                        act.wait_ge(out_ready, 8 * RKV[what] + m + 1)
                        act.dma_start(mem.rkv_dram[RKV[what], bass.ds(m * P, P), :], mem.rkvout[even][:, :]).then_inc(out_stored[even], 16)
                        act.sem_inc(ps_free, 1)
                    elif what == "w":
                        act.activation(by3(mem.lora_wa[0:64, :]), ps3[0:64], ACT.Tanh).then_inc(ps_free, 1)
                    elif what == "a":
                        act.copy(by3(mem.lora_wa[64:128, :]), ps3[64:128]).then_inc(ps_free, 1)
                    elif m == 0:
                        act.wait_ge(out_stored[0], 16 * 13)
                        act.activation(by3(mem.lora_g[:, :]), ps3, ACT.Sigmoid).then_inc(ps_free, 1)
                    else:
                        act.wait_ge(out_stored[1], 16 * 13)
                        act.activation(by3(mem.lora_g2[96:128, :]), ps3[96:128], ACT.Sigmoid).then_inc(ps_free, 1)

                m = m_lo
                if m_hi - m_lo >= 6:
                    with act.Fori(0, 3) as i:
                        for u in range(2):
                            one(n0 + m + 2 * i + u, m + 2 * i + u, (n0 + m + u) % 2, (m + u) % 2)
                    m += 6
                for m in range(m, m_hi):
                    one(n0 + m, m, (n0 + m) % 2, m % 2)

            act.sem_inc(out_stored[0], 16)
            act.sem_inc(out_stored[1], 16)
            for j, (mu, blocks, what) in enumerate(JOBS):
                mix(j, mu)
                if j:
                    leave(j - 1, JOBS[j - 1][1] - 1, JOBS[j - 1][1])
                leave(j, 0, blocks - 1)
            leave(len(JOBS) - 1, 1, 2)

        @block.vector
        def _(dve):
            for j, (mu, blocks, what) in enumerate(JOBS):
                def add(k):
                    dve.wait_ge(scaled, KB * j + k + 1)
                    if KB * j + k >= 2:
                        dve.wait_ge(lo_done, KB * j + k - 1)
                    dve.scalar_tensor_tensor(mem.mt2[:, k % 2, 0:TPAD - 1], mem.xnp[:, k, 0:TPAD - 1], mem.vec[:, k, VEC["mu0"] + mu:VEC["mu0"] + mu + 1],
                                             mem.mt1[:, k % 2, 0:TPAD - 1], ALU.mult, ALU.add).then_inc(summed, 1)

                def lo(k):
                    dve.wait_ge(hi_done, 2 * (KB * j + k) + 2)
                    dve.tensor_tensor(mem.mixed[:, 1, k, 0:TP], mem.mt2[:, k % 2, 0:TP], mem.mixed[:, 0, k, 0:TP].bitcast(F32), ALU.subtract)
                    dve.tensor_tensor(mem.mixed[:, 1, k, TP:T].rearrange("p (b t) -> p b t", b=NS), streams(mem.mt2[:, k % 2, :]),
                                      mem.mixed[:, 0, k, TP:T].bitcast(F32).rearrange("p (b t) -> p b t", b=NS), ALU.subtract).then_inc(lo_done, 1)

                add(0)
                for k in range(KB):
                    if k + 1 < KB:
                        add(k + 1)
                    lo(k)


def recurrence_areas(mem):
    m, at = Memory(), 0

    def cut(cols, *shape):
        nonlocal at
        ap = mem.arena[:, at:at + cols]
        at += cols
        return ap

    m.r, m.k, m.v = cut(T), cut(T), cut(T)
    m.ar = cut(NCH * 192).rearrange("p (n c) -> p n c", n=NCH)
    m.bbd, m.kbd, m.vbd = (cut(NCH * P).rearrange("p (n c) -> p n c", n=NCH) for _ in range(3))
    shared = at
    m.sg, m.cum, m.em, m.en, m.a, m.kn, m.k2 = (cut(T) for _ in range(7))
    end = at
    at = shared
    m.at = cut(2 * 4 * 512).rearrange("p (g q c) -> p g q c", g=2, q=4)
    m.tm = cut(2 * 4 * 384).rearrange("p (g q c) -> p g q c", g=2, q=4)
    at = max(at, end)
    m.x = cut(512).rearrange("p (q c) -> p q c", q=4)
    m.y = cut(1024).rearrange("p (g q c) -> p g q c", g=2, q=4)
    m.q = cut(512).rearrange("p (q c) -> p q c", q=4)
    m.lt = cut(1024).rearrange("p (l q c) -> p l q c", l=2, q=4)
    m.s = cut(256).rearrange("p (l c) -> p l c", l=2)
    m.sp, m.w, m.u, m.z, m.sfin = (cut(P) for _ in range(5))
    m.pc = cut(24)
    m.pp = cut(NROW)
    m.oka = cut(1)
    m.lw = cut(3 * P).rearrange("p (a c) -> p a c", a=3)
    m.mask, m.mask16 = cut(512), cut(512)
    m.level = cut(6 * P).rearrange("p (l c) -> p l c", l=6)
    m.m4 = cut(8).rearrange("p (e b) -> p e b", e=2)
    m.reset = cut(T)
    m.ep = cut(T)
    m.s0 = cut(NS * P).rearrange("p (b c) -> p b c", b=NS)
    m.out, m.bonus = m.r, m.k
    m.kq = m.ep
    m.s0t = m.v[:, 0:NS * P].rearrange("p (b c) -> p b c", b=NS)
    m.um, m.vm = m.x, m.q
    m.post1, m.post2 = m.sg, m.cum
    assert at <= mem.arena.shape[1], (at, mem.arena.shape)
    return m


def recurrence_phase(nc, t, mem, o):
    m = recurrence_areas(mem)
    LEVELS = [5, 5, 5, 5, 3]
    with ExitStack() as ctx:
        sem = phase_semaphores(nc, ctx, "scan")
        s = Memory()
        weight_sems(sem, s)
        consts, cchain = sem("consts"), sem("cchain")
        pair_done = sem("pair_done")
        rkv_in, lw_in, s0_in, states_out = sem("rkv_in"), sem("lw_in"), sem("s0_in"), sem("states_out")
        dve_chain, pool2, inverse, root = sem("dve_chain"), sem("pool2"), sem("inverse"), sem("root")
        pp_ready, wa_done, sg_ready, a_ready, kq_ready, kk_done = (sem(x) for x in
            ("pp_ready", "wa_done", "sg_ready", "a_ready", "kq_ready", "kk_done"))
        cum_ready, lme_ready, ep_ready, k2_ready, rk_ready, rk_done = (sem(x) for x in
            ("cum_ready", "lme_ready", "ep_ready", "k2_ready", "rk_ready", "rk_done"))
        operands, pool_operands = sem("operands"), sem("pool_operands")
        p1_done, at_ready, t_done, tm_ready = sem("p1_done"), sem("at_ready"), sem("t_done"), sem("tm_ready")
        lt_ready, m1_done, q_ready, m3_done, xy_ready = (sem(x) for x in ("lt_ready", "m1_done", "q_ready", "m3_done", "xy_ready"))
        w_done, w_ready, u_done, u_ready, s_done, s_ready, sp_ready, serial_done, o_ready = (sem(x) for x in
            ("w_done", "w_ready", "u_done", "u_ready", "s_done", "s_ready", "sp_ready", "serial_done", "o_ready"))
        s0t_done, s0t_ready, z_done, z_ready, um_ready, ns_done, ns_ready, nst_done, ns_out = (sem(x) for x in
            ("s0t_done", "s0t_ready", "z_done", "z_ready", "um_ready", "ns_done", "ns_ready", "nst_done", "ns_out"))
        fin_done, fin_ready = sem("fin_done"), sem("fin_ready")
        mean_done, xc_ready, sq_ready, var_done, norm_ready, aff_ready, gate_done, of_ready, oh_ready, ol_ready = (sem(x) for x in
            ("mean_done", "xc_ready", "sq_ready", "var_done", "norm_ready", "aff_ready", "gate_done", "of_ready", "oh_ready", "ol_ready"))
        proj_done, proj_free = sem("proj_done"), sem("proj_free")
        block = ctx.enter_context(nc.Block())
        vp = lambda name: m.pp[:, VEC[name]:VEC[name] + 1]
        halves = ((0, 64), (64, 128))
        bank = mem.ps

        @block.sync
        def _(sp):
            with sp.Fori(0, PAIRS) as p:
                hold(sp, s.sp_passed, pair_done, p + 1)
                for j, dst in enumerate((m.r, m.k, m.v)):
                    sp.dma_start(dst, mem.rkv_dram[j, bass.ds(p * P, P), :]).then_inc(rkv_in, 16)
                cols = bass.ds(p * P, P)
                sp.dma_start(m.lw[0:64, 0, :], t["rwkv_decay_w2"][0][:, cols]).then_inc(lw_in, 16)
                sp.dma_start(m.lw[64:128, 0, :], t["rwkv_iclr_a2"][0][:, cols]).then_inc(lw_in, 16)
                sp.dma_start(m.lw[:, 1, :], t["rwkv_gate_g2"][0][0:P, cols]).then_inc(lw_in, 16)
                sp.dma_start(m.lw[96:128, 2, :], t["rwkv_gate_g2"][0][P:P + 32, cols]).then_inc(lw_in, 16)
                for u in range(2):
                    hold(sp, s.sp_passed, s.w_split, 2 * p + u + 1)
                    sp.dma_start(mem.stage[:, u, 0:512], t["rwkv_w_out"][0][bass.ds(p * P, P), u * 512:u * 512 + 512]).then_inc(s.w_load[u], 16)
                for h, (lo, hi) in enumerate(halves):
                    if h == 0:
                        hold(sp, s.sp_passed, states_out, 96 * p + 16)
                    sp.dma_start(m.s0[lo:hi, :, lo:hi], t["state_wkv"][0][:, bass.ds(2 * p + h, 1), :, :].rearrange("b a v c -> v (a b) c")
                                 ).then_inc(s0_in, 16)
                hold(sp, s.sp_passed, fin_ready, p + 1)
                for h, (lo, hi) in enumerate(halves):
                    sp.dma_start(o["wkv_p"][0, 0, bass.ds(2 * p + h, 1), :, :].rearrange("a v c -> (a v) c"), m.sfin[lo:hi, lo:hi]).then_inc(states_out, 16)
                for e in range(2):
                    hold(sp, s.sp_passed, ns_out, 2 * p + e + 1)
                    for h, (lo, hi) in enumerate(halves):
                        sp.dma_start(o["wkv_s"][0, 4 * e:4 * e + 4, bass.ds(2 * p + h, 1), :, :].rearrange("b a v c -> v (a b) c"),
                                     m.s0[lo:hi, 4 * e:4 * e + 4, lo:hi]).then_inc(states_out, 16)
            hold(sp, s.sp_passed, states_out, 96 * PAIRS + 16)

        @block.gpsimd
        def _(pool):
            pool.sem_inc(s.w_split, 2)
            c = Chain(pool, cchain)
            for ap in (m.ar, m.bbd, m.kbd, m.vbd, m.s0, m.z):
                c.link(pool.memset(ap, 0.0))
            c.link(pool.memset(m.reset, 1.0))
            c.link(pool.memset(m.reset[:, 0:TP].rearrange("p (n c) -> p n c", c=CHUNK)[:, :, 0], 0.0))
            c.link(pool.memset(m.reset[:, TP:T].rearrange("p (n c) -> p n c", c=TS)[:, :, 0], 0.0))

            def same_block(ap, width, rows):
                n = ap.shape[-1] // width
                v = ap.rearrange("p (n w) -> p n w", w=width)
                c.link(pool.affine_select(out=v, in_=v, compare_op=ALU.is_ge, fill=0.0, base=0, pattern=[[-width, n], [0, width]], channel_multiplier=1))
                c.link(pool.affine_select(out=v, in_=v, compare_op=ALU.is_ge, fill=0.0, base=width - 1, pattern=[[width, n], [0, width]], channel_multiplier=-1))

            for mask, width in ((m.mask, 64), (m.mask16, TS)):
                c.link(pool.memset(mask, 1.0))
                for at in (0, 192):
                    aa, ar = mask[:, at:at + P], mask[:, at + P:at + 192]
                    same_block(aa, width, P)
                    c.link(pool.affine_select(out=aa, in_=aa, compare_op=ALU.is_gt, fill=0.0, base=0, pattern=[[1, P]], channel_multiplier=-1))
                    for lo, hi in halves:
                        h = ar[lo:hi]
                        same_block(h, width, 64)
                        c.link(pool.affine_select(out=h, in_=h, compare_op=ALU.is_ge, fill=0.0, base=0, pattern=[[1, 64]], channel_multiplier=-1))
                aa = mask[:, 384:512]
                same_block(aa, width, P)
                c.link(pool.affine_select(out=aa, in_=aa, compare_op=ALU.is_gt, fill=0.0, base=0, pattern=[[-1, P]], channel_multiplier=1))
            c.link(pool.memset(m.level, 1.0))
            for l in range(6):
                same_block(m.level[:, l, :], 2 ** (l + 1), P)
            for l in range(5, 0, -1):
                c.link(pool.tensor_tensor(m.level[:, l, :], m.level[:, l, :], m.level[:, l - 1, :], ALU.subtract))
            c.link(pool.tensor_tensor(m.level[:, 0, :], m.level[:, 0, :], mem.ident[:, :], ALU.subtract))
            c.link(pool.memset(m.m4, 1.0))
            for lo, hi in halves:
                v = m.m4[lo:hi]
                c.link(pool.affine_select(out=v, in_=v, compare_op=ALU.is_ge, fill=0.0, base=0, pattern=[[0, 2], [-TS, 4]], channel_multiplier=1))
                c.link(pool.affine_select(out=v, in_=v, compare_op=ALU.is_ge, fill=0.0, base=TS - 1, pattern=[[0, 2], [TS, 4]], channel_multiplier=-1))
            pool.sem_inc(consts, 1)
            pool.sem_inc(states_out, 16)

            with pool.Fori(0, PAIRS) as p:
                chain = Chain(pool, pool2, p, 5)
                pool.wait_ge(a_ready, p + 1)
                hold(pool, s.pool_passed, pp_ready, p + 1)
                chain.link(pool.tensor_scalar(m.k2, m.a, vp("ka"), m.oka, ALU.mult, ALU.add))
                pool.wait_ge(rkv_in, 48 * p + 48)
                pool.tensor_tensor(m.k2, m.k2, m.k, ALU.mult).then_inc(k2_ready, 1)
                pool.wait_ge(k2_ready, p + 1)
                pool.wait_ge(ep_ready, 3 * p + 2)
                for lo, hi in halves:
                    chain.mark(pool.tensor_tensor(m.kbd[lo:hi, :, lo:hi], chunks(m.k2[lo:hi]), chunks(m.en[lo:hi]), ALU.mult))
                for lo, hi in halves:
                    chain.mark(pool.tensor_scalar(m.vbd[lo:hi, :, lo:hi], chunks(m.v[lo:hi]), 1.0, None, ALU.mult))
                chain.gather()
                pool.sem_inc(pool_operands, 1)
                split = Chain(pool, s.pool_chain, p, 2)
                for u in range(2):
                    pool.wait_ge(s.w_load[u], 16 * p + 16)
                    hold(pool, s.pool_passed, s.tile_done, 2 * p + u + 1)
                    split_weight(pool, mem, u, split, 512).then_inc(s.w_split, 1)
                split.close("split")
                for g, (c0, G) in enumerate(GROUPS):
                    pool.wait_ge(at_ready, NCH * p + c0 + G + 2)
                    for l in range(1, LEVELS[g] + 1):
                        n = 23 * p + 5 * g + l - 1
                        pool.wait_ge(m1_done, (n if l == 1 else n - 1) + 1)
                        pool.tensor_tensor(m.lt[:, l % 2, 0:G, :], m.at[:, g % 2, 0:G, 0:P],
                                           spread(m.level[:, l, :], G), ALU.mult).then_inc(lt_ready, 1)
                chain.close("recurrence, Pool")

        def invert(g):
            return [(l, half) for l in range(1, LEVELS[g] + 1) for half in range(2)]

        def order():
            yield "form", 0, None
            for l, half in invert(0):
                yield "invert", 0, (l, half)
            for g in range(5):
                c0, G = GROUPS[g]
                todo = []
                if g < 4:
                    yield "form", g + 1, None
                    todo = invert(g + 1)
                slots = [(q, part) for q in range(G) for part in range(3)]
                for i, (q, part) in enumerate(slots):
                    yield ("step" if g < 4 else "stream"), g, (q, part)
                    if i < len(todo):
                        yield "invert", g + 1, todo[i]
                yield "leave", g, None

        ORDER = list(order())
        first_level = lambda g: 5 * g
        first_xy = lambda g: 6 * g

        @block.tensor
        def _(pe):
            pe.sem_inc(s.tile_done, 2)
            pe.sem_inc(serial_done, 1)
            pe.sem_inc(m1_done, 1)
            with pe.Fori(0, PAIRS) as p:
                def wide(b0, lhsT, rhs, start=True, stop=True):
                    for c in range(3):
                        last = pe.matmul(bank[:, b0 + c, 0:CW], lhsT, rhs[:, c * CW:(c + 1) * CW], start=start, stop=stop)
                    return last

                pe.wait_ge(pair_done, p + 1)
                pe.wait_ge(lw_in, 64 * p + 64)
                wide(0, m.lw[0:64, 0, :], mem.lora_wa[0:64, :]).then_inc(wa_done, 1)
                wide(3, m.lw[64:128, 0, :], mem.lora_wa[64:128, :]).then_inc(wa_done, 1)
                pe.wait_ge(kq_ready, p + 1)
                pe.wait_ge(sg_ready, p + 1)
                wide(0, mem.headones[:, :], m.kq).then_inc(kk_done, 1)
                pe.wait_ge(rk_ready, p + 1)
                pe.wait_ge(a_ready, p + 1)
                wide(3, mem.headones[:, :], m.cum).then_inc(rk_done, 1)
                pe.wait_ge(operands, p + 1)
                pe.wait_ge(pool_operands, p + 1)
                pe.wait_ge(consts, 1)
                for what, g, arg in ORDER:
                    c0, G = GROUPS[g]
                    n0 = NCH * p + c0
                    gb = g % 2
                    if what == "form":
                        for q in range(G):
                            n = c0 + q
                            pe.wait_ge(at_ready, n0 + q + 1)
                            b = bank[:, n % 2, :]
                            pe.matmul(b[:, 0:192], m.bbd[:, n, :], m.ar[:, n, :], start=True, stop=True)
                            pe.matmul(b[:, 192:384], m.kbd[:, n, :], m.ar[:, n, :], start=True, stop=True)
                            pe.matmul(b[:, 384:512], m.ar[:, n, 0:P], m.bbd[:, n, :], start=True, stop=True).then_inc(p1_done, 1)
                            pe.wait_ge(tm_ready, n0 + q + 1)
                            for j, x in enumerate((m.bbd, m.kbd, m.vbd)):
                                last = pe.transpose(bank[:, 2, j * P:(j + 1) * P], x[:, n, :], mem.ident[:, :])
                            last.then_inc(t_done, 1)
                    elif what == "invert":
                        l, half = arg
                        n = 23 * p + first_level(g) + l - 1
                        if half == 0:
                            pe.wait_ge(lt_ready, n + 1)
                            pe.wait_ge(xy_ready, 28 * p + first_xy(g) + l)
                            for q in range(G):
                                last = pe.matmul(bank[:, 3, q * P:(q + 1) * P], m.lt[:, l % 2, q, :], m.x[:, q, :], start=True, stop=True)
                            last.then_inc(m1_done, 1)
                        else:
                            pe.wait_ge(q_ready, n + 1)
                            if l < LEVELS[g]:
                                for q in range(G):
                                    pe.matmul(bank[:, 4, q * P:(q + 1) * P], m.y[:, gb, q, :], m.q[:, q, :], start=True, stop=True)
                            for q in range(G):
                                last = pe.matmul(bank[:, 5, q * P:(q + 1) * P], m.q[:, q, :], m.y[:, gb, q, :], start=True, stop=True)
                            last.then_inc(m3_done, 1)
                    elif what == "step":
                        q, part = arg
                        n, now = c0 + q, NCH * p + c0 + q
                        at, tm = m.at[:, gb, q, :], m.tm[:, gb, q, :]
                        S = m.s[:, n % 2, :]
                        if part == 0:
                            pe.wait_ge(s_ready, 17 * p + n + 1)
                            if q == 0:
                                pe.wait_ge(at_ready, n0 + G + 2)
                                pe.wait_ge(tm_ready, n0 + G + 1)
                            pe.matmul(bank[:, 6, 0:P], m.ar[:, n, 0:P], S, start=True, stop=False)
                            pe.matmul(bank[:, 6, 0:P], at[:, 192:320], tm[:, 256:384], start=False, stop=True).then_inc(w_done, 1)
                        elif part == 1:
                            pe.wait_ge(w_ready, now + 1)
                            if q == 0:
                                pe.wait_ge(xy_ready, 28 * p + first_xy(g) + LEVELS[g] + 1)
                            pe.matmul(bank[:, 6, P:2 * P], m.y[:, gb, q, :], m.w, start=True, stop=True).then_inc(u_done, 1)
                        else:
                            pe.wait_ge(u_ready, now + 1)
                            pe.matmul(bank[:, 6, 2 * P:3 * P], tm[:, 0:P], m.u, start=True, stop=False)
                            pe.matmul(bank[:, 6, 2 * P:3 * P], tm[:, P:2 * P], tm[:, 256:384], start=False, stop=True).then_inc(s_done, 1)
                            if q == 0:
                                pe.wait_ge(o_ready, 5 * p + g + 1)
                            ob = bank[:, 7, q * 64:(q + 1) * 64]
                            pe.matmul(ob, S, m.ar[:, n, P:192], start=True, stop=False)
                            pe.matmul(ob, m.u, at[:, P:192], start=False, stop=False)
                            pe.matmul(ob, tm[:, 256:384], at[:, 320:384], start=False, stop=True).then_inc(serial_done, 1)
                    elif what == "stream":
                        q, part = arg
                        n, now = c0 + q, NCH * p + c0 + q
                        at, tm = m.at[:, gb, q, :], m.tm[:, gb, q, :]
                        if part == 0:
                            if q == 0:
                                pe.wait_ge(s_ready, 17 * p + 17)
                                pe.wait_ge(m3_done, 23 * p + 23)
                                pe.wait_ge(xy_ready, 28 * p + 28)
                                pe.wait_ge(s0_in, 32 * p + 32)
                                pe.transpose(bank[:, 3, 0:P], m.s[:, 0, :], mem.ident[:, :]).then_inc(fin_done, 1)
                                for b in range(NS):
                                    last = pe.transpose(bank[:, 4 + b // 4, (b % 4) * P:(b % 4 + 1) * P], m.s0[:, b, :], mem.ident[:, :])
                                last.then_inc(s0t_done, 1)
                                pe.wait_ge(s0t_ready, 2 * p + 2)
                                pe.wait_ge(at_ready, n0 + G + 2)
                                pe.wait_ge(tm_ready, n0 + G + 1)
                            two = lambda ap, b: ap.rearrange("p (h t) -> p h t", h=2)[:, :, TS * b:TS * b + TS]
                            for b in range(4):
                                last = pe.matmul(two(bank[:, 6, 0:P], b), m.s0t[:, 4 * q + b, :], two(m.ar[:, n, 0:P], b), start=True, stop=True)
                            last.then_inc(z_done, 1)
                            pe.wait_ge(z_ready, 2 * p + q + 1)
                            pe.matmul(bank[:, 6, P:2 * P], m.z, mem.ident[:, :], start=True, stop=False)
                            pe.matmul(bank[:, 6, P:2 * P], at[:, 192:320], tm[:, 256:384], start=False, stop=True).then_inc(w_done, 1)
                        elif part == 1:
                            pe.wait_ge(w_ready, now + 1)
                            pe.matmul(bank[:, 6, 2 * P:3 * P], m.y[:, gb, q, :], m.w, start=True, stop=True).then_inc(u_done, 1)
                        else:
                            pe.wait_ge(u_ready, now + 1)
                            if q == 0:
                                pe.wait_ge(o_ready, 5 * p + g + 1)
                            ob = bank[:, 7, q * 64:(q + 1) * 64]
                            pe.matmul(ob, m.u, at[:, P:192], start=True, stop=False)
                            pe.matmul(ob, tm[:, 256:384], at[:, 320:384], start=False, stop=False)
                            for b in range(4):
                                last = pe.matmul(ob[:, TS * b:TS * b + TS], m.s0t[:, 4 * q + b, :], m.ar[:, n, P + TS * b:P + TS * b + TS],
                                                 start=False, stop=(b == 3))
                            last.then_inc(serial_done, 1)
                            pe.wait_ge(um_ready, 2 * p + q + 1)
                            pe.matmul(bank[:, 4, :], tm[:, 0:P], m.um, start=True, stop=False)
                            pe.matmul(bank[:, 4, :], tm[:, P:2 * P], m.vm, start=False, stop=True).then_inc(ns_done, 1)
                            pe.wait_ge(ns_ready, 2 * p + q + 1)
                            if q:
                                pe.wait_ge(ns_out, 2 * p + q)
                            for b in range(4):
                                last = pe.transpose(bank[:, 5, b * P:(b + 1) * P], m.s0t[:, 4 * q + b, :], mem.ident[:, :])
                            last.then_inc(nst_done, 1)
                pe.wait_ge(o_ready, 5 * p + 6)
                wide(0, mem.headones[:, :], m.out).then_inc(mean_done, 1)
                pe.wait_ge(ns_out, 2 * p + 2)
                pe.wait_ge(sq_ready, p + 1)
                wide(3, mem.headones[:, :], m.post1).then_inc(var_done, 1)
                pe.wait_ge(xc_ready, p + 1)
                wide(0, m.lw[:, 1, :], mem.lora_g[:, :], stop=False)
                wide(0, m.lw[96:128, 2, :], mem.lora_g2[96:128, :], start=False).then_inc(gate_done, 1)
                for k in range(KB):
                    if k % 4 == 0:
                        pe.wait_ge(s.w_split, 2 * p + k // 4 + 3)
                    pe.wait_ge(proj_free, KB * p + k + 1)
                    if k == 0:
                        pe.wait_ge(norm_ready, p + 1)
                        pe.wait_ge(of_ready, p + 1)
                        pe.wait_ge(ol_ready, p + 1)
                    last = outer(pe, mem, bank[:, 3 * (k % 2):3 * (k % 2) + 3, :], [(k // 4, mem.oh)], k % 4)
                    last.then_inc(proj_done, 1)
                    if k % 4 == 3:
                        pe.wait_ge(proj_done, KB * p + k + 1)
                        pe.sem_inc(s.tile_done, 1)

        @block.scalar
        def _(act):
            act.sem_inc(tm_ready, 1)
            act.sem_inc(o_ready, 1)
            with act.Fori(0, PAIRS) as p:
                act.wait_ge(rkv_in, 48 * p + 48)
                act.wait_ge(pp_ready, p + 1)
                act.activation(m.kq, m.k, ACT.Square, scale=vp("kk")).then_inc(kq_ready, 1)
                act.wait_ge(wa_done, 2 * p + 1)
                act.activation(by3(m.sg), bank[:, 0:3, 0:CW], ACT.Sigmoid, bias=vp("w0")).then_inc(sg_ready, 1)
                act.wait_ge(wa_done, 2 * p + 2)
                act.activation(by3(m.a), bank[:, 3:6, 0:CW], ACT.Sigmoid, bias=vp("a0")).then_inc(a_ready, 1)
                act.wait_ge(cum_ready, p + 1)
                act.activation(m.kn, m.cum, ACT.Exp, scale=-DECAY).then_inc(ep_ready, 1)
                act.activation(m.en, m.cum, ACT.Exp, scale=DECAY).then_inc(ep_ready, 1)
                act.wait_ge(lme_ready, p + 1)
                act.activation(m.em, m.sg, ACT.Exp, scale=-DECAY).then_inc(ep_ready, 1)
                act.wait_ge(inverse, 2 * p + 1)
                act.activation(m.kn, m.kn, ACT.Sqrt).then_inc(root, 1)
                act.wait_ge(operands, p + 1)
                act.wait_ge(pool_operands, p + 1)
                for what, g, arg in ORDER:
                    c0, G = GROUPS[g]
                    gb = g % 2
                    if what == "form":
                        act.wait_ge(serial_done, NCH * p + (GROUPS[g - 1][0] if g >= 2 else 0) + 1)
                        for q in range(G):
                            act.wait_ge(t_done, NCH * p + c0 + q + 1)
                            act.copy(m.tm[:, gb, q, :], bank[:, 2, 0:384]).then_inc(tm_ready, 1)
                    elif what == "invert" and arg[1] == 0:
                        n = 23 * p + first_level(g) + arg[0] - 1
                        act.wait_ge(m1_done, n + 2)
                        act.copy(m.q[:, 0:G, :], bank[:, 3, 0:G * P].rearrange("p (q c) -> p q c", q=G)).then_inc(q_ready, 1)
                    elif what == "step" and arg[1] == 0:
                        n = c0 + arg[0]
                        act.wait_ge(s_ready, 17 * p + n + 1)
                        act.activation(m.sp, m.s[:, n % 2, :], ACT.Copy, scale=m.pc[:, n:n + 1]).then_inc(sp_ready, 1)
                    elif what == "stream":
                        q, part = arg
                        if q == 0 and part == 0:
                            act.wait_ge(fin_done, p + 1)
                            act.copy(m.sfin, bank[:, 3, 0:P]).then_inc(fin_ready, 1)
                            act.wait_ge(s0t_done, p + 1)
                            for j in range(2):
                                act.copy(m.s0t[:, 4 * j:4 * j + 4, :], bank[:, 4 + j, :].rearrange("p (b c) -> p b c", b=4)).then_inc(s0t_ready, 1)
                        if part == 2:
                            act.wait_ge(nst_done, 2 * p + q + 1)
                            act.copy(m.s0[:, 4 * q:4 * q + 4, :], bank[:, 5, :].rearrange("p (b c) -> p b c", b=4)).then_inc(ns_out, 1)
                    elif what == "leave":
                        act.wait_ge(serial_done, NCH * p + c0 + G + 1)
                        act.copy(m.out[:, c0 * CHUNK:(c0 + G) * CHUNK], bank[:, 7, 0:G * CHUNK]).then_inc(o_ready, 1)
                act.wait_ge(xc_ready, p + 1)
                act.activation(m.post1, m.out, ACT.Square).then_inc(sq_ready, 1)
                act.wait_ge(inverse, 2 * p + 2)
                act.activation(m.post2, m.post2, ACT.Sqrt).then_inc(root, 1)
                act.wait_ge(norm_ready, p + 1)
                act.activation(m.out, m.out, ACT.Identity, scale=vp("lnw"), bias=vp("lnb")).then_inc(aff_ready, 1)
                act.wait_ge(of_ready, p + 1)
                act.copy(mem.oh[:, 0, :], m.out).then_inc(oh_ready, 1)

        @block.vector
        def _(dve):
            dve.sem_inc(pair_done, 1)
            dve.sem_inc(at_ready, 2)
            dve.sem_inc(proj_free, 2)
            dve.wait_ge(consts, 1)
            with dve.Fori(0, PAIRS) as p:
                chain = Chain(dve, dve_chain, p, DVE_LINKS)
                chain.link(dve.tensor_copy(m.pp, mem.vec[:, bass.ds(p, 1), :].rearrange("p a n -> p (a n)")))
                dve.tensor_scalar(m.oka, vp("ka"), -1.0, 1.0, ALU.mult, ALU.add).then_inc(pp_ready, 1)
                dve.wait_ge(sg_ready, p + 1)
                dve.tensor_tensor_scan(m.cum, m.reset, m.sg, 0.0, ALU.mult, ALU.add).then_inc(cum_ready, 1)
                dve.wait_ge(cum_ready, p + 1)
                dve.tensor_tensor(m.sg, m.cum, m.sg, ALU.subtract).then_inc(lme_ready, 1)
                dve.wait_ge(ep_ready, 3 * p + 1)
                dve.wait_ge(rkv_in, 48 * p + 48)
                chain.link(dve.tensor_tensor(m.ar[:, :, P:192], chunks(m.r), chunks(m.kn), ALU.mult))
                chain.link(dve.tensor_copy(m.pc[:, 0:16], m.kn[:, 0:TP].rearrange("p (n c) -> p n c", c=CHUNK)[:, :, CHUNK - 1]))
                chain.link(dve.tensor_copy(m.pc[:, 16:24], m.kn[:, TP:T].rearrange("p (n c) -> p n c", c=TS)[:, :, TS - 1]))
                dve.wait_ge(kk_done, p + 1)
                chain.link(dve.tensor_scalar(by3(m.kn), bank[:, 0:3, 0:CW], 1e-24, None, ALU.max))
                dve.reciprocal(m.kn, m.kn).then_inc(inverse, 1)
                dve.wait_ge(root, 2 * p + 1)
                chain.link(dve.scalar_tensor_tensor(m.kn, m.k, vp("kk"), m.kn, ALU.mult, ALU.mult))
                dve.wait_ge(ep_ready, 3 * p + 3)
                for lo, hi in halves:
                    chain.link(dve.scalar_tensor_tensor(m.ar[lo:hi, :, lo:hi], chunks(m.kn[lo:hi]), -1.0, chunks(m.em[lo:hi]), ALU.mult, ALU.mult))
                dve.wait_ge(a_ready, p + 1)
                chain.link(dve.tensor_tensor(m.kn, m.kn, m.a, ALU.mult))
                for lo, hi in halves:
                    chain.link(dve.tensor_tensor(m.bbd[lo:hi, :, lo:hi], chunks(m.kn[lo:hi]), chunks(m.en[lo:hi]), ALU.mult))
                dve.wait_ge(k2_ready, p + 1)
                dve.wait_ge(ep_ready, 3 * p + 3)
                dve.scalar_tensor_tensor(m.cum, m.r, vp("rk"), m.k2, ALU.mult, ALU.mult).then_inc(rk_ready, 1)
                dve.wait_ge(rk_done, p + 1)
                dve.wait_ge(pool_operands, p + 1)
                dve.tensor_tensor(by3(m.bonus), bank[:, 3:6, 0:CW], by3(m.v), ALU.mult).then_inc(operands, 1)
                dve.wait_ge(operands, p + 1)
                dve.memset(m.s[:, 0, :], 0.0).then_inc(s_ready, 1)
                for what, g, arg in ORDER:
                    c0, G = GROUPS[g]
                    gb = g % 2
                    if what == "form":
                        dve.wait_ge(serial_done, NCH * p + (GROUPS[g - 1][0] if g >= 2 else 0) + 1)
                        for q in range(G):
                            dve.wait_ge(p1_done, NCH * p + c0 + q + 1)
                            dve.tensor_tensor(m.at[:, gb, q, :], bank[:, (c0 + q) % 2, :], m.mask if g < 4 else m.mask16, ALU.mult).then_inc(at_ready, 1)
                        dve.wait_ge(at_ready, NCH * p + c0 + G + 2)
                        one, eye = spread(m.level[:, 0, :], G), spread(mem.ident[:, :], G)
                        chain.link(dve.tensor_tensor(m.x[:, 0:G, :], m.at[:, gb, 0:G, 384:512], one, ALU.mult))
                        chain.link(dve.tensor_tensor(m.x[:, 0:G, :], m.x[:, 0:G, :], eye, ALU.add))
                        chain.link(dve.tensor_tensor(m.y[:, gb, 0:G, :], m.at[:, gb, 0:G, 0:P], one, ALU.mult))
                        dve.tensor_tensor(m.y[:, gb, 0:G, :], m.y[:, gb, 0:G, :], eye, ALU.add).then_inc(xy_ready, 1)
                    elif what == "invert" and arg[1] == 1:
                        l = arg[0]
                        n = 23 * p + first_level(g) + l - 1
                        wide = lambda b: bank[:, b, 0:G * P].rearrange("p (q c) -> p q c", q=G)
                        dve.wait_ge(m3_done, n + 1)
                        dve.wait_ge(xy_ready, 28 * p + first_xy(g) + l)
                        if l < LEVELS[g]:
                            chain.link(dve.tensor_tensor(m.x[:, 0:G, :], wide(4), m.x[:, 0:G, :], ALU.add))
                        dve.tensor_tensor(m.y[:, gb, 0:G, :], wide(5), m.y[:, gb, 0:G, :], ALU.add).then_inc(xy_ready, 1)
                    elif what == "step":
                        q, part = arg
                        n, now = c0 + q, NCH * p + c0 + q
                        if part == 0:
                            dve.wait_ge(w_done, now + 1)
                            dve.tensor_copy(m.w, bank[:, 6, 0:P]).then_inc(w_ready, 1)
                        elif part == 1:
                            dve.wait_ge(u_done, now + 1)
                            dve.tensor_copy(m.u, bank[:, 6, P:2 * P]).then_inc(u_ready, 1)
                        else:
                            dve.wait_ge(s_done, 16 * p + n + 1)
                            dve.wait_ge(sp_ready, 16 * p + n + 1)
                            dve.scalar_tensor_tensor(m.s[:, (n + 1) % 2, :], bank[:, 6, 2 * P:3 * P], m.pc[:, n:n + 1], m.sp, ALU.mult, ALU.add).then_inc(s_ready, 1)
                    elif what == "stream":
                        q, part = arg
                        now = NCH * p + c0 + q
                        if part == 0:
                            dve.wait_ge(z_done, 2 * p + q + 1)
                            dve.tensor_copy(m.z, bank[:, 6, 0:P]).then_inc(z_ready, 1)
                            dve.wait_ge(w_done, now + 1)
                            dve.tensor_copy(m.w, bank[:, 6, P:2 * P]).then_inc(w_ready, 1)
                        elif part == 1:
                            dve.wait_ge(u_done, now + 1)
                            dve.tensor_copy(m.u, bank[:, 6, 2 * P:3 * P]).then_inc(u_ready, 1)
                        else:
                            dve.wait_ge(u_ready, now + 1)
                            dve.wait_ge(tm_ready, now + 2)
                            rows = m.m4[:, 0, :].unsqueeze(2).to_broadcast((P, 4, P))
                            if q:
                                dve.wait_ge(ns_done, 2 * p + q)
                            chain.link(dve.tensor_tensor(m.um, spread(m.u, 4), rows, ALU.mult))
                            dve.tensor_tensor(m.vm, spread(m.tm[:, gb, q, 256:384], 4), rows, ALU.mult).then_inc(um_ready, 1)
                            dve.wait_ge(ns_done, 2 * p + q + 1)
                            dve.wait_ge(serial_done, now + 2)
                            st = m.s0t[:, 4 * q:4 * q + 4, :]
                            chain.link(dve.tensor_tensor(st, bank[:, 4, :].rearrange("p (b c) -> p b c", b=4), st, ALU.add))
                            dve.tensor_tensor(st, st, m.pc[:, 16 + 4 * q:20 + 4 * q].unsqueeze(2).to_broadcast((P, 4, P)), ALU.mult).then_inc(ns_ready, 1)
                dve.wait_ge(mean_done, p + 1)
                dve.wait_ge(o_ready, 5 * p + 6)
                dve.scalar_tensor_tensor(by3(m.out), bank[:, 0:3, 0:CW], -1.0 / HD, by3(m.out), ALU.mult, ALU.add).then_inc(xc_ready, 1)
                dve.wait_ge(var_done, p + 1)
                chain.link(dve.tensor_scalar(by3(m.post2), bank[:, 3:6, 0:CW], 1.0 / HD, LNX_EPS, ALU.mult, ALU.add))
                dve.reciprocal(m.post2, m.post2).then_inc(inverse, 1)
                dve.wait_ge(root, 2 * p + 2)
                dve.tensor_tensor(m.out, m.out, m.post2, ALU.mult).then_inc(norm_ready, 1)
                dve.wait_ge(aff_ready, p + 1)
                chain.link(dve.tensor_tensor(m.out, m.out, m.bonus, ALU.add))
                dve.wait_ge(gate_done, p + 1)
                dve.tensor_tensor(by3(m.out), bank[:, 0:3, 0:CW], by3(m.out), ALU.mult).then_inc(of_ready, 1)
                dve.wait_ge(of_ready, p + 1)
                dve.wait_ge(oh_ready, p + 1)
                dve.tensor_tensor(mem.oh[:, 1, :], m.out, mem.oh[:, 0, :].bitcast(F32), ALU.subtract).then_inc(ol_ready, 1)
                for k in range(KB):
                    dve.wait_ge(proj_done, KB * p + k + 1)
                    ins = dve.tensor_tensor(by3(mem.H[:, k, :]), bank[:, 3 * (k % 2):3 * (k % 2) + 3, 0:CW], by3(mem.H[:, k, :]), ALU.add)
                    ins.then_inc(proj_free, 1)
                dve.wait_ge(proj_free, KB * p + KB + 2)
                dve.sem_inc(pair_done, 1)
                chain.close("recurrence, VectorE")


def ffn_phase(nc, t, mem, layer):
    TURNS = HB // 2
    with ExitStack() as ctx:
        sem = phase_semaphores(nc, ctx, f"ffn_{layer}")
        s = Memory()
        weight_sems(sem, s)
        done, free = [sem("doneA"), sem("doneB")], [sem("freeA"), sem("freeB")]
        silu_ready, hf_ready, hh_ready, hid_ready, hid_used = (sem(x) for x in
            ("silu_ready", "hf_ready", "hh_ready", "hid_ready", "hid_used"))
        block = ctx.enter_context(nc.Block())
        gu = t["ffn_w_gu"][layer].rearrange("(k p) m -> p k m", p=P)
        down = t["ffn_w_down"][layer]

        @block.sync
        def _(sp):
            with sp.Fori(0, TURNS) as g:
                for u in range(6):
                    hold(sp, s.sp_passed, s.w_split, 6 * g + u + 1)
                    if u < 4:
                        src = gu[:, :, bass.ds((2 * g + u // 2) * P + (u % 2) * DFF, P)]
                        dst = mem.stage[:, u % 2, :].rearrange("p (k m) -> p k m", k=KB)
                    else:
                        src, dst = down[bass.ds((2 * g + u - 4) * P, P), :], mem.stage[:, u % 2, :]
                    sp.dma_start(dst, src).then_inc(s.w_load[u % 2], 16)

        @block.gpsimd
        def _(pool):
            split_tiles(pool, mem, s, 6 * TURNS)

        @block.tensor
        def _(pe):
            pe.sem_inc(s.tile_done, 2)
            with pe.Fori(0, TURNS) as g:
                for u in range(4):
                    pe.wait_ge(s.w_split, 6 * g + u + 3)
                    pe.wait_ge(free[u % 2], 6 * g + u // 2 + 1)
                    product(pe, mem, mem.ps[:, 3 * (u % 2):3 * (u % 2) + 3, :], u % 2, mem.xs).then_inc(done[u % 2], 1)
                    pe.wait_ge(done[u % 2], 6 * g + u // 2 + 1)
                    pe.sem_inc(s.tile_done, 1)
                pe.wait_ge(s.w_split, 6 * g + 8)
                for k in range(KB):
                    pe.wait_ge(free[k % 2], 6 * g + 3 + k // 2)
                    if k == 0:
                        pe.wait_ge(hid_ready, 2 * g + 3)
                    outer(pe, mem, mem.ps[:, 3 * (k % 2):3 * (k % 2) + 3, :],
                          [(0, mem.hid[:, 0]), (1, mem.hid[:, 1])], k).then_inc(done[k % 2], 1)
                pe.wait_ge(done[1], 6 * g + 6)
                pe.sem_inc(s.tile_done, 2)
                pe.sem_inc(hid_used, 1)

        @block.scalar
        def _(act):
            act.sem_inc(free[0], 1)
            with act.Fori(0, TURNS) as g:
                for b in range(2):
                    act.wait_ge(done[0], 6 * g + b + 1)
                    act.wait_ge(hf_ready, 2 * g + b + 1)
                    act.activation(by3(mem.sg[:, :]), mem.ps[:, 0:3, 0:CW], ACT.Silu).then_inc(silu_ready, 1)
                    act.wait_ge(silu_ready, 2 * g + b + 1)
                    act.sem_inc(free[0], 1)
                    act.wait_ge(hf_ready, 2 * g + b + 2)
                    act.wait_ge(hid_used, g + 1)
                    act.copy(mem.hid[:, b, 0, :], mem.hf[:, :]).then_inc(hh_ready, 1)

        @block.vector
        def _(dve):
            dve.sem_inc(free[1], 1)
            dve.sem_inc(hf_ready, 1)
            dve.sem_inc(hid_used, 1)
            dve.sem_inc(hid_ready, 1)
            with dve.Fori(0, TURNS) as g:
                for b in range(2):
                    dve.wait_ge(silu_ready, 2 * g + b + 1)
                    dve.wait_ge(done[1], 6 * g + b + 1)
                    dve.wait_ge(hid_ready, 2 * g + b + 1)
                    dve.tensor_tensor(by3(mem.hf[:, :]), mem.ps[:, 3:6, 0:CW], by3(mem.sg[:, :]), ALU.mult).then_inc(hf_ready, 1)
                    dve.wait_ge(hf_ready, 2 * g + b + 2)
                    dve.sem_inc(free[1], 1)
                    dve.wait_ge(hh_ready, 2 * g + b + 1)
                    dve.tensor_tensor(mem.hid[:, b, 1, :], mem.hf[:, :], mem.hid[:, b, 0, :].bitcast(F32), ALU.subtract).then_inc(hid_ready, 1)
                for k in range(KB):
                    dve.wait_ge(done[k % 2], 6 * g + 3 + k // 2)
                    dve.tensor_tensor(by3(mem.H[:, k, :]), mem.ps[:, 3 * (k % 2):3 * (k % 2) + 3, 0:CW], by3(mem.H[:, k, :]),
                                      ALU.add).then_inc(free[k % 2], 1)


def attention_phase(nc, t, mem, o):
    ITEMS = [(i, h) for i in range(TP // P) for h in range(2)]
    NI = len(ITEMS)
    with ExitStack() as ctx:
        sem = phase_semaphores(nc, ctx, "attention")
        s = Memory()
        weight_sems(sem, s)
        pair_done, consts, cchain = sem("pair_done"), sem("consts"), sem("cchain")
        dve_chain, qs_ready = sem("dve_chain"), sem("qs_ready")
        bias_in, bs_in, ck_in, cv_in, kv_out = sem("bias_in"), sem("bs_in"), [sem("ck_in0"), sem("ck_in1")], sem("cv_in"), sem("kv_out")
        qkv_done, q_ready, k_ready, v_ready = sem("qkv_done"), sem("q_ready"), sem("k_ready"), sem("v_ready")
        vt_done, vtm_ready, kt_done, kout_ready = sem("vt_done"), sem("vtm_ready"), sem("kt_done"), sem("kout_ready")
        sc_done, sm_ready, ex_ready, nm_ready, pt_done, pt_ready, pv_done, on_ready, ot_done, ot_ready = (sem(x) for x in
            ("sc_done", "sm_ready", "ex_ready", "nm_ready", "pt_done", "pt_ready", "pv_done", "on_ready", "ot_done", "ot_ready"))
        kc_done, kc_ready, ssc_done, ssm_ready, snm_ready, sex_ready, spr_ready, spt_done, spt_ready, spv_done, so_ready = (sem(x) for x in
            ("kc_done", "kc_ready", "ssc_done", "ssm_ready", "snm_ready", "sex_ready", "spr_ready", "spt_done", "spt_ready", "spv_done", "so_ready"))
        oh_ready, ol_ready, proj_done, proj_free = sem("oh_ready"), sem("ol_ready"), sem("proj_done"), sem("proj_free")
        block = ctx.enter_context(nc.Block())
        ps = mem.ps
        flat = mem.ps[:, :, :].rearrange("p b c -> p (b c)")
        halves = ((0, 64), (64, 128))
        wqkv = t["attn_w_qkv"][0].rearrange("(k p) m -> p k m", p=P)
        keys_of = lambda i: (max(0, i - 4), min(i, 4) + 1)
        ck = lambda b, p: t["cache_k"][0][b].rearrange("(a k) h d -> k a (h d)", k=P)[:, :, bass.ds(p * P, P)]
        cv = lambda b, p: t["cache_v"][0][b].rearrange("(a k) h d -> k a (h d)", k=P)[:, :, bass.ds(p * P, P)]

        @block.sync
        def _(sp):
            with sp.Fori(0, PAIRS) as p:
                cols = bass.ds(p * P, P)
                for u in range(3):
                    hold(sp, s.sp_passed, s.w_split, 4 * p + u + 1)
                    sp.dma_start(mem.stage[:, u % 2, :].rearrange("p (k m) -> p k m", k=KB), wqkv[:, :, bass.ds(p * P + u * D, P)]
                                 ).then_inc(s.w_load[u % 2], 16)
                hold(sp, s.sp_passed, pair_done, p + 1)
                for h in range(2):
                    sp.dma_start(mem.bt[:, h, :], mem.tab_dram[bass.ds(2 * p + h, 1), :, :].rearrange("a q k -> (a q) k")).then_inc(bias_in, 16)
                hold(sp, s.sp_passed, bias_in, 32 * p + 32)
                for b in range(4):
                    for h in range(2):
                        lo = 32 * b + 16 * h
                        sp.dma_start(mem.bs[lo:lo + 16, :], mem.bt[0:16, h, 0:SPAN]).then_inc(bs_in, 16)
                hold(sp, s.sp_passed, s.w_split, 4 * p + 4)
                sp.dma_start(mem.stage[:, 1, :], t["attn_w_out"][0][cols, :]).then_inc(s.w_load[1], 16)
                for b in range(2):
                    hold(sp, s.sp_passed, kc_ready, NS * p + b + 1)
                    sp.dma_start(mem.ck[:, b % 2, :, :], ck(b, p)).then_inc(ck_in[b % 2], 16)
                for b in range(4):
                    sp.dma_start(mem.cv[:, b, :, :], cv(b, p)).then_inc(cv_in, 16)
                hold(sp, s.sp_passed, kout_ready, p + 1)
                hold(sp, s.sp_passed, vtm_ready, p + 1)
                for src, dp, ds_ in ((mem.kout[:, :, :], "k_p", "k_s"), (mem.vtm[:, 4:9, :], "v_p", "v_s")):
                    sp.dma_start(o[dp][0, 0].rearrange("(a k) h d -> k a (h d)", k=P)[:, :, cols], src[:, 0:4, :]).then_inc(kv_out, 16)
                    sp.dma_start(o[ds_][0].rearrange("b t h d -> (b t) (h d)")[:, cols], src[:, 4, :]).then_inc(kv_out, 16)
                for b in range(2, NS):
                    hold(sp, s.sp_passed, kc_ready, NS * p + b + 1)
                    sp.dma_start(mem.ck[:, b % 2, :, :], ck(b, p)).then_inc(ck_in[b % 2], 16)
                hold(sp, s.sp_passed, spv_done, 2 * p + 1)
                for b in range(4):
                    sp.dma_start(mem.cv[:, b, :, :], cv(b + 4, p)).then_inc(cv_in, 16)
                hold(sp, s.sp_passed, kv_out, 64 * p + 64)

        @block.gpsimd
        def _(pool):
            c = Chain(pool, cchain)
            c.link(pool.memset(mem.qz[:, :, :], 0.0))
            c.link(pool.memset(mem.smask[:, :, :], 1.0))
            for e in range(2):
                v = mem.smask[:, e, :].rearrange("p (b t) -> p b t", b=NS)
                c.link(pool.affine_select(out=v, in_=v, compare_op=ALU.is_ge, fill=0.0, base=128 * e, pattern=[[-32, NS], [0, TS]], channel_multiplier=1))
                c.link(pool.affine_select(out=v, in_=v, compare_op=ALU.is_ge, fill=0.0, base=31 - 128 * e, pattern=[[32, NS], [0, TS]], channel_multiplier=-1))
            pool.sem_inc(consts, 1)
            split_tiles(pool, mem, s, 4 * PAIRS)

        @block.tensor
        def _(pe):
            pe.sem_inc(s.tile_done, 2)
            pe.wait_ge(consts, 1)
            with pe.Fori(0, PAIRS) as p:
                pe.wait_ge(pair_done, p + 1)
                for u in range(3):
                    pe.wait_ge(s.w_split, 4 * p + u + 3)
                    if u == 2:
                        pe.wait_ge(q_ready, 2 * p + 2)
                    product(pe, mem, ps[:, 3 * (u % 2):3 * (u % 2) + 3, :], u % 2, mem.xs).then_inc(qkv_done, 1)
                    pe.wait_ge(qkv_done, 3 * p + u + 1)
                    pe.sem_inc(s.tile_done, 1)
                pe.wait_ge(k_ready, p + 1)
                for i in range(5):
                    last = pe.transpose(flat[:, 3 * 512 + i * P:3 * 512 + (i + 1) * P], mem.kT[:, (4 + i) * P:(5 + i) * P], mem.ident[:, :])
                last.then_inc(kt_done, 1)
                pe.wait_ge(v_ready, p + 1)
                for i in range(9):
                    last = pe.transpose(flat[:, 5 * 512 + i * P:5 * 512 + (i + 1) * P], mem.ofm[:, i * P:(i + 1) * P], mem.ident[:, :])
                last.then_inc(vt_done, 1)
                pe.wait_ge(vtm_ready, p + 1)
                pe.wait_ge(kout_ready, p + 1)

                def scores(n):
                    i, h = ITEMS[n]
                    k0, nk = keys_of(i)
                    if n >= 2:
                        pe.wait_ge(sm_ready, NI * p + n - 1)
                    at = 1024 * (n % 2)
                    w = nk * P
                    for lo in range(0, w, 512):
                        hi = min(w, lo + 512)
                        last = pe.matmul(flat[:, at + lo:at + hi], mem.qz[:, h, i * P:(i + 1) * P], mem.kT[:, k0 * P + lo:k0 * P + hi], start=True, stop=True)
                    last.then_inc(sc_done, 1)

                def turn(n):
                    i, h = ITEMS[n]
                    k0, nk = keys_of(i)
                    pe.wait_ge(ex_ready, NI * p + n + 1)
                    if n >= 1:
                        pe.wait_ge(pt_ready, NI * p + n)
                    for j in range(nk):
                        last = pe.transpose(flat[:, 2048 + j * P:2048 + (j + 1) * P], mem.pr[:, n % 2, j * P:(j + 1) * P], mem.ident[:, :])
                    last.then_inc(pt_done, 1)

                def values(n):
                    i, h = ITEMS[n]
                    k0, nk = keys_of(i)
                    pe.wait_ge(pt_ready, NI * p + n + 1)
                    if n >= 1:
                        pe.wait_ge(on_ready, NI * p + n)
                    for j in range(nk):
                        last = pe.matmul(ps[:, 6, 0:64], mem.pt[:, n % 2, j * P:(j + 1) * P], mem.vtm[:, k0 + j, h * 64:(h + 1) * 64],
                                         start=(j == 0), stop=(j == nk - 1))
                    last.then_inc(pv_done, 1)

                def back(i):
                    pe.wait_ge(on_ready, NI * p + 2 * i + 2)
                    if i >= 1:
                        pe.wait_ge(ot_ready, 8 * p + i)
                    pe.transpose(ps[:, 7, 0:P], mem.otm[:, i % 2, :], mem.ident[:, :]).then_inc(ot_done, 1)

                for n in range(NI + 3):
                    if n < NI:
                        scores(n)
                    if 1 <= n <= NI:
                        turn(n - 1)
                    if 2 <= n < NI + 2:
                        values(n - 2)
                    if n >= 4 and n % 2 == 0:
                        back((n - 4) // 2)
                pe.wait_ge(sm_ready, NI * p + NI)
                pe.wait_ge(pt_ready, NI * p + NI)
                pe.wait_ge(ot_ready, 8 * p + 8)
                pe.wait_ge(qs_ready, p + 1)
                for e in range(2):
                    if e:
                        pe.wait_ge(ssm_ready, 2 * p + 1)
                    for b in range(4):
                        n = 4 * e + b
                        pe.wait_ge(ck_in[n % 2], 16 * (4 * p + n // 2) + 16)
                        if n >= 2:
                            pe.wait_ge(kc_ready, NS * p + n - 2 + 3)
                        for a in range(4):
                            last = pe.transpose(ps[:, 2 + n % 2, a * P:(a + 1) * P], mem.ck[:, n % 2, a, :], mem.ident[:, :])
                        last.then_inc(kc_done, 1)
                        pe.wait_ge(kc_ready, NS * p + n + 3)
                        rows = slice(32 * b, 32 * b + 32)
                        q = mem.qs[:, n, :]
                        new = slice(TP + TS * n, TP + TS * n + TS)
                        pe.matmul(flat[rows, 0:512], q, mem.kc[:, n % 2, :], start=True, stop=True)
                        last = pe.matmul(flat[rows, 512:SPAN], q, mem.kT[:, new], start=True, stop=True)
                    last.then_inc(ssc_done, 1)
                    pe.wait_ge(spr_ready, 2 * p + e + 1)
                    if e:
                        pe.wait_ge(spt_ready, 2 * p + 1)
                    for j in range(4):
                        pe.transpose(flat[:, 2048 + j * P:2048 + (j + 1) * P], mem.pr[:, 0, j * P:(j + 1) * P], mem.ident[:, :])
                    pe.transpose(flat[:, 2048 + 512:2048 + 640], mem.pr[:, 1, 0:P], mem.ident[:, :]).then_inc(spt_done, 1)
                    pe.wait_ge(spt_ready, 2 * p + e + 1)
                    pe.wait_ge(cv_in, 128 * p + 64 * (e + 1))
                    if e:
                        pe.wait_ge(so_ready, 2 * p + 1)
                    for b in range(4):
                        out = ps[:, 6, 32 * b:32 * b + 32]
                        for j in range(4):
                            pe.matmul(out, mem.cv[:, b, j, :], mem.pt[:, 0, j * P + 32 * b:j * P + 32 * b + 32], start=(j == 0), stop=False)
                        last = pe.matmul(out, mem.vtm[:, 8, :], mem.pt[:, 0, 512 + 32 * b:512 + 32 * b + 32], start=False, stop=True)
                    last.then_inc(spv_done, 1)
                pe.wait_ge(s.w_split, 4 * p + 6)
                pe.wait_ge(ol_ready, p + 1)
                for k in range(KB):
                    pe.wait_ge(proj_free, KB * p + k + 1)
                    outer(pe, mem, ps[:, 3 * (k % 2):3 * (k % 2) + 3, :], [(1, mem.osp)], k).then_inc(proj_done, 1)
                pe.wait_ge(proj_done, KB * p + KB)
                pe.sem_inc(s.tile_done, 1)

        @block.scalar
        def _(act):
            act.sem_inc(kc_ready, 2)
            with act.Fori(0, PAIRS) as p:
                act.wait_ge(consts, 1)
                act.wait_ge(qkv_done, 3 * p + 1)
                for h, (lo, hi) in enumerate(halves):
                    act.mul(by3(mem.qz[lo:hi, h, :]), ps[lo:hi, 0:3, 0:CW], HD ** -0.5).then_inc(q_ready, 1)
                act.wait_ge(qkv_done, 3 * p + 3)
                act.copy(by3(mem.ofm[:, :]), ps[:, 0:3, 0:CW]).then_inc(v_ready, 1)
                act.wait_ge(q_ready, 2 * p + 2)
                act.copy(mem.qs[:, :, :].rearrange("p b (h t) -> p b h t", h=2),
                         mem.qz[:, :, TP:T].rearrange("p h (b t) -> p b h t", b=NS)).then_inc(qs_ready, 1)
                act.wait_ge(vt_done, p + 1)
                act.copy(mem.vtm[:, :, :].rearrange("p i c -> p (i c)"), flat[:, 2560:2560 + 9 * P]).then_inc(vtm_ready, 1)

                def expo(n):
                    i, h = ITEMS[n]
                    w = keys_of(i)[1] * P
                    act.wait_ge(nm_ready, NI * p + n + 1)
                    act.activation(mem.pr[:, n % 2, 0:w], mem.pr[:, n % 2, 0:w], ACT.Exp, bias=mem.nm[:, n:n + 1], accum_out=mem.rsum[:, n:n + 1]).then_inc(ex_ready, 1)

                def copy_pt(n):
                    w = keys_of(ITEMS[n][0])[1] * P
                    if n == 0:
                        act.wait_ge(kv_out, 64 * p + 64)
                    act.wait_ge(pt_done, NI * p + n + 1)
                    if n >= 2:
                        act.wait_ge(pv_done, NI * p + n - 1)
                    act.copy(mem.pt[:, n % 2, 0:w], flat[:, 2048:2048 + w]).then_inc(pt_ready, 1)

                for n in range(NI + 1):
                    if n < NI:
                        expo(n)
                    if n >= 1:
                        copy_pt(n - 1)
                for e in range(2):
                    for b in range(4):
                        n = 4 * e + b
                        act.wait_ge(kc_done, NS * p + n + 1)
                        if e and b == 0:
                            act.wait_ge(ssc_done, 2 * p + 1)
                        act.copy(mem.kc[:, n % 2, :], ps[:, 2 + n % 2, :]).then_inc(kc_ready, 1)
                    act.wait_ge(snm_ready, 2 * p + e + 1)
                    act.activation(mem.sx[:, :], mem.sx[:, :], ACT.Exp, bias=mem.nm[:, 16 + e:17 + e], accum_out=mem.rsum[:, 16 + e:17 + e]).then_inc(sex_ready, 1)
                    act.wait_ge(spt_done, 2 * p + e + 1)
                    if e:
                        act.wait_ge(spv_done, 2 * p + 1)
                    act.copy(mem.pt[:, 0, :], flat[:, 2048:2048 + 640]).then_inc(spt_ready, 1)
                act.wait_ge(so_ready, 2 * p + 2)
                act.wait_ge(ot_ready, 8 * p + 8)
                act.copy(mem.osp[:, 0, :], mem.ofm[:, :]).then_inc(oh_ready, 1)

        @block.vector
        def _(dve):
            dve.sem_inc(pair_done, 1)
            dve.sem_inc(proj_free, 2)
            with dve.Fori(0, PAIRS) as p:
                chain = Chain(dve, dve_chain, p, ATTENTION_LINKS)
                dve.wait_ge(qkv_done, 3 * p + 2)
                dve.tensor_copy(by3(mem.kT[:, :]), ps[:, 3:6, 0:CW]).then_inc(k_ready, 1)
                dve.wait_ge(kt_done, p + 1)
                dve.tensor_copy(mem.kout[:, :, :].rearrange("p i c -> p (i c)"), flat[:, 1536:1536 + 640]).then_inc(kout_ready, 1)
                dve.wait_ge(bias_in, 32 * p + 32)
                dve.wait_ge(bs_in, 128 * p + 128)
                for h in range(2):
                    chain.link(dve.memset(mem.bt[0:64, h, BAND - 64:BAND], NEG))
                    chain.link(dve.memset(mem.bt[64:128, h, 0:64], NEG))

                def biased(n):
                    i, h = ITEMS[n]
                    k0, nk = keys_of(i)
                    w, at = nk * P, 1024 * (n % 2)
                    dve.wait_ge(sc_done, NI * p + n + 1)
                    if n >= 2:
                        dve.wait_ge(pt_done, NI * p + n - 1)
                    dve.sem_inc(s.dve_passed, 1)
                    dve.tensor_tensor_reduce(mem.pr[:, n % 2, 0:w], flat[:, at:at + w], mem.bt[:, h, BAND - w:BAND], 1.0, -3e38,
                                             ALU.add, ALU.max, mem.mx[:, n:n + 1]).then_inc(sm_ready, 1)
                    dve.wait_ge(sm_ready, NI * p + n + 1)
                    dve.tensor_scalar(mem.nm[:, n:n + 1], mem.mx[:, n:n + 1], -1.0, None, ALU.mult).then_inc(nm_ready, 1)

                def scaled(n):
                    i, h = ITEMS[n]
                    dve.wait_ge(ex_ready, NI * p + n + 1)
                    chain.link(dve.reciprocal(mem.rinv[:, n:n + 1], mem.rsum[:, n:n + 1]))
                    dve.wait_ge(pv_done, NI * p + n + 1)
                    if i >= 2 and h == 0:
                        dve.wait_ge(ot_done, 8 * p + i - 1)
                    dve.tensor_scalar(mem.otm[:, i % 2, h * 64:(h + 1) * 64], ps[:, 6, 0:64], mem.rinv[:, n:n + 1], None, ALU.mult).then_inc(on_ready, 1)

                def home(i):
                    dve.wait_ge(ot_done, 8 * p + i + 1)
                    dve.tensor_copy(mem.ofm[:, i * P:(i + 1) * P], ps[:, 7, 0:P]).then_inc(ot_ready, 1)

                for n in range(NI + 3):
                    if n < NI:
                        biased(n)
                    if 2 <= n < NI + 2:
                        scaled(n - 2)
                    if n >= 4 and n % 2 == 0:
                        home((n - 4) // 2)
                for e in range(2):
                    hold(dve, s.dve_passed, ssc_done, 2 * p + e + 1)
                    dve.tensor_tensor_reduce(mem.sx[:, :], flat[:, 0:SPAN], mem.bs[:, :], 1.0, -3e38, ALU.add, ALU.max, mem.mx[:, 16 + e:17 + e]).then_inc(ssm_ready, 1)
                    dve.wait_ge(ssm_ready, 2 * p + e + 1)
                    dve.tensor_scalar(mem.nm[:, 16 + e:17 + e], mem.mx[:, 16 + e:17 + e], -1.0, None, ALU.mult).then_inc(snm_ready, 1)
                    dve.wait_ge(sex_ready, 2 * p + e + 1)
                    chain.link(dve.reciprocal(mem.rinv[:, 16 + e:17 + e], mem.rsum[:, 16 + e:17 + e]))
                    rinv = mem.rinv[:, 16 + e:17 + e]
                    if e:
                        dve.wait_ge(spt_done, 2 * p + 1)
                    chain.link(dve.tensor_scalar(mem.pr[:, 0, 0:512], mem.sx[:, 0:512], rinv, None, ALU.mult))
                    dve.scalar_tensor_tensor(mem.pr[:, 1, 0:P].rearrange("p (b t) -> p b t", b=NS), spread(mem.sx[:, 512:SPAN], NS), rinv,
                                             mem.smask[:, e, :].rearrange("p (b t) -> p b t", b=NS), ALU.mult, ALU.mult).then_inc(spr_ready, 1)
                    dve.wait_ge(spv_done, 2 * p + e + 1)
                    for h, (lo, hi) in enumerate(halves):
                        ins = dve.tensor_copy(mem.ofm[lo:hi, TP + 64 * e:TP + 64 * e + 64].rearrange("p (b t) -> p b t", b=4),
                                              ps[lo:hi, 6, 0:P].rearrange("p (b h t) -> p b h t", b=4, h=2)[:, :, h, :])
                        if h == 0:
                            chain.link(ins)
                    ins.then_inc(so_ready, 1)
                dve.wait_ge(oh_ready, p + 1)
                dve.tensor_tensor(mem.osp[:, 1, :], mem.ofm[:, :], mem.osp[:, 0, :].bitcast(F32), ALU.subtract).then_inc(ol_ready, 1)
                for k in range(KB):
                    dve.wait_ge(proj_done, KB * p + k + 1)
                    dve.tensor_tensor(by3(mem.H[:, k, :]), ps[:, 3 * (k % 2):3 * (k % 2) + 3, 0:CW], by3(mem.H[:, k, :]), ALU.add).then_inc(proj_free, 1)
                dve.wait_ge(proj_free, KB * p + KB + 2)
                dve.wait_ge(kv_out, 64 * p + 64)
                dve.sem_inc(pair_done, 1)
                chain.close("attention, VectorE")


OUTPUTS = [
    ("y_p", (1, TP, D)), ("y_s", (NS, TS, D)), ("wkv_p", (1, 1, 16, HD, HD)), ("shift_p", (1, 1, D)),
    ("k_p", (1, 1, 512, 16, HD)), ("v_p", (1, 1, 512, 16, HD)), ("wkv_s", (1, NS, 16, HD, HD)),
    ("shift_s", (1, NS, D)), ("k_s", (1, NS, TS, 16, HD)), ("v_s", (1, NS, TS, 16, HD)),
]
INPUTS = [
    "x_prompt", "x_sample", "state_wkv", "state_shift", "cache_k", "cache_v", "norm_mix", "norm_ffn", "norm_final",
    "rwkv_mu", "rwkv_w_rkv", "rwkv_w_out", "rwkv_decay_w0", "rwkv_decay_w1", "rwkv_decay_w2", "rwkv_iclr_a0",
    "rwkv_iclr_a1", "rwkv_iclr_a2", "rwkv_gate_g1", "rwkv_gate_g2", "rwkv_k_k", "rwkv_k_a", "rwkv_r_k",
    "rwkv_lnx_w", "rwkv_lnx_b", "attn_w_qkv", "attn_w_out", "attn_rel_bias", "ffn_w_gu", "ffn_w_down",
]


def build(nc, t, o):
    mem = Memory()
    with ExitStack() as ctx:
        def sb(stack, name, shape, dt=F32):
            return stack.enter_context(nc.sbuf_tensor(name, shape, dt))

        mem.H = sb(ctx, "H", [P, KB, T])
        mem.stage = sb(ctx, "stage", [P, 2, 1024])
        mem.wsplit = sb(ctx, "wsplit", [P, 2, 2, 1024], F32R)
        mem.ident = sb(ctx, "ident", [P, P])
        mem.ones = sb(ctx, "ones", [P, P])
        mem.headones = sb(ctx, "headones", [P, P])
        mem.vec = sb(ctx, "vec", [P, KB, NROW])
        mem.omu = sb(ctx, "omu", [P, KB, 6])
        mem.ps = ctx.enter_context(nc.psum_tensor("ps", [P, 8, 512], F32))
        mem.rkv_dram = nc.dram_tensor("rkv_scratch", (3, D, T), F32, kind="Internal").ap()
        mem.ext_dram = nc.dram_tensor("bias_scratch", (16, 768), F32, kind="Internal").ap()
        mem.tab_dram = nc.dram_tensor("bias_table", (16, P, BAND), F32, kind="Internal").ap()

        setup_and_rwkv(nc, t, mem, o, sb)
        with ExitStack() as later:
            mem.xs = sb(later, "xs", [P, 2, KB, T], F32R)
            mem.rstd = sb(later, "rstd", [P, T])

            def norm(n, gain, to):
                with ExitStack() as stack:
                    mem.tt = sb(stack, f"tt{n}", [P, 2, T])
                    mem.yrow = sb(stack, f"yrow{n}", [P, 2, D])
                    norm_phase(nc, mem, o, gain, to)

            def ffn(layer):
                with ExitStack() as stack:
                    mem.hid = sb(stack, f"hid{layer}", [P, 2, 2, T], F32R)
                    mem.sg = sb(stack, f"sg{layer}", [P, T])
                    mem.hf = sb(stack, f"hf{layer}", [P, T])
                    ffn_phase(nc, t, mem, layer)

            norm(0, "ffn0", "split")
            ffn(0)
            norm(1, "mix1", "split")
            with ExitStack() as att:
                attention_memory(att, mem, sb)
                attention_phase(nc, t, mem, o)
            norm(2, "ffn1", "split")
            ffn(1)
            norm(3, "final", "out")


def setup_and_rwkv(nc, t, mem, o, sb):
    with ExitStack() as rwkv:
        mem.lora_wa = sb(rwkv, "lora_wa", [P, T])
        mem.lora_g = sb(rwkv, "lora_g", [P, T])
        mem.lora_g2 = sb(rwkv, "lora_g2", [P, T])
        with ExitStack() as before:
            mem.xnp = sb(before, "xnp", [P, KB, TPAD])
            with ExitStack() as first:
                mem.xrow = sb(first, "xrow", [P, 2, D])
                mem.rows = sb(first, "rows", [NROW, D])
                mem.sq0 = sb(first, "sq0", [P, 2, T])
                mem.rs0 = sb(first, "rs0", [P, T])
                mem.shiftcol = sb(first, "shiftcol", [P, KB, 1 + NS])
                mem.shiftrow = sb(first, "shiftrow", [1 + NS, D])
                setup_phase(nc, t, mem)
                norm_phase(nc, mem, o, "mix0", "padded")
            with ExitStack() as mix:
                mem.mixed = sb(mix, "mixed", [P, 2, KB, T], F32R)
                mem.mt1 = sb(mix, "mt1", [P, 2, TPAD])
                mem.mt2 = sb(mix, "mt2", [P, 2, TPAD])
                mem.rkvout = (mem.lora_g, mem.lora_g2)
                mix_phase(nc, t, mem)
        with ExitStack() as scan:
            mem.oh = sb(scan, "oh", [P, 2, T], F32R)
            mem.arena = sb(scan, "arena", [P, (nc.sbuf_bytes_remaining - 64) // 4])
            recurrence_phase(nc, t, mem, o)


def attention_memory(att, mem, sb):
    mem.qz = sb(att, "qz", [P, 2, T])
    mem.kT = sb(att, "kT", [P, T])
    mem.vtm = sb(att, "vtm", [P, 9, P])
    mem.ofm = mem.rstd
    mem.osp = sb(att, "osp", [P, 2, T], F32R)
    mem.bt = sb(att, "bt", [P, 2, BAND])
    mem.bs = sb(att, "bs", [P, SPAN])
    mem.pr = sb(att, "pr", [P, 2, BAND])
    mem.pt = sb(att, "pt", [P, 2, BAND])
    mem.sx = sb(att, "sx", [P, SPAN])
    mem.otm = sb(att, "otm", [P, 2, P])
    mem.qs = sb(att, "qs", [P, NS, 32])
    mem.kc = sb(att, "kc", [P, 2, 512])
    mem.smask = sb(att, "smask", [P, 2, P])
    mem.mx, mem.nm, mem.rsum, mem.rinv = (sb(att, x, [P, 18]) for x in ("mx", "nm", "rsum", "rinv"))
    mem.cv = sb(att, "cv", [P, 4, 4, P])
    mem.ck = sb(att, "ck", [P, 2, 4, P])
    mem.kout = mem.pt[:, :, :].rearrange("p a c -> p (a c)")[:, 0:640].rearrange("p (i c) -> p i c", i=5)


def kernel(**inputs):
    import concourse.bacc as bacc
    from concourse.bass_utils import run_bass_kernel_spmd

    nc = bacc.Bacc("TRN2", target_bir_lowering=False, num_devices=1)
    arrays = {f"in_{n}": np.ascontiguousarray(inputs[n]) for n in INPUTS}
    t = {n: nc.dram_tensor(f"in_{n}", arrays[f"in_{n}"].shape, F32, kind="ExternalInput").ap() for n in INPUTS}
    o = {n: nc.dram_tensor(f"out_{n}", shape, F32, kind="ExternalOutput").ap() for n, shape in OUTPUTS}
    build(nc, t, o)
    got = run_bass_kernel_spmd(nc, [arrays], core_ids=[0]).results[0]
    return tuple(got[f"out_{n}"] for n, _ in OUTPUTS)
```

```python
from contextlib import ExitStack

import numpy as np

import concourse.bass as bass
from concourse import mybir

F32 = mybir.dt.float32
F32R = mybir.dt.float32r
ALU = mybir.AluOpType
ACT = mybir.ActivationFunctionType
AX = mybir.AxisListType

P = 128
D = 1024
KB = D // P
TP = 1024
NS, TS = 8, 16
T = TP + NS * TS
CW = T // 3
DFF = 2816
HB = DFF // P
HD = 64
PAIRS = D // P
BAND = 640
CACHE = 512
SPAN = CACHE + TS
REL = 320
NEG = -1e30
RMS_EPS = 1e-6
LNX_EPS = 64e-5
DECAY = float(np.exp(-0.5))
PROMPT_PAD = 1
TPAD = PROMPT_PAD + TP + NS * (TS + 1)
CHUNK = 64
NCH = T // CHUNK
GROUPS = [(0, 3), (3, 3), (6, 3), (9, 3), (12, 4), (16, 2)]
VEC = {n: i for i, n in enumerate(
    ["mix0", "mix1", "ffn0", "ffn1", "final", "mu0", "mu1", "mu2", "mu3", "mu4", "mu5",
     "w0", "a0", "kk", "ka", "rk", "lnw", "lnb"])}
NV = len(VEC)
NROW = NV + NS


class Chain:

    def __init__(self, eng, sem, turn=0, per=0, start=0):
        self.eng, self.sem, self.base, self.per, self.n = eng, sem, turn * per + start, per, 0

    def link(self, ins):
        self.n += 1
        ins.then_inc(self.sem, 1)
        self.eng.wait_ge(self.sem, self.base + self.n)

    def mark(self, ins):
        self.n += 1
        ins.then_inc(self.sem, 1)

    def gather(self):
        self.eng.wait_ge(self.sem, self.base + self.n)

    def close(self, what):
        assert self.n == self.per, f"{what}: {self.n} links a turn, not {self.per}"

LINKS_START, LINKS_TURN = 8, 18
ATTENTION_LINKS = 24


def hold(eng, passed, sem, value):
    eng.wait_ge(sem, value)
    eng.sem_inc(passed, 1)


class Memory:
    pass


def split_weight(pool, mem, u, chain, n=1024):
    chain.link(pool.tensor_scalar(mem.wsplit[:, u, 0, 0:n], mem.stage[:, u, 0:n], 1.0, None, ALU.mult))
    return pool.tensor_tensor(mem.wsplit[:, u, 1, 0:n], mem.stage[:, u, 0:n],
                              mem.wsplit[:, u, 0, 0:n].bitcast(F32), ALU.subtract)


def split_tiles(pool, mem, s, tiles):
    pool.sem_inc(s.w_split, 2)
    with pool.Fori(0, tiles // 2) as i:
        chain = Chain(pool, s.pool_chain, i, 2)
        for u in range(2):
            pool.wait_ge(s.w_load[u], 16 * i + 16)
            hold(pool, s.pool_passed, s.tile_done, 2 * i + u + 1)
            split_weight(pool, mem, u, chain).then_inc(s.w_split, 1)
        chain.close("split_tiles")


def weight_sems(sem, s):
    s.w_load = [sem("w_load0"), sem("w_load1")]
    s.w_split = sem("w_split")
    s.tile_done = sem("tile_done")
    s.pool_chain = sem("pool_chain")
    s.sp_passed, s.pool_passed, s.dve_passed = sem("sp_passed"), sem("pool_passed"), sem("dve_passed")


PASSES = ((0, 0), (0, 1), (1, 0))


def product(pe, mem, ps3, u, x, blocks_ready=None):
    for k in range(KB):
        if blocks_ready is not None:
            pe.wait_ge(blocks_ready, k + 1)
        for a, (w, part) in enumerate(PASSES):
            for c in range(3):
                last = pe.matmul(ps3[:, c, 0:CW], mem.wsplit[:, u, w, k * P:(k + 1) * P],
                                 x[:, part, k, c * CW:(c + 1) * CW],
                                 start=(k == 0 and a == 0), stop=(k == KB - 1 and a == 2))
    return last


def outer(pe, mem, ps3, blocks, m):
    n = len(blocks)
    for b, (u, x) in enumerate(blocks):
        for a, (w, part) in enumerate(PASSES):
            for c in range(3):
                last = pe.matmul(ps3[:, c, 0:CW], mem.wsplit[:, u, w, m * P:(m + 1) * P],
                                 x[:, part, c * CW:(c + 1) * CW],
                                 start=(b == 0 and a == 0), stop=(b == n - 1 and a == 2))
    return last


def by3(ap):
    return ap.rearrange("p (c n) -> p c n", c=3)


def streams(ap):
    return ap[:, TP + 1:TPAD].rearrange("p (b t) -> p b t", b=NS)[:, :, 0:TS]


def chunks(ap):
    return ap.rearrange("p (n c) -> p n c", c=CHUNK)


def spread(ap, n):
    return ap.unsqueeze(1).to_broadcast((ap.shape[0], n, ap.shape[1]))


def phase_semaphores(nc, ctx, phase):
    held = []

    def sem(name):
        held.append(nc.alloc_semaphore(f"{name}_{phase}"))
        return held[-1]

    def give_back():
        nc.clear_and_free_semaphores(held)
        nc.all_engine_barrier()
    ctx.callback(give_back)
    return sem


def setup_phase(nc, t, mem):
    with ExitStack() as ctx:
        sem = phase_semaphores(nc, ctx, "setup")
        rows_in, x_in = sem("rows_in"), [sem("x_in0"), sem("x_in1")]
        pool_chain, consts = sem("pool_chain"), sem("consts")
        turned, rows_turned, act_out, dve_out = sem("turned"), sem("rows_turned"), sem("act_out"), sem("dve_out")
        vec_ready, omu_ready = sem("vec_ready"), sem("omu_ready")
        bias_in, ext_ready, ext_out = sem("bias_in"), sem("ext_ready"), sem("ext_out")
        block = ctx.enter_context(nc.Block())
        sources = [t["norm_mix"][0:1, :], t["norm_mix"][1:2, :], t["norm_ffn"][0:1, :], t["norm_ffn"][1:2, :],
                   t["norm_final"].rearrange("(a d) -> a d", a=1), t["rwkv_mu"][0],
                   t["rwkv_decay_w0"], t["rwkv_iclr_a0"], t["rwkv_k_k"], t["rwkv_k_a"],
                   t["rwkv_r_k"].rearrange("n h c -> n (h c)"), t["rwkv_lnx_w"], t["rwkv_lnx_b"],
                   t["state_shift"][0]]
        bias, ext = mem.sq[0:16, 0, 0:REL], mem.sq[0:16, 1, 0:768]
        xp, xs = t["x_prompt"][0], t["x_sample"].rearrange("b t d -> (b t) d")

        @block.sync
        def _(sp):
            for i in range(T // P):
                if i >= 2:
                    sp.wait_ge(turned, 2 * (i - 1))
                src = xp[i * P:(i + 1) * P, :] if i < TP // P else xs
                sp.dma_start(mem.xrow[:, i % 2, :], src).then_inc(x_in[i % 2], 16)

        @block.gpsimd
        def _(pool):
            chain = Chain(pool, pool_chain)
            chain.link(pool.memset(mem.ones[:, :], 1.0))
            pool.affine_select(out=mem.ident[:, :], in_=mem.ones[:, :], compare_op=ALU.is_equal, fill=0.0,
                               base=0, pattern=[[-1, P]], channel_multiplier=1).then_inc(consts, 1)
            chain.link(pool.memset(mem.headones[:, :], 0.0))
            pool.memset(mem.headones[0:64, 0:64], 1.0).then_inc(consts, 1)
            pool.memset(mem.headones[64:128, 64:128], 1.0).then_inc(consts, 1)

        @block.tensor
        def _(pe):
            pe.wait_ge(consts, 1)
            for i in range(T // P):
                pe.wait_ge(x_in[i % 2], 16 * (i // 2 + 1))
                for half in range(2):
                    n = 2 * i + half
                    if n >= 6:
                        pe.wait_ge(dve_out if half else act_out, i - 2)
                    for k in range(4):
                        last = pe.transpose(mem.ps[:, n % 6, k * P:(k + 1) * P],
                                            mem.xrow[:, i % 2, (4 * half + k) * P:(4 * half + k + 1) * P], mem.ident[:, :])
                    last.then_inc(turned, 1)
            pe.wait_ge(rows_in, 16 * len(sources))
            for k in range(KB):
                last = pe.transpose(mem.ps[:, 7, k * NROW:(k + 1) * NROW], mem.rows[:, k * P:(k + 1) * P], mem.ident[0:NROW, 0:NROW])
            last.then_inc(rows_turned, 1)

        @block.scalar
        def _(act):
            at = 0
            for src in sources:
                n = src.shape[0]
                act.dma_start(mem.rows[at:at + n, :], src).then_inc(rows_in, 16)
                at += n
            act.dma_start(bias, t["attn_rel_bias"][0]).then_inc(bias_in, 16)
            for i in range(T // P):
                if i == 5:
                    act.wait_ge(ext_ready, 3)
                    act.dma_start(mem.ext_dram[:, :], ext).then_inc(ext_out, 16)
                act.wait_ge(turned, 1 + 2 * i)
                act.copy(mem.H[:, 0:4, i * P:(i + 1) * P],
                         mem.ps[:, (2 * i) % 6, :].rearrange("p (k n) -> p k n", k=4)).then_inc(act_out, 1)
            act.wait_ge(ext_out, 16)

        @block.vector
        def _(dve):
            dve.wait_ge(bias_in, 16)
            dve.tensor_copy(ext[:, 0:384], bias[:, REL - 1:REL].to_broadcast((16, 384))).then_inc(ext_ready, 1)
            dve.tensor_copy(ext[:, 384:384 + REL - 1], bass.AP(bias.tensor, bias.offset + REL - 2, [bias.ap[0], [-1, REL - 1]])).then_inc(ext_ready, 1)
            dve.tensor_copy(ext[:, 383 + REL:768], bias[:, 0:1].to_broadcast((16, 385 - REL))).then_inc(ext_ready, 1)
            for i in range(T // P):
                dve.wait_ge(turned, 2 + 2 * i)
                dve.tensor_copy(mem.H[:, 4:8, i * P:(i + 1) * P],
                                mem.ps[:, (2 * i + 1) % 6, :].rearrange("p (k n) -> p k n", k=4)).then_inc(dve_out, 1)
            dve.wait_ge(rows_turned, 1)
            dve.tensor_copy(mem.vec[:, :, :], mem.ps[:, 7, 0:KB * NROW].rearrange("p (k n) -> p k n", k=KB)).then_inc(vec_ready, 1)
            dve.wait_ge(vec_ready, 1)
            dve.tensor_scalar(mem.omu[:, :, :], mem.vec[:, :, VEC["mu0"]:VEC["mu0"] + 6], -1.0, 1.0, ALU.mult, ALU.add).then_inc(omu_ready, 1)


class Norm:

    def __init__(self, mem, sem, gain, tt, total):
        self.mem, self.gain, self.tt, self.total = mem, VEC[gain], tt, total
        self.selected, self.sq_act, self.sq_dve, self.sums_done, self.sums_read = (sem(x) for x in
            ("selected", "sq_act", "sq_dve", "sums_done", "sums_read"))
        self.inverse, self.root, self.turned, self.turned_read, self.spread_done = (sem(x) for x in
            ("inverse", "root", "turned", "turned_read", "spread_done"))
        self.t_ready, self.hi_ready, self.lo_done = sem("t_ready"), sem("hi_ready"), sem("lo_done")

    def pool(self, pool):
        sel = self.mem.sel9[0:9, :].rearrange("p (i c) -> p i c", i=9)
        pool.memset(sel, 1.0).then_inc(self.selected, 1)
        pool.wait_ge(self.selected, 1)
        pool.affine_select(out=sel, in_=sel, compare_op=ALU.is_equal, fill=0.0, base=0, pattern=[[-1, 9], [0, P]],
                           channel_multiplier=1).then_inc(self.selected, 1)

    def tensor(self, pe):
        mem = self.mem
        pe.wait_ge(self.sq_dve, KB)
        for i in range(9):
            last = pe.matmul(mem.ps[:, 7, i:i + 1], self.total[:, i * P:(i + 1) * P], mem.ones[:, 0:1], start=True, stop=True)
        last.then_inc(self.sums_done, 1)
        pe.wait_ge(self.root, 1)
        pe.transpose(mem.ps[0:9, 6, 0:P], mem.rms[:, 0:9], mem.ident[:, :]).then_inc(self.turned, 1)
        pe.wait_ge(self.turned_read, 1)
        pe.wait_ge(self.selected, 2)
        for i in range(9):
            last = pe.matmul(mem.ps[:, 3 + i // 3, (i % 3) * P:(i % 3 + 1) * P], mem.sel9[0:9, i * P:(i + 1) * P], mem.rmst[0:9, :], start=True, stop=True)
        last.then_inc(self.spread_done, 1)

    def scalar(self, act):
        mem = self.mem
        for k in range(KB - 1):
            if k >= 2:
                act.wait_ge(self.sq_dve, k)
            act.activation(self.tt[:, k % 2, :], mem.H[:, k, :], ACT.Square).then_inc(self.sq_act, 1)
        act.wait_ge(self.inverse, 1)
        act.activation(mem.rms[:, :], mem.rms[:, :], ACT.Sqrt).then_inc(self.root, 1)

    def vector(self, dve):
        mem = self.mem
        total = self.total
        dve.tensor_tensor(total, mem.H[:, KB - 1, :], mem.H[:, KB - 1, :], ALU.mult).then_inc(self.sq_dve, 1)
        for k in range(KB - 1):
            dve.wait_ge(self.sq_act, k + 1)
            dve.wait_ge(self.sq_dve, k + 1)
            dve.tensor_tensor(total, total, self.tt[:, k % 2, :], ALU.add).then_inc(self.sq_dve, 1)
        dve.wait_ge(self.sums_done, 1)
        dve.tensor_scalar(mem.rms[:, :], mem.ps[:, 7, 0:9], 1.0 / D, RMS_EPS, ALU.mult, ALU.add).then_inc(self.sums_read, 1)
        dve.wait_ge(self.sums_read, 1)
        dve.reciprocal(mem.rms[:, :], mem.rms[:, :]).then_inc(self.inverse, 1)
        dve.wait_ge(self.turned, 1)
        dve.tensor_copy(mem.rmst[0:9, :], mem.ps[0:9, 6, 0:P]).then_inc(self.turned_read, 1)
        dve.wait_ge(self.spread_done, 1)

    def scalar_split(self, act):
        tt = self.tt
        for k in range(KB):
            act.wait_ge(self.t_ready, k + 1)
            act.copy(self.mem.xs[:, 0, k, :], tt[:, k % 2, :]).then_inc(self.hi_ready, 1)

    def vector_split(self, dve):
        mem, tt = self.mem, self.tt

        def write(k):
            if k >= 2:
                dve.wait_ge(self.lo_done, k - 1)
            dve.scalar_tensor_tensor(by3(tt[:, k % 2, :]), by3(mem.H[:, k, :]), mem.vec[:, k, self.gain:self.gain + 1],
                                     mem.ps[:, 3:6, 0:CW], ALU.mult, ALU.mult).then_inc(self.t_ready, 1)
        write(0)
        for k in range(KB):
            if k + 1 < KB:
                write(k + 1)
            dve.wait_ge(self.hi_ready, k + 1)
            dve.wait_ge(self.t_ready, k + 1)
            dve.tensor_tensor(mem.xs[:, 1, k, :], tt[:, k % 2, :], mem.xs[:, 0, k, :].bitcast(F32), ALU.subtract).then_inc(self.lo_done, 1)


def norm_phase(nc, mem, o, gain, to):
    with ExitStack() as ctx:
        sem = phase_semaphores(nc, ctx, gain)
        norm = Norm(mem, sem, gain, mem.sq, mem.total[:, :])
        t_ready, dve_chain = norm.t_ready, sem("dve_chain")
        rows_turned, rows_out, rows_out_act, col_ready, stored = (sem(x) for x in
            ("rows_turned", "rows_out", "rows_out_act", "col_ready", "stored"))
        store_free = [sem("store0"), sem("store1")]
        block = ctx.enter_context(nc.Block())
        g = VEC[gain]
        pads = lambda k: mem.xnp[:, k, PROMPT_PAD + TP:TPAD].rearrange("p (b t) -> p b t", b=NS)
        half_bank = lambda n: (0, 1, 2, 6)[n % 4]

        @block.gpsimd
        def _(pool):
            norm.pool(pool)

        @block.tensor
        def _(pe):
            norm.tensor(pe)
            if to == "padded":
                pe.wait_ge(col_ready, 2)
                for k in range(KB):
                    last = pe.transpose(mem.ps[0:1 + NS, k // 4, (k % 4) * P:(k % 4 + 1) * P], mem.shiftcol[:, k, :], mem.ident[:, :])
                last.then_inc(rows_turned, 1)
            if to == "out":
                pe.wait_ge(t_ready, KB)
                for i in range(T // P):
                    for half in range(2):
                        n = 2 * i + half
                        if n >= 4:
                            pe.wait_ge(rows_out if half else rows_out_act, i - 1)
                        for k in range(4):
                            last = pe.transpose(mem.ps[:, half_bank(n), k * P:(k + 1) * P],
                                                mem.H[:, 4 * half + k, i * P:(i + 1) * P], mem.ident[:, :])
                        last.then_inc(rows_turned, 1)

        @block.scalar
        def _(act):
            norm.scalar(act)
            if to == "out":
                for i in range(T // P):
                    if i >= 2:
                        act.wait_ge(store_free[i % 2], 16 * (i // 2))
                    act.wait_ge(rows_turned, 2 * i + 1)
                    act.copy(mem.yrow[:, i % 2, 0:512], mem.ps[:, half_bank(2 * i), :]).then_inc(rows_out_act, 1)

        @block.vector
        def _(dve):
            chain = Chain(dve, dve_chain)
            if to == "padded":
                chain.link(dve.memset(mem.xnp[:, :, 0:1], 0.0))
                for k in range(KB):
                    chain.link(dve.tensor_copy(pads(k)[:, :, 0], mem.vec[:, k, NV:NROW]))
            norm.vector(dve)
            if to == "padded":
                for k in range(KB):
                    gk = mem.vec[:, k, g:g + 1]
                    for c in range(3):
                        hi = min(TP, (c + 1) * CW)
                        chain.mark(dve.scalar_tensor_tensor(mem.xnp[:, k, PROMPT_PAD + c * CW:PROMPT_PAD + hi], mem.H[:, k, c * CW:hi], gk,
                                                            mem.ps[:, 3 + c, 0:hi - c * CW], ALU.mult, ALU.mult))
                    chain.mark(dve.scalar_tensor_tensor(
                        pads(k)[:, :, 1:1 + TS], mem.H[:, k, TP:T].rearrange("p (b t) -> p b t", b=NS), gk,
                        mem.ps[:, 5, TP - 2 * CW:CW].rearrange("p (b t) -> p b t", b=NS), ALU.mult, ALU.mult))
                chain.gather()
                dve.tensor_copy(mem.shiftcol[:, :, 0], mem.xnp[:, :, TP]).then_inc(col_ready, 1)
                dve.tensor_copy(mem.shiftcol[:, :, 1:1 + NS],
                                mem.xnp[:, :, PROMPT_PAD + TP:TPAD].rearrange("p k (b t) -> p k b t", b=NS)[:, :, :, TS]).then_inc(col_ready, 1)
                dve.wait_ge(rows_turned, 1)
                dve.tensor_copy(mem.shiftrow[:, :].rearrange("p (a n) -> p a n", a=2), mem.ps[0:1 + NS, 0:2, :]).then_inc(rows_out, 1)
            else:
                for k in range(KB):
                    dve.scalar_tensor_tensor(by3(mem.H[:, k, :]), by3(mem.H[:, k, :]), mem.vec[:, k, g:g + 1], mem.ps[:, 3:6, 0:CW],
                                             ALU.mult, ALU.mult).then_inc(t_ready, 1)
                for i in range(T // P):
                    if i >= 2:
                        dve.wait_ge(store_free[i % 2], 16 * (i // 2))
                    dve.wait_ge(rows_turned, 2 * i + 2)
                    dve.tensor_copy(mem.yrow[:, i % 2, 512:1024], mem.ps[:, half_bank(2 * i + 1), :]).then_inc(rows_out, 1)

        @block.sync
        def _(sp):
            if to == "padded":
                sp.dma_start(mem.h_dram.rearrange("p (k n) -> p k n", k=KB), mem.H[:, :, :]).then_inc(stored, 16)
                sp.dma_start(mem.tab_dram[:, :, :], bass.AP(mem.ext_dram.tensor, mem.ext_dram.offset + P - 1, [[768, 16], [-1, P], [1, BAND]])
                             ).then_inc(stored, 16)
                sp.wait_ge(rows_out, 1)
                sp.dma_start(o["shift_p"][0], mem.shiftrow[0:1, :]).then_inc(stored, 16)
                sp.dma_start(o["shift_s"][0], mem.shiftrow[1:1 + NS, :]).then_inc(stored, 16)
                sp.wait_ge(stored, 64)
            if to == "out":
                for i in range(T // P):
                    sp.wait_ge(rows_out, i + 1)
                    sp.wait_ge(rows_out_act, i + 1)
                    dst = o["y_p"][0, i * P:(i + 1) * P, :] if i < TP // P else o["y_s"].rearrange("b t d -> (b t) d")
                    sp.dma_start(dst, mem.yrow[:, i % 2, :]).then_inc(store_free[i % 2], 16)
                sp.wait_ge(store_free[0], 16 * 5)
                sp.wait_ge(store_free[1], 16 * 4)


def mix_phase(nc, t, mem):
    JOBS = [(0, 8, "r"), (3, 1, "w"), (1, 8, "k"), (4, 1, "a"), (2, 8, "v"), (5, 2, "g")]
    FIRST = [sum(b for _, b, _ in JOBS[:j]) for j in range(len(JOBS))]
    TILES = sum(b for _, b, _ in JOBS)
    RKV = {"r": 0, "k": 1, "v": 2}
    with ExitStack() as ctx:
        sem = phase_semaphores(nc, ctx, "mix")
        s = Memory()
        weight_sems(sem, s)
        scaled, summed, hi_done, lo_done = sem("scaled"), sem("summed"), sem("hi_done"), sem("lo_done")
        mix_used = sem("mix_used")
        ps_free = sem("ps_free")
        out_ready, out_stored = sem("out_ready"), [sem("out_stored0"), sem("out_stored1")]
        block = ctx.enter_context(nc.Block())
        wr = t["rwkv_w_rkv"][0]

        @block.sync
        def _(sp):
            def slot(n):
                return mem.stage[:, n % 2, :].rearrange("p (k m) -> p k m", k=KB)

            for j, (mu, blocks, what) in enumerate(JOBS):
                n0 = FIRST[j]
                if what in RKV:
                    rank = RKV[what]
                    w = wr[rank].rearrange("(k p) m -> p k m", p=P)
                    with sp.Fori(0, 4) as i:
                        for u in range(2):
                            hold(sp, s.sp_passed, s.w_split, n0 + 2 * i + u + 1)
                            sp.dma_start(slot(n0 + u), w[:, :, bass.ds((2 * i + u) * P, P)]).then_inc(s.w_load[(n0 + u) % 2], 16)
                else:
                    for u in range(blocks):
                        n = n0 + u
                        hold(sp, s.sp_passed, s.w_split, n + 1)
                        if what == "g":
                            g1 = t["rwkv_gate_g1"][0].rearrange("(k p) m -> p k m", p=P)
                            sp.dma_start(slot(n), g1[:, :, 32 * u:32 * u + P]).then_inc(s.w_load[n % 2], 16)
                        else:
                            sp.dma_start(slot(n)[:, :, 0:64], t["rwkv_decay_w1"][0].rearrange("(k p) m -> p k m", p=P)
                                         ).then_inc(s.w_load[n % 2], 16)
                            sp.dma_start(slot(n)[:, :, 64:128], t["rwkv_iclr_a1"][0].rearrange("(k p) m -> p k m", p=P)
                                         ).then_inc(s.w_load[n % 2], 16)

        @block.gpsimd
        def _(pool):
            pool.sem_inc(s.w_split, 2)
            loads = [0, 0]
            for j, (mu, blocks, what) in enumerate(JOBS):
                n0 = FIRST[j]
                if what in RKV:
                    with pool.Fori(0, 4) as i:
                        chain = Chain(pool, s.pool_chain, n0 + 2 * i, 1)
                        for u in range(2):
                            v = (n0 + u) % 2
                            pool.wait_ge(s.w_load[v], loads[v] + 16 * i + 16)
                            hold(pool, s.pool_passed, s.tile_done, n0 + 2 * i + u + 1)
                            split_weight(pool, mem, v, chain).then_inc(s.w_split, 1)
                    loads = [x + 64 for x in loads]
                else:
                    chain = Chain(pool, s.pool_chain, n0, 1)
                    for u in range(blocks):
                        v = (n0 + u) % 2
                        loads[v] += 16 if what == "g" else 32
                        pool.wait_ge(s.w_load[v], loads[v])
                        hold(pool, s.pool_passed, s.tile_done, n0 + u + 1)
                        split_weight(pool, mem, v, chain).then_inc(s.w_split, 1)

        @block.tensor
        def _(pe):
            pe.sem_inc(s.tile_done, 2)

            def tile(n, v, j):
                pe.wait_ge(s.w_split, n + 3)
                pe.wait_ge(ps_free, n + 1)
                for k in range(KB):
                    pe.wait_ge(lo_done, KB * j + k + 1)
                    for a, (w, part) in enumerate(PASSES):
                        for c in range(3):
                            last = pe.matmul(mem.ps[:, 3 * v + c, 0:CW], mem.wsplit[:, v, w, k * P:(k + 1) * P],
                                             mem.mixed[:, part, k, c * CW:(c + 1) * CW],
                                             start=(k == 0 and a == 0), stop=(k == KB - 1 and a == 2))
                    last.then_inc(mix_used if k < KB - 1 else s.tile_done, 1)

            for j, (mu, blocks, what) in enumerate(JOBS):
                n0 = FIRST[j]
                if blocks == 8:
                    with pe.Fori(0, 4) as i:
                        for u in range(2):
                            tile(n0 + 2 * i + u, (n0 + u) % 2, j)
                else:
                    for u in range(blocks):
                        tile(n0 + u, (n0 + u) % 2, j)


        @block.scalar
        def _(act):
            act.sem_inc(ps_free, 2)

            def mix(j, mu):
                def scale(k):
                    if KB * j + k >= 2:
                        act.wait_ge(summed, KB * j + k - 1)
                    act.activation(mem.mt1[:, k % 2, 0:TPAD - 1], mem.xnp[:, k, 1:TPAD], ACT.Copy, scale=mem.omu[:, k, mu:mu + 1]).then_inc(scaled, 1)

                def hi(k):
                    act.wait_ge(summed, KB * j + k + 1)
                    if j:
                        if k < KB - 1:
                            act.wait_ge(mix_used, 7 * (FIRST[j] - 1) + k + 1)
                        else:
                            act.wait_ge(s.tile_done, FIRST[j] + 2)
                    act.copy(mem.mixed[:, 0, k, 0:TP], mem.mt2[:, k % 2, 0:TP]).then_inc(hi_done, 1)
                    act.copy(mem.mixed[:, 0, k, TP:T].rearrange("p (b t) -> p b t", b=NS), streams(mem.mt2[:, k % 2, :])).then_inc(hi_done, 1)

                scale(0)
                for k in range(KB):
                    if k + 1 < KB:
                        scale(k + 1)
                    hi(k)

            def leave(j, m_lo, m_hi):
                what = JOBS[j][2]
                n0 = FIRST[j]

                def one(n, m, v, even):
                    act.wait_ge(s.tile_done, n + 3)
                    ps3 = mem.ps[:, 3 * v:3 * v + 3, 0:CW]
                    if what in RKV:
                        act.wait_ge(out_stored[even], 16 * (4 * RKV[what]) + 8 * (m - even) + 16)
                        act.copy(by3(mem.rkvout[even][:, :]), ps3).then_inc(out_ready, 1)
                        act.wait_ge(out_ready, 8 * RKV[what] + m + 1)
                        act.dma_start(mem.rkv_dram[RKV[what], bass.ds(m * P, P), :], mem.rkvout[even][:, :]).then_inc(out_stored[even], 16)
                        act.sem_inc(ps_free, 1)
                    elif what == "w":
                        act.activation(by3(mem.lora_wa[0:64, :]), ps3[0:64], ACT.Tanh).then_inc(ps_free, 1)
                    elif what == "a":
                        act.copy(by3(mem.lora_wa[64:128, :]), ps3[64:128]).then_inc(ps_free, 1)
                    elif m == 0:
                        act.wait_ge(out_stored[0], 16 * 13)
                        act.activation(by3(mem.lora_g[:, :]), ps3, ACT.Sigmoid).then_inc(ps_free, 1)
                    else:
                        act.wait_ge(out_stored[1], 16 * 13)
                        act.activation(by3(mem.lora_g2[96:128, :]), ps3[96:128], ACT.Sigmoid).then_inc(ps_free, 1)

                m = m_lo
                if m_hi - m_lo >= 6:
                    with act.Fori(0, 3) as i:
                        for u in range(2):
                            one(n0 + m + 2 * i + u, m + 2 * i + u, (n0 + m + u) % 2, (m + u) % 2)
                    m += 6
                for m in range(m, m_hi):
                    one(n0 + m, m, (n0 + m) % 2, m % 2)

            act.sem_inc(out_stored[0], 16)
            act.sem_inc(out_stored[1], 16)
            for j, (mu, blocks, what) in enumerate(JOBS):
                mix(j, mu)
                if j:
                    leave(j - 1, JOBS[j - 1][1] - 1, JOBS[j - 1][1])
                leave(j, 0, blocks - 1)
            leave(len(JOBS) - 1, 1, 2)

        @block.vector
        def _(dve):
            for j, (mu, blocks, what) in enumerate(JOBS):
                def add(k):
                    dve.wait_ge(scaled, KB * j + k + 1)
                    if KB * j + k >= 2:
                        dve.wait_ge(lo_done, KB * j + k - 1)
                    dve.scalar_tensor_tensor(mem.mt2[:, k % 2, 0:TPAD - 1], mem.xnp[:, k, 0:TPAD - 1], mem.vec[:, k, VEC["mu0"] + mu:VEC["mu0"] + mu + 1],
                                             mem.mt1[:, k % 2, 0:TPAD - 1], ALU.mult, ALU.add).then_inc(summed, 1)

                def lo(k):
                    dve.wait_ge(hi_done, 2 * (KB * j + k) + 2)
                    dve.tensor_tensor(mem.mixed[:, 1, k, 0:TP], mem.mt2[:, k % 2, 0:TP], mem.mixed[:, 0, k, 0:TP].bitcast(F32), ALU.subtract)
                    dve.tensor_tensor(mem.mixed[:, 1, k, TP:T].rearrange("p (b t) -> p b t", b=NS), streams(mem.mt2[:, k % 2, :]),
                                      mem.mixed[:, 0, k, TP:T].bitcast(F32).rearrange("p (b t) -> p b t", b=NS), ALU.subtract).then_inc(lo_done, 1)

                add(0)
                for k in range(KB):
                    if k + 1 < KB:
                        add(k + 1)
                    lo(k)


def recurrence_areas(mem):
    m, at = Memory(), 0

    def cut(cols):
        nonlocal at
        ap = mem.arena[:, at:at + cols]
        at += cols
        return ap

    m.r, m.k, m.v, m.sg, m.cum, m.a, m.before, m.inv, m.upto, m.kkn, m.k2 = (cut(T) for _ in range(11))
    m.out, m.bonus, m.post1, m.post2 = (cut(T) for _ in range(4))
    m.ar = cut(NCH * 192).rearrange("p (n c) -> p n c", n=NCH)
    m.bbd, m.kbd, m.vbd = (cut(NCH * P).rearrange("p (n c) -> p n c", n=NCH) for _ in range(3))
    m.at = cut(2 * 4 * 512).rearrange("p (g q c) -> p g q c", g=2, q=4)
    m.tm = cut(2 * 4 * 384).rearrange("p (g q c) -> p g q c", g=2, q=4)
    m.x = cut(512).rearrange("p (q c) -> p q c", q=4)
    m.y = cut(1024).rearrange("p (g q c) -> p g q c", g=2, q=4)
    m.q = cut(512).rearrange("p (q c) -> p q c", q=4)
    m.lt = cut(1024).rearrange("p (l q c) -> p l q c", l=2, q=4)
    m.s = cut(256).rearrange("p (l c) -> p l c", l=2)
    m.sp, m.w, m.u, m.z, m.sfin = (cut(P) for _ in range(5))
    m.pc, m.pcn = cut(24), cut(24)
    m.pp, m.oka, m.lnp = cut(NROW), cut(1), cut(2)
    m.lw = cut(P)
    m.lg = cut(2 * P).rearrange("p (a c) -> p a c", a=2)
    m.mask, m.mask16 = cut(512), cut(512)
    m.level = cut(6 * P).rearrange("p (l c) -> p l c", l=6)
    m.m4 = cut(4)
    m.reset = cut(T)
    m.s0 = cut(NS * P).rearrange("p (b c) -> p b c", b=NS)
    m.s0t = cut(NS * P).rearrange("p (b c) -> p b c", b=NS)
    m.um, m.vm = (cut(512).rearrange("p (b c) -> p b c", b=4) for _ in range(2))
    m.sel = cut(9 * P).rearrange("p (i c) -> p i c", i=9)
    m.headcol, m.center = cut(2), cut(P)
    m.kst, m.vst = cut(18), cut(18)
    m.kstt, m.vstt = cut(P), cut(P)
    assert at <= mem.arena.shape[1], (at, mem.arena.shape)
    return m


PIECES = {"w", "a", "kstat", "kturn", "ksel", "rk", "center", "vstat", "vturn", "vsel", "gate", "fin", "s0t", "ns", "nst"}
LEVELS = [5, 5, 5, 5, 5, 3]
NL = sum(LEVELS)
NY = NL + len(LEVELS)
NG = len(GROUPS)


def three(what, o):
    return [(what, o, c) for c in range(3)]


def prepare(o):
    return ([("params", o, None)] + three("w", o) + [("kq", o, None), ("scan", o, None)] + three("a", o)
            + [("decays", o, None), ("kstat", o, None), ("kturn", o, None)] + three("ksel", o)
            + [("k2", o, None), ("b", o, None)])


def finish(o):
    return ([("lnp", o, None)] + three("center", o) + [("vstat", o, None), ("vturn", o, None)] + three("vsel", o)
            + [("affine", o, None)] + three("gate", o) + [("posted", o, None)])


def bonus(o):
    return [("rkr", o, None)] + three("rk", o) + [("bonused", o, None)]


def merge(main, side):
    out, n = [], 0
    for i, item in enumerate(main):
        out.append(item)
        while n < len(side) and n * len(main) < (i + 1) * len(side):
            out.append(side[n])
            n += 1
    return out + side[n:]


def group(o, g, following, side):
    if g < NG - 1:
        steps = [("step", o, (g, q, part)) for q in range(GROUPS[g][1]) for part in range(3)]
    else:
        steps = [("fin", o, None), ("s0t", o, 0), ("s0t", o, 1)]
        for q in range(2):
            steps += [(x, o, q) for x in ("z", "sw", "su", "so", "ns", "nst")]
    todo = []
    if following:
        fo, fg = following
        todo = [("invert", fo, (fg, l, half)) for l in range(1, LEVELS[fg] + 1) for half in range(2)]
    main = []
    if following:
        fo, fg = following
        n = GROUPS[fg][1]
        for q in range(n):
            main += [("form", fo, (fg, q))] + steps[q:q + 1]
        main.append(("init", fo, fg))
        steps = steps[n:]
    for i in range(max(len(steps), len(todo))):
        main += steps[i:i + 1] + todo[i:i + 1]
    return merge(main, side) + [("leave", o, g)]


def number(items):
    out, n = [], 0
    for what, o, arg in items:
        piece = None
        if what in PIECES:
            piece = (n % 2, n // 2)
            n += 1
        out.append((what, o, arg, piece))
    return out, n


def write(o, *groups):
    return [("write", o, g) for g in groups]


def turn(last):
    side = [[]] * NG
    if not last:
        prep = prepare(1)
        n = len(prep) // 3
        side = [[], prep[:n], prep[n:2 * n], prep[2 * n:], write(1, 0, 1, 2, 3), write(1, 4)]
    items = []
    for g in range(1, NG):
        following = (0, g + 1) if g < NG - 1 else (None if last else (1, 0))
        items += group(0, g, following, side[g])
    if last:
        return items + finish(0)
    return items + [("begin", 1, None)] + group(1, 0, (1, 1), write(1, 5) + finish(0) + bonus(1))


START, N_START = number(prepare(0) + write(0, 0, 1, 2, 3, 4) + [("begin", 0, None)]
                        + [("form", 0, (0, q)) for q in range(GROUPS[0][1])] + [("init", 0, 0)]
                        + [("invert", 0, (0, l, half)) for l in range(1, LEVELS[0] + 1) for half in range(2)]
                        + group(0, 0, (0, 1), write(0, 5) + bonus(0)))
TURN, N_TURN = number(turn(False))
END, N_END = number(turn(True))
assert N_START % 2 == 0 and N_TURN % 2 == 0


def first_pair(pr):
    return isinstance(pr, int) and pr == 0


def recurrence_phase(nc, t, mem, o):
    m = recurrence_areas(mem)
    with ExitStack() as ctx:
        sem = phase_semaphores(nc, ctx, "scan")
        consts, cchain, zeroed = sem("consts"), sem("cchain"), sem("zeroed")
        rkv_in, lw_in, lg_in, s0_in, states_out, out_stored = (sem(x) for x in
            ("rkv_in", "lw_in", "lg_in", "s0_in", "states_out", "out_stored"))
        sp_passed, pool_passed, dve_chain, pool_chain = sem("sp_passed"), sem("pool_passed"), sem("dve_chain"), sem("pool_chain")
        piece_done, piece_free = [sem("piece_done6"), sem("piece_done7")], [sem("piece_free6"), sem("piece_free7")]
        pp_ready, kq_ready, cum_ready, lme_ready, decays_ready, k2_ready, rk_ready = (sem(x) for x in
            ("pp_ready", "kq_ready", "cum_ready", "lme_ready", "decays_ready", "k2_ready", "rk_ready"))
        kinv, kroot, vinv, vroot = sem("kinv"), sem("kroot"), sem("vinv"), sem("vroot")
        written_dve, written_pool, bonus_done, post_done = sem("written_dve"), sem("written_pool"), sem("bonus_done"), sem("post_done")
        p1_done, at_ready, t_done, tm_ready = sem("p1_done"), sem("at_ready"), sem("t_done"), sem("tm_ready")
        lt_ready, m1_done, q_ready, m2_done, m3_done, x_ready, y_ready = (sem(x) for x in
            ("lt_ready", "m1_done", "q_ready", "m2_done", "m3_done", "x_ready", "y_ready"))
        w_done, w_ready, u_done, u_ready, s_done, s_ready, sp_ready, serial_done, o_ready = (sem(x) for x in
            ("w_done", "w_ready", "u_done", "u_ready", "s_done", "s_ready", "sp_ready", "serial_done", "o_ready"))
        z_done, z_ready, um_ready, ns_ready, ns_out, fin_ready = (sem(x) for x in
            ("z_done", "z_ready", "um_ready", "ns_ready", "ns_out", "fin_ready"))
        block = ctx.enter_context(nc.Block())
        vp = lambda name: m.pp[:, VEC[name]:VEC[name] + 1]
        halves = ((0, 64), (64, 128))
        bank = mem.ps
        P1, TB, MX, MY, WUS, OB, PIECE = 0, 1, 2, 3, 4, 5, 6
        third = lambda ap, c: ap[:, c * CW:(c + 1) * CW]
        first_level = lambda g: sum(LEVELS[:g])
        first_y = lambda g: sum(LEVELS[:g]) + g
        after = lambda g: GROUPS[g][0] + GROUPS[g][1]
        reuse = lambda pr, g: NCH * pr + (GROUPS[g - 1][0] if g >= 2 else (0, -2)[g == 0]) + 3

        def sections(run, eng):
            run(START, 0, 0)
            with eng.Fori(0, PAIRS - 1) as p:
                run(TURN, p, N_START // 2 + (N_TURN // 2) * p)
            run(END, PAIRS - 1, N_START // 2 + (N_TURN // 2) * (PAIRS - 1))

        def piece_of(items, what, arg=2):
            return next(x[3] for x in items if x[0] == what and x[2] == arg)

        @block.sync
        def _(sp):
            def load(q):
                if not first_pair(q):
                    hold(sp, sp_passed, bonus_done, q)
                    hold(sp, sp_passed, written_dve, NG * q)
                    hold(sp, sp_passed, written_pool, NG * q)
                for j, dst in enumerate((m.r, m.k, m.v)):
                    sp.dma_start(dst, mem.rkv_dram[j, bass.ds(q * P, P), :]).then_inc(rkv_in, 16)
                cols = bass.ds(q * P, P)
                sp.dma_start(m.lw[0:64, :], t["rwkv_decay_w2"][0][:, cols]).then_inc(lw_in, 16)
                sp.dma_start(m.lw[64:128, :], t["rwkv_iclr_a2"][0][:, cols]).then_inc(lw_in, 16)

            def rest(p):
                cols = bass.ds(p * P, P)
                hold(sp, sp_passed, post_done, p + 1)
                sp.dma_start(m.lg[:, 0, :], t["rwkv_gate_g2"][0][0:P, cols]).then_inc(lg_in, 16)
                sp.dma_start(m.lg[96:128, 1, :], t["rwkv_gate_g2"][0][P:P + 32, cols]).then_inc(lg_in, 16)
                hold(sp, sp_passed, states_out, 96 * p + 16)
                for h, (lo, hi) in enumerate(halves):
                    sp.dma_start(m.s0[lo:hi, :, lo:hi], t["state_wkv"][0][:, bass.ds(2 * p + h, 1), :, :].rearrange("b a v c -> v (a b) c")
                                 ).then_inc(s0_in, 16)
                hold(sp, sp_passed, fin_ready, p + 1)
                for h, (lo, hi) in enumerate(halves):
                    sp.dma_start(o["wkv_p"][0, 0, bass.ds(2 * p + h, 1), :, :].rearrange("a v c -> (a v) c"), m.sfin[lo:hi, lo:hi]).then_inc(states_out, 16)
                for e in range(2):
                    hold(sp, sp_passed, ns_out, 2 * p + e + 1)
                    for h, (lo, hi) in enumerate(halves):
                        sp.dma_start(o["wkv_s"][0, 4 * e:4 * e + 4, bass.ds(2 * p + h, 1), :, :].rearrange("b a v c -> v (a b) c"),
                                     m.s0[lo:hi, 4 * e:4 * e + 4, lo:hi]).then_inc(states_out, 16)
                hold(sp, sp_passed, post_done, p + 2)
                sp.dma_start(mem.gated_dram[bass.ds(p * P, P), :], m.post2).then_inc(out_stored, 16)

            load(0)
            sp.wait_ge(zeroed, 6)
            with sp.Fori(0, PAIRS - 1) as p:
                load(p + 1)
                rest(p)
            rest(PAIRS - 1)
            sp.wait_ge(states_out, 96 * PAIRS + 16)
            sp.wait_ge(out_stored, 16 * PAIRS + 16)

        @block.gpsimd
        def _(pool):
            pool.sem_inc(states_out, 16)
            pool.sem_inc(out_stored, 16)
            c = Chain(pool, cchain)
            head_selectors(pool, c, m.sel[0:18], m.headcol)
            c.link(pool.memset(m.reset, 1.0))
            c.link(pool.memset(m.reset[:, 0:TP].rearrange("p (n c) -> p n c", c=CHUNK)[:, :, 0], 0.0))
            c.link(pool.memset(m.reset[:, TP:T].rearrange("p (n c) -> p n c", c=TS)[:, :, 0], 0.0))
            pool.sem_inc(consts, 1)

            def same_block(ap, width):
                n = ap.shape[-1] // width
                v = ap.rearrange("p (n w) -> p n w", w=width)
                c.link(pool.affine_select(out=v, in_=v, compare_op=ALU.is_ge, fill=0.0, base=0, pattern=[[-width, n], [0, width]], channel_multiplier=1))
                c.link(pool.affine_select(out=v, in_=v, compare_op=ALU.is_ge, fill=0.0, base=width - 1, pattern=[[width, n], [0, width]], channel_multiplier=-1))

            for mask, width in ((m.mask, 64), (m.mask16, TS)):
                c.link(pool.memset(mask, 1.0))
                for at in (0, 192):
                    aa, ar = mask[:, at:at + P], mask[:, at + P:at + 192]
                    same_block(aa, width)
                    c.link(pool.affine_select(out=aa, in_=aa, compare_op=ALU.is_gt, fill=0.0, base=0, pattern=[[1, P]], channel_multiplier=-1))
                    for lo, hi in halves:
                        h = ar[lo:hi]
                        if width < 64:
                            same_block(h, width)
                        c.link(pool.affine_select(out=h, in_=h, compare_op=ALU.is_ge, fill=0.0, base=0, pattern=[[1, 64]], channel_multiplier=-1))
                aa = mask[:, 384:512]
                same_block(aa, width)
                c.link(pool.affine_select(out=aa, in_=aa, compare_op=ALU.is_gt, fill=0.0, base=0, pattern=[[-1, P]], channel_multiplier=1))
            c.link(pool.memset(m.level, 1.0))
            for l in range(6):
                same_block(m.level[:, l, :], 2 ** (l + 1))
            for l in range(5, 0, -1):
                c.link(pool.tensor_tensor(m.level[:, l, :], m.level[:, l, :], m.level[:, l - 1, :], ALU.subtract))
            c.link(pool.tensor_tensor(m.level[:, 0, :], m.level[:, 0, :], mem.ident[:, :], ALU.subtract))
            c.link(pool.memset(m.m4, 1.0))
            for lo, hi in halves:
                v = m.m4[lo:hi]
                c.link(pool.affine_select(out=v, in_=v, compare_op=ALU.is_ge, fill=0.0, base=0, pattern=[[-TS, 4]], channel_multiplier=1))
                c.link(pool.affine_select(out=v, in_=v, compare_op=ALU.is_ge, fill=0.0, base=TS - 1, pattern=[[TS, 4]], channel_multiplier=-1))
            c.link(pool.tensor_scalar(m.center, mem.headones[:, :], -1.0 / HD, None, ALU.mult))
            c.link(pool.tensor_tensor(m.center, m.center, mem.ident[:, :], ALU.add))
            pool.sem_inc(consts, 1)
            pool.wait_ge(zeroed, 6)

            def run(items, p, before):
                chain = Chain(pool, pool_chain, p + (0 if items is START else 1), 2)
                levels = []
                for what, ahead, arg, piece in items:
                    pr = p + ahead
                    if what == "k2":
                        b, n = piece_of(items, "a")
                        pool.wait_ge(piece_free[b], before + n + 2)
                        hold(pool, pool_passed, kinv, pr + 1)
                        chain.link(pool.tensor_scalar(m.k2, m.a, vp("ka"), m.oka, ALU.mult, ALU.add))
                        pool.wait_ge(rkv_in, 48 * pr + 48)
                        pool.tensor_tensor(m.k2, m.k2, m.k, ALU.mult).then_inc(k2_ready, 1)
                    elif what == "b":
                        b, n = piece_of(items, "ksel")
                        pool.wait_ge(piece_free[b], before + n + 2)
                        pool.wait_ge(k2_ready, pr + 1)
                        chain.link(pool.tensor_tensor(m.a, m.kkn, m.a, ALU.mult))
                    elif what == "write":
                        g = arg
                        c0, G = GROUPS[g]
                        pool.wait_ge(decays_ready, 3 * pr + 2)
                        if not first_pair(pr):
                            pool.wait_ge(serial_done, NCH * (pr - 1) + after(g) + 3)
                        if levels:
                            pool.wait_ge(lt_ready, NL * levels[-1][0] + levels[-1][1])
                        part = lambda ap: chunks(ap)[:, c0:c0 + G, :]
                        for lo, hi in halves:
                            pool.tensor_tensor(m.bbd[lo:hi, c0:c0 + G, lo:hi], part(m.a[lo:hi]), part(m.inv[lo:hi]), ALU.mult)
                        for lo, hi in halves:
                            pool.tensor_tensor(m.kbd[lo:hi, c0:c0 + G, lo:hi], part(m.k2[lo:hi]), part(m.inv[lo:hi]), ALU.mult)
                        for lo, hi in halves:
                            ins = pool.tensor_scalar(m.vbd[lo:hi, c0:c0 + G, lo:hi], part(m.v[lo:hi]), 1.0, None, ALU.mult)
                        ins.then_inc(written_pool, 1)
                        pool.wait_ge(written_pool, NG * pr + g + 1)
                    elif what == "invert" and arg[2] == 0:
                        g, l, _ = arg
                        c0, G = GROUPS[g]
                        n = first_level(g) + l - 1
                        pool.wait_ge(at_ready, NCH * pr + after(g) + 1)
                        pool.wait_ge(m1_done, NL * pr + n + 1)
                        pool.tensor_tensor(m.lt[:, n % 2, 0:G, :], m.at[:, g % 2, 0:G, 0:P],
                                           spread(m.level[:, l, :], G), ALU.mult).then_inc(lt_ready, 1)
                        levels.append((pr, n + 1))
                if items is not END:
                    chain.close("recurrence, Pool")

            sections(run, pool)

        @block.tensor
        def _(pe):
            pe.sem_inc(serial_done, 3)
            pe.sem_inc(m1_done, 2)
            pe.wait_ge(consts, 1)

            def run(items, p, before):
                for what, ahead, arg, piece in items:
                    pr = p + ahead
                    if piece:
                        b, n = piece
                        pb = bank[:, PIECE + b, :]
                        pe.wait_ge(piece_free[b], before + n + 1)
                    if what == "w":
                        pe.wait_ge(lw_in, 32 * pr + 32)
                        pe.matmul(pb[:, 0:CW], m.lw[0:64, :], third(mem.lora_wa[0:64, :], arg), start=True, stop=True).then_inc(piece_done[b], 1)
                    elif what == "a":
                        pe.matmul(pb[:, 0:CW], m.lw[64:128, :], third(mem.lora_wa[64:128, :], arg), start=True, stop=True).then_inc(piece_done[b], 1)
                    elif what in ("kstat", "vstat"):
                        if what == "kstat":
                            pe.wait_ge(kq_ready, pr + 1)
                            src = m.k2
                        else:
                            cb, cn = piece_of(items, "center")
                            pe.wait_ge(piece_free[cb], before + cn + 2)
                            src = m.post1
                        for i in range(9):
                            last = pe.matmul(pb[:, 2 * i:2 * i + 2], src[:, i * P:(i + 1) * P], m.headcol, start=True, stop=True)
                        last.then_inc(piece_done[b], 1)
                    elif what in ("kturn", "vturn"):
                        pe.wait_ge(kroot if what == "kturn" else vroot, pr + 1)
                        pe.transpose(pb[0:18, 0:P], m.kst if what == "kturn" else m.vst, mem.ident[:, :]).then_inc(piece_done[b], 1)
                    elif what in ("ksel", "vsel"):
                        rows = m.kstt if what == "ksel" else m.vstt
                        tb, tn = piece_of(items, "kturn" if what == "ksel" else "vturn", None)
                        pe.wait_ge(piece_free[tb], before + tn + 2)
                        for j in range(3):
                            last = pe.matmul(pb[:, j * P:(j + 1) * P], m.sel[0:18, 3 * arg + j, :], rows[0:18, :], start=True, stop=True)
                        last.then_inc(piece_done[b], 1)
                    elif what == "rk":
                        pe.wait_ge(rk_ready, pr + 1)
                        pe.matmul(pb[:, 0:CW], mem.headones[:, :], third(m.cum, arg), start=True, stop=True).then_inc(piece_done[b], 1)
                    elif what == "center":
                        pe.wait_ge(o_ready, NG * pr + NG + 1)
                        pe.matmul(pb[:, 0:CW], m.center, third(m.out, arg), start=True, stop=True).then_inc(piece_done[b], 1)
                    elif what == "gate":
                        pe.wait_ge(lg_in, 32 * pr + 32)
                        pe.matmul(pb[:, 0:CW], m.lg[:, 0, :], third(mem.lora_g[:, :], arg), start=True, stop=False)
                        pe.matmul(pb[:, 0:CW], m.lg[96:128, 1, :], third(mem.lora_g2[96:128, :], arg), start=False, stop=True).then_inc(piece_done[b], 1)
                    elif what == "form":
                        g, q = arg
                        if q == 0:
                            pe.wait_ge(consts, 2)
                            pe.wait_ge(written_dve, NG * pr + g + 1)
                            pe.wait_ge(written_pool, NG * pr + g + 1)
                        n = GROUPS[g][0] + q
                        now = NCH * pr + n
                        pe.wait_ge(at_ready, now + 1)
                        f = bank[:, P1, :]
                        pe.matmul(f[:, 0:192], m.bbd[:, n, :], m.ar[:, n, :], start=True, stop=True)
                        pe.matmul(f[:, 192:384], m.kbd[:, n, :], m.ar[:, n, :], start=True, stop=True)
                        pe.matmul(f[:, 384:512], m.ar[:, n, 0:P], m.bbd[:, n, :], start=True, stop=True).then_inc(p1_done, 1)
                        pe.wait_ge(tm_ready, now + 1)
                        for j, x in enumerate((m.bbd, m.kbd, m.vbd)):
                            last = pe.transpose(bank[:, TB, j * P:(j + 1) * P], x[:, n, :], mem.ident[:, :])
                        last.then_inc(t_done, 1)
                    elif what == "invert":
                        g, l, half = arg
                        G, gb = GROUPS[g][1], g % 2
                        n = first_level(g) + l - 1
                        if half == 0:
                            pe.wait_ge(lt_ready, NL * pr + n + 1)
                            pe.wait_ge(x_ready, NL * pr + n + 1)
                            for q in range(G):
                                last = pe.matmul(bank[:, MX, q * P:(q + 1) * P], m.lt[:, n % 2, q, :], m.x[:, q, :], start=True, stop=True)
                            last.then_inc(m1_done, 1)
                        else:
                            pe.wait_ge(q_ready, NL * pr + n + 1)
                            pe.wait_ge(y_ready, NY * pr + first_y(g) + l)
                            if l < LEVELS[g]:
                                for q in range(G):
                                    last = pe.matmul(bank[:, MX, q * P:(q + 1) * P], m.y[:, gb, q, :], m.q[:, q, :], start=True, stop=True)
                                last.then_inc(m2_done, 1)
                            for q in range(G):
                                last = pe.matmul(bank[:, MY, q * P:(q + 1) * P], m.q[:, q, :], m.y[:, gb, q, :], start=True, stop=True)
                            last.then_inc(m3_done, 1)
                    elif what == "step":
                        g, q, part = arg
                        c0, G = GROUPS[g]
                        gb = g % 2
                        n, now = c0 + q, NCH * pr + c0 + q
                        at, tm = m.at[:, gb, q, :], m.tm[:, gb, q, :]
                        S = m.s[:, n % 2, :]
                        if part == 0:
                            pe.wait_ge(s_ready, 17 * pr + n + 1)
                            if q == 0:
                                pe.wait_ge(at_ready, NCH * pr + after(g) + 1)
                                pe.wait_ge(tm_ready, NCH * pr + after(g) + 1)
                            pe.matmul(bank[:, WUS, 0:P], m.ar[:, n, 0:P], S, start=True, stop=False)
                            pe.matmul(bank[:, WUS, 0:P], at[:, 192:320], tm[:, 256:384], start=False, stop=True).then_inc(w_done, 1)
                        elif part == 1:
                            pe.wait_ge(w_ready, now + 1)
                            if q == 0:
                                pe.wait_ge(y_ready, NY * pr + first_y(g) + LEVELS[g] + 1)
                            pe.matmul(bank[:, WUS, P:2 * P], m.y[:, gb, q, :], m.w, start=True, stop=True).then_inc(u_done, 1)
                        else:
                            pe.wait_ge(u_ready, now + 1)
                            pe.matmul(bank[:, WUS, 2 * P:3 * P], tm[:, 0:P], m.u, start=True, stop=False)
                            pe.matmul(bank[:, WUS, 2 * P:3 * P], tm[:, P:2 * P], tm[:, 256:384], start=False, stop=True).then_inc(s_done, 1)
                            if q == 0:
                                pe.wait_ge(o_ready, NG * pr + g + 1)
                            ob = bank[:, OB, q * 64:(q + 1) * 64]
                            pe.matmul(ob, S, m.ar[:, n, P:192], start=True, stop=False)
                            pe.matmul(ob, m.u, at[:, P:192], start=False, stop=False)
                            pe.matmul(ob, tm[:, 256:384], at[:, 320:384], start=False, stop=True).then_inc(serial_done, 1)
                    elif what == "fin":
                        pe.wait_ge(s_ready, 17 * pr + 17)
                        pe.wait_ge(s0_in, 32 * pr + 32)
                        pe.transpose(pb[:, 0:P], m.s[:, 0, :], mem.ident[:, :]).then_inc(piece_done[b], 1)
                    elif what == "s0t":
                        for j in range(4):
                            last = pe.transpose(pb[:, j * P:(j + 1) * P], m.s0[:, 4 * arg + j, :], mem.ident[:, :])
                        last.then_inc(piece_done[b], 1)
                    elif what in ("z", "sw", "su", "so", "ns", "nst"):
                        g, q = NG - 1, arg
                        c0, G = GROUPS[g]
                        gb = g % 2
                        n, now = c0 + q, NCH * pr + c0 + q
                        at, tm = m.at[:, gb, q, :], m.tm[:, gb, q, :]
                        two = lambda ap, e: ap.rearrange("p (h t) -> p h t", h=2)[:, :, TS * e:TS * e + TS]
                        if what == "z":
                            sb, sn = piece_of(items, "s0t", q)
                            pe.wait_ge(piece_free[sb], before + sn + 2)
                            if q == 0:
                                pe.wait_ge(at_ready, NCH * pr + after(g) + 1)
                                pe.wait_ge(tm_ready, NCH * pr + after(g) + 1)
                            for e in range(4):
                                last = pe.matmul(two(bank[:, WUS, 0:P], e), m.s0t[:, 4 * q + e, :], two(m.ar[:, n, 0:P], e), start=True, stop=True)
                            last.then_inc(z_done, 1)
                        elif what == "sw":
                            pe.wait_ge(z_ready, 2 * pr + q + 1)
                            pe.matmul(bank[:, WUS, P:2 * P], m.z, mem.ident[:, :], start=True, stop=False)
                            pe.matmul(bank[:, WUS, P:2 * P], at[:, 192:320], tm[:, 256:384], start=False, stop=True).then_inc(w_done, 1)
                        elif what == "su":
                            pe.wait_ge(w_ready, now + 1)
                            if q == 0:
                                pe.wait_ge(y_ready, NY * pr + first_y(g) + LEVELS[g] + 1)
                            pe.matmul(bank[:, WUS, 2 * P:3 * P], m.y[:, gb, q, :], m.w, start=True, stop=True).then_inc(u_done, 1)
                        elif what == "so":
                            pe.wait_ge(u_ready, now + 1)
                            if q == 0:
                                pe.wait_ge(o_ready, NG * pr + g + 1)
                            ob = bank[:, OB, q * 64:(q + 1) * 64]
                            pe.matmul(ob, m.u, at[:, P:192], start=True, stop=False)
                            pe.matmul(ob, tm[:, 256:384], at[:, 320:384], start=False, stop=False)
                            for e in range(4):
                                last = pe.matmul(ob[:, TS * e:TS * e + TS], m.s0t[:, 4 * q + e, :], m.ar[:, n, P + TS * e:P + TS * e + TS],
                                                 start=False, stop=(e == 3))
                            last.then_inc(serial_done, 1)
                        elif what == "ns":
                            pe.wait_ge(um_ready, 2 * pr + q + 1)
                            pe.matmul(pb, tm[:, 0:P], m.um, start=True, stop=False)
                            pe.matmul(pb, tm[:, P:2 * P], m.vm, start=False, stop=True).then_inc(piece_done[b], 1)
                        else:
                            pe.wait_ge(ns_ready, 2 * pr + q + 1)
                            for j in range(4):
                                last = pe.transpose(pb[:, j * P:(j + 1) * P], m.s0t[:, 4 * q + j, :], mem.ident[:, :])
                            last.then_inc(piece_done[b], 1)

            sections(run, pe)

        @block.scalar
        def _(act):
            act.sem_inc(tm_ready, 1)
            act.sem_inc(o_ready, 1)
            act.sem_inc(piece_free[0], 1)
            act.sem_inc(piece_free[1], 1)

            def run(items, p, before):
                for what, ahead, arg, piece in items:
                    pr = p + ahead
                    if piece and what in ("w", "a", "center", "fin", "s0t", "nst"):
                        b, n = piece
                        pb = bank[:, PIECE + b, :]
                        act.wait_ge(piece_done[b], before + n + 1)
                    if what == "w":
                        act.wait_ge(pp_ready, pr + 1)
                        act.activation(third(m.sg, arg), pb[:, 0:CW], ACT.Sigmoid, bias=vp("w0")).then_inc(piece_free[b], 1)
                    elif what == "a":
                        if arg == 0 and not first_pair(pr):
                            act.wait_ge(written_pool, NG * pr)
                        act.activation(third(m.a, arg), pb[:, 0:CW], ACT.Sigmoid, bias=vp("a0")).then_inc(piece_free[b], 1)
                    elif what == "kq":
                        act.wait_ge(rkv_in, 48 * pr + 48)
                        if not first_pair(pr):
                            act.wait_ge(written_pool, NG * pr)
                            act.wait_ge(rk_ready, pr)
                        act.activation(m.k2, m.k, ACT.Square, scale=vp("kk")).then_inc(kq_ready, 1)
                    elif what == "decays":
                        if not first_pair(pr):
                            act.wait_ge(written_dve, NG * pr)
                        act.wait_ge(cum_ready, pr + 1)
                        act.activation(m.upto, m.cum, ACT.Exp, scale=-DECAY).then_inc(decays_ready, 1)
                        act.activation(m.inv, m.cum, ACT.Exp, scale=DECAY).then_inc(decays_ready, 1)
                        act.wait_ge(lme_ready, pr + 1)
                        act.activation(m.before, m.sg, ACT.Exp, scale=-DECAY).then_inc(decays_ready, 1)
                    elif what == "kstat":
                        act.wait_ge(kinv, pr + 1)
                        act.activation(m.kst, m.kst, ACT.Sqrt).then_inc(kroot, 1)
                    elif what == "vstat":
                        act.wait_ge(vinv, pr + 1)
                        act.activation(m.vst, m.vst, ACT.Sqrt).then_inc(vroot, 1)
                    elif what == "center":
                        if arg == 0:
                            act.wait_ge(out_stored, 16 * pr + 16)
                        act.activation(third(m.post1, arg), pb[:, 0:CW], ACT.Square)
                        act.copy(third(m.post2, arg), pb[:, 0:CW]).then_inc(piece_free[b], 1)
                    elif what == "form":
                        g, q = arg
                        if q == 0:
                            act.wait_ge(serial_done, reuse(pr, g))
                        act.wait_ge(t_done, NCH * pr + GROUPS[g][0] + q + 1)
                        act.copy(m.tm[:, g % 2, q, :], bank[:, TB, 0:384]).then_inc(tm_ready, 1)
                    elif what == "invert" and arg[2] == 0:
                        g, l, _ = arg
                        G = GROUPS[g][1]
                        act.wait_ge(m1_done, NL * pr + first_level(g) + l - 1 + 3)
                        act.copy(m.q[:, 0:G, :], bank[:, MX, 0:G * P].rearrange("p (q c) -> p q c", q=G)).then_inc(q_ready, 1)
                    elif what == "step" and arg[2] == 0:
                        n = GROUPS[arg[0]][0] + arg[1]
                        act.wait_ge(s_ready, 17 * pr + n + 1)
                        act.activation(m.sp, m.s[:, n % 2, :], ACT.Copy, scale=m.pc[:, n:n + 1]).then_inc(sp_ready, 1)
                    elif what == "fin":
                        act.copy(m.sfin, pb[:, 0:P]).then_inc(piece_free[b], 1)
                        act.wait_ge(piece_free[b], before + n + 2)
                        act.sem_inc(fin_ready, 1)
                    elif what == "s0t":
                        act.copy(m.s0t[:, 4 * arg:4 * arg + 4, :], pb.rearrange("p (b c) -> p b c", b=4)).then_inc(piece_free[b], 1)
                    elif what == "nst":
                        act.copy(m.s0[:, 4 * arg:4 * arg + 4, :], pb.rearrange("p (b c) -> p b c", b=4)).then_inc(piece_free[b], 1)
                        act.wait_ge(piece_free[b], before + n + 2)
                        act.sem_inc(ns_out, 1)
                    elif what == "leave":
                        c0, G = GROUPS[arg]
                        act.wait_ge(serial_done, NCH * pr + c0 + G + 3)
                        act.copy(m.out[:, c0 * CHUNK:(c0 + G) * CHUNK], bank[:, OB, 0:G * CHUNK]).then_inc(o_ready, 1)

            sections(run, act)

        @block.vector
        def _(dve):
            dve.sem_inc(at_ready, 1)
            dve.sem_inc(post_done, 1)
            for ap in (m.ar, m.bbd, m.kbd, m.vbd, m.s0, m.z):
                dve.memset(ap, 0.0).then_inc(zeroed, 1)
            dve.wait_ge(zeroed, 6)
            dve.wait_ge(consts, 1)

            def run(items, p, before):
                chain = Chain(dve, dve_chain, p, LINKS_TURN, 0 if items is START else LINKS_START)
                for what, ahead, arg, piece in items:
                    pr = p + ahead
                    if piece and what in ("kstat", "kturn", "ksel", "rk", "vstat", "vturn", "vsel", "gate", "ns"):
                        b, n = piece
                        pb = bank[:, PIECE + b, :]
                        dve.wait_ge(piece_done[b], before + n + 1)
                    if what == "params":
                        if not first_pair(pr):
                            dve.wait_ge(k2_ready, pr)
                        chain.link(dve.tensor_copy(m.pp, mem.vec[:, bass.ds(pr, 1), :].rearrange("p a n -> p (a n)")))
                        dve.tensor_scalar(m.oka, vp("ka"), -1.0, 1.0, ALU.mult, ALU.add).then_inc(pp_ready, 1)
                    elif what == "scan":
                        wb, wn = piece_of(items, "w")
                        dve.wait_ge(piece_free[wb], before + wn + 2)
                        dve.tensor_tensor_scan(m.cum, m.reset, m.sg, 0.0, ALU.mult, ALU.add).then_inc(cum_ready, 1)
                        dve.wait_ge(cum_ready, pr + 1)
                        dve.tensor_tensor(m.sg, m.cum, m.sg, ALU.subtract).then_inc(lme_ready, 1)
                    elif what == "kstat":
                        dve.tensor_scalar(m.kst, pb[:, 0:18], 1e-24, None, ALU.max).then_inc(piece_free[b], 1)
                        dve.wait_ge(piece_free[b], before + n + 2)
                        dve.reciprocal(m.kst, m.kst).then_inc(kinv, 1)
                    elif what == "vstat":
                        dve.tensor_scalar(m.vst, pb[:, 0:18], 1.0 / HD, LNX_EPS, ALU.mult, ALU.add).then_inc(piece_free[b], 1)
                        dve.wait_ge(piece_free[b], before + n + 2)
                        dve.reciprocal(m.vst, m.vst).then_inc(vinv, 1)
                    elif what in ("kturn", "vturn"):
                        dve.tensor_copy((m.kstt if what == "kturn" else m.vstt)[0:18, :], pb[0:18, 0:P]).then_inc(piece_free[b], 1)
                    elif what == "ksel":
                        dve.scalar_tensor_tensor(third(m.kkn, arg), third(m.k, arg), vp("kk"), pb[:, 0:CW], ALU.mult, ALU.mult).then_inc(piece_free[b], 1)
                        if arg == 2:
                            dve.wait_ge(decays_ready, 3 * pr + 1)
                            chain.link(dve.tensor_copy(m.pcn[:, 0:16], m.upto[:, 0:TP].rearrange("p (n c) -> p n c", c=CHUNK)[:, :, CHUNK - 1]))
                            chain.link(dve.tensor_copy(m.pcn[:, 16:24], m.upto[:, TP:T].rearrange("p (n c) -> p n c", c=TS)[:, :, TS - 1]))
                            dve.wait_ge(piece_free[b], before + n + 2)
                    elif what == "write":
                        g = arg
                        c0, G = GROUPS[g]
                        dve.wait_ge(decays_ready, 3 * pr + 3)
                        if not first_pair(pr):
                            dve.wait_ge(serial_done, NCH * (pr - 1) + after(g) + 3)
                        part = lambda ap: chunks(ap)[:, c0:c0 + G, :]
                        for lo, hi in halves:
                            dve.scalar_tensor_tensor(m.ar[lo:hi, c0:c0 + G, lo:hi], part(m.kkn[lo:hi]), -1.0, part(m.before[lo:hi]), ALU.mult, ALU.mult)
                        dve.tensor_tensor(m.ar[:, c0:c0 + G, P:192], part(m.r), part(m.upto), ALU.mult).then_inc(written_dve, 1)
                    elif what == "begin":
                        if not first_pair(pr):
                            dve.wait_ge(fin_ready, pr)
                            dve.wait_ge(ns_ready, 2 * pr)
                        chain.link(dve.tensor_copy(m.pc, m.pcn))
                        dve.memset(m.s[:, 0, :], 0.0).then_inc(s_ready, 1)
                    elif what == "rkr":
                        dve.wait_ge(k2_ready, pr + 1)
                        dve.wait_ge(decays_ready, 3 * pr + 2)
                        dve.scalar_tensor_tensor(m.cum, m.r, vp("rk"), m.k2, ALU.mult, ALU.mult).then_inc(rk_ready, 1)
                    elif what == "rk":
                        dve.tensor_tensor(third(m.bonus, arg), pb[:, 0:CW], third(m.v, arg), ALU.mult).then_inc(piece_free[b], 1)
                    elif what == "bonused":
                        rb, rn = piece_of(items, "rk")
                        dve.wait_ge(piece_free[rb], before + rn + 2)
                        dve.sem_inc(bonus_done, 1)
                    elif what == "lnp":
                        chain.link(dve.tensor_copy(m.lnp, mem.vec[:, bass.ds(pr, 1), VEC["lnw"]:VEC["lnw"] + 2].rearrange("p a n -> p (a n)")))
                    elif what == "vsel":
                        dve.tensor_tensor(third(m.post2, arg), pb[:, 0:CW], third(m.post2, arg), ALU.mult).then_inc(piece_free[b], 1)
                    elif what == "affine":
                        vb, vn = piece_of(items, "vsel")
                        dve.wait_ge(piece_free[vb], before + vn + 2)
                        chain.link(dve.scalar_tensor_tensor(m.post2, m.post2, m.lnp[:, 0:1], m.bonus, ALU.mult, ALU.add))
                    elif what == "gate":
                        dve.scalar_tensor_tensor(third(m.post2, arg), third(m.post2, arg), m.lnp[:, 1:2], pb[:, 0:CW], ALU.add, ALU.mult).then_inc(piece_free[b], 1)
                    elif what == "posted":
                        gb, gn = piece_of(items, "gate")
                        dve.wait_ge(piece_free[gb], before + gn + 2)
                        dve.sem_inc(post_done, 1)
                    elif what == "form":
                        g, q = arg
                        if q == 0:
                            dve.wait_ge(consts, 2)
                            dve.wait_ge(serial_done, reuse(pr, g))
                        dve.wait_ge(p1_done, NCH * pr + GROUPS[g][0] + q + 1)
                        dve.tensor_tensor(m.at[:, g % 2, q, :], bank[:, P1, :], m.mask if g < NG - 1 else m.mask16, ALU.mult).then_inc(at_ready, 1)
                    elif what == "init":
                        g = arg
                        G, gb = GROUPS[g][1], g % 2
                        dve.wait_ge(at_ready, NCH * pr + after(g) + 1)
                        one, eye = spread(m.level[:, 0, :], G), spread(mem.ident[:, :], G)
                        chain.mark(dve.tensor_tensor(m.x[:, 0:G, :], m.at[:, gb, 0:G, 384:512], one, ALU.mult))
                        chain.link(dve.tensor_tensor(m.y[:, gb, 0:G, :], m.at[:, gb, 0:G, 0:P], one, ALU.mult))
                        dve.tensor_tensor(m.x[:, 0:G, :], m.x[:, 0:G, :], eye, ALU.add).then_inc(x_ready, 1)
                        dve.tensor_tensor(m.y[:, gb, 0:G, :], m.y[:, gb, 0:G, :], eye, ALU.add).then_inc(y_ready, 1)
                    elif what == "invert" and arg[2] == 1:
                        g, l, _ = arg
                        G, gb = GROUPS[g][1], g % 2
                        wide = lambda b: bank[:, b, 0:G * P].rearrange("p (q c) -> p q c", q=G)
                        n = first_level(g) + l - 1
                        if l < LEVELS[g]:
                            dve.wait_ge(m2_done, (NL - NG) * pr + n - g + 1)
                            dve.wait_ge(x_ready, NL * pr + n + 1)
                            dve.tensor_tensor(m.x[:, 0:G, :], wide(MX), m.x[:, 0:G, :], ALU.add).then_inc(x_ready, 1)
                        dve.wait_ge(m3_done, NL * pr + n + 1)
                        dve.wait_ge(y_ready, NY * pr + first_y(g) + l)
                        dve.tensor_tensor(m.y[:, gb, 0:G, :], wide(MY), m.y[:, gb, 0:G, :], ALU.add).then_inc(y_ready, 1)
                    elif what == "step":
                        g, q, part = arg
                        n = GROUPS[g][0] + q
                        now = NCH * pr + n
                        if part == 0:
                            dve.wait_ge(w_done, now + 1)
                            dve.tensor_copy(m.w, bank[:, WUS, 0:P]).then_inc(w_ready, 1)
                        elif part == 1:
                            dve.wait_ge(u_done, now + 1)
                            dve.tensor_copy(m.u, bank[:, WUS, P:2 * P]).then_inc(u_ready, 1)
                        else:
                            dve.wait_ge(s_done, 16 * pr + n + 1)
                            dve.wait_ge(sp_ready, 16 * pr + n + 1)
                            dve.scalar_tensor_tensor(m.s[:, (n + 1) % 2, :], bank[:, WUS, 2 * P:3 * P], m.pc[:, n:n + 1], m.sp, ALU.mult, ALU.add).then_inc(s_ready, 1)
                    elif what == "z":
                        dve.wait_ge(z_done, 2 * pr + arg + 1)
                        dve.tensor_copy(m.z, bank[:, WUS, 0:P]).then_inc(z_ready, 1)
                    elif what == "sw":
                        now = NCH * pr + GROUPS[NG - 1][0] + arg
                        dve.wait_ge(w_done, now + 1)
                        dve.tensor_copy(m.w, bank[:, WUS, P:2 * P]).then_inc(w_ready, 1)
                    elif what == "su":
                        q = arg
                        now = NCH * pr + GROUPS[NG - 1][0] + q
                        dve.wait_ge(u_done, now + 1)
                        dve.tensor_copy(m.u, bank[:, WUS, 2 * P:3 * P]).then_inc(u_ready, 1)
                        dve.wait_ge(u_ready, now + 1)
                        dve.wait_ge(tm_ready, now + 2)
                        rows = m.m4.unsqueeze(2).to_broadcast((P, 4, P))
                        dve.tensor_tensor(m.um, spread(m.u, 4), rows, ALU.mult)
                        dve.tensor_tensor(m.vm, spread(m.tm[:, (NG - 1) % 2, q, 256:384], 4), rows, ALU.mult).then_inc(um_ready, 1)
                    elif what == "ns":
                        q = arg
                        now = NCH * pr + GROUPS[NG - 1][0] + q
                        dve.wait_ge(serial_done, now + 4)
                        st = m.s0t[:, 4 * q:4 * q + 4, :]
                        dve.tensor_tensor(st, pb.rearrange("p (b c) -> p b c", b=4), st, ALU.add).then_inc(piece_free[b], 1)
                        dve.wait_ge(piece_free[b], before + n + 2)
                        dve.tensor_tensor(st, st, m.pc[:, 16 + 4 * q:20 + 4 * q].unsqueeze(2).to_broadcast((P, 4, P)), ALU.mult).then_inc(ns_ready, 1)
                if items is not END:
                    assert chain.n == (LINKS_START if items is START else LINKS_TURN), chain.n

            sections(run, dve)


def head_selectors(pool, c, sel, headcol):
    c.link(pool.memset(sel, 1.0))
    v = sel.rearrange("p i (h f) -> p i h f", h=2)
    c.link(pool.affine_select(out=v, in_=v, compare_op=ALU.is_equal, fill=0.0, base=0, pattern=[[-2, 9], [-1, 2], [0, HD]], channel_multiplier=1))
    c.link(pool.memset(headcol, 0.0))
    for h in range(2):
        c.link(pool.memset(headcol[h * HD:(h + 1) * HD, h:h + 1], 1.0))


def project_phase(nc, t, mem):
    with ExitStack() as ctx:
        sem = phase_semaphores(nc, ctx, "project")
        s = Memory()
        weight_sems(sem, s)
        row_in, h_in, hi_done, lo_done, proj_done, proj_free = ([sem("row_in0"), sem("row_in1")], sem("h_in"), sem("hi_done"),
            sem("lo_done"), sem("proj_done"), sem("proj_free"))
        block = ctx.enter_context(nc.Block())
        w = t["rwkv_w_out"][0].rearrange("(k p) m -> p k m", p=P)

        @block.sync
        def _(sp):
            def load(n, u):
                hold(sp, s.sp_passed, s.w_split, n + 1)
                sp.dma_start(mem.stage[:, u, :].rearrange("p (k m) -> p k m", k=KB), w[:, :, bass.ds(n * P, P)]).then_inc(s.w_load[u], 16)

            load(0, 0)
            for k in range(KB):
                if k >= 2:
                    sp.wait_ge(lo_done, k - 1)
                sp.dma_start(mem.tt[:, k % 2, :], mem.gated_dram[k * P:(k + 1) * P, :]).then_inc(row_in[k % 2], 16)
                if k == 1:
                    load(1, 1)
            sp.dma_start(mem.H[:, :, :], mem.h_dram.rearrange("p (k n) -> p k n", k=KB)).then_inc(h_in, 16)
            with sp.Fori(1, KB // 2) as i:
                for u in range(2):
                    load(2 * i + u, u)

        @block.gpsimd
        def _(pool):
            split_tiles(pool, mem, s, KB)

        @block.tensor
        def _(pe):
            pe.sem_inc(s.tile_done, 2)

            def tile(m, u, first):
                pe.wait_ge(s.w_split, m + 3)
                pe.wait_ge(proj_free, m + 1)
                for k in range(KB):
                    if first:
                        pe.wait_ge(lo_done, k + 1)
                    for a, (part, xpart) in enumerate(PASSES):
                        for c in range(3):
                            last = pe.matmul(mem.ps[:, 3 * u + c, 0:CW], mem.wsplit[:, u, part, k * P:(k + 1) * P],
                                             mem.xs[:, xpart, k, c * CW:(c + 1) * CW], start=(k == 0 and a == 0), stop=(k == KB - 1 and a == 2))
                last.then_inc(s.tile_done, 1)

            tile(0, 0, True)
            tile(1, 1, False)
            with pe.Fori(1, KB // 2) as i:
                for u in range(2):
                    tile(2 * i + u, u, False)

        @block.scalar
        def _(act):
            for k in range(KB):
                act.wait_ge(row_in[k % 2], 16 * (k // 2) + 16)
                act.copy(mem.xs[:, 0, k, :], mem.tt[:, k % 2, :]).then_inc(hi_done, 1)

        @block.vector
        def _(dve):
            dve.sem_inc(proj_free, 2)
            for k in range(KB):
                dve.wait_ge(hi_done, k + 1)
                dve.tensor_tensor(mem.xs[:, 1, k, :], mem.tt[:, k % 2, :], mem.xs[:, 0, k, :].bitcast(F32), ALU.subtract).then_inc(lo_done, 1)
            dve.wait_ge(h_in, 16)
            for m in range(KB):
                dve.wait_ge(s.tile_done, m + 3)
                h = by3(mem.H[:, m, :])
                dve.tensor_tensor(h, mem.ps[:, 3 * (m % 2):3 * (m % 2) + 3, 0:CW], h, ALU.add).then_inc(proj_free, 1)


def ffn_phase(nc, t, mem, layer):
    TURNS = HB // 2
    with ExitStack() as ctx:
        sem = phase_semaphores(nc, ctx, f"ffn_{layer}")
        w_load = [sem(f"w_load{u}") for u in range(3)]
        w_split = sem("w_split")
        passed, pool_chain, sp_passed = sem("pool_passed"), sem("pool_chain"), sem("sp_passed")
        done, free = [sem("doneA"), sem("doneB")], [sem("freeA"), sem("freeB")]
        silu_ready, hf_ready, hh_ready, hid_ready = (sem(x) for x in ("silu_ready", "hf_ready", "hh_ready", "hid_ready"))
        norm = Norm(mem, sem, f"ffn{layer}", mem.tt, mem.total[:, :])
        block = ctx.enter_context(nc.Block())
        gu = t["ffn_w_gu"][layer].rearrange("(k p) m -> p k m", p=P)
        down = t["ffn_w_down"][layer]
        A, B = 0, 1
        BANKS = (mem.ps[:, 0:3, :], mem.ps[:, 3:6, :])
        TURN = lambda g: [("gate", g, 0, (B, 6 * g - 5)), ("down", g - 1, 0, (A, 6 * g - 4)), ("down", g - 1, 1, (B, 6 * g - 4)),
                          ("up", g, 0, (A, 6 * g - 3)), ("gate", g, 1, (A, 6 * g + 1)), ("up", g, 1, (A, 6 * g + 1))]
        FIRST = [("gate", 0, 0, None), ("up", 0, 0, None), ("gate", 0, 1, None), ("up", 0, 1, (A, 1))]
        LAST = [("down", TURNS - 1, 0, (B, 6 * TURNS - 5)), ("down", TURNS - 1, 1, (A, 6 * TURNS - 4))]

        @block.sync
        def _(sp):
            def load(n, slot, what, g, b):
                hold(sp, sp_passed, w_split, n + 1)
                if what == "down":
                    src, dst = down[bass.ds((2 * g + b) * P, P), :], mem.stage3[:, slot, :]
                else:
                    src = gu[:, :, bass.ds((2 * g + b) * P + (DFF if what == "up" else 0), P)]
                    dst = mem.stage3[:, slot, :].rearrange("p (k m) -> p k m", k=KB)
                sp.dma_start(dst, src).then_inc(w_load[slot], 16)

            for n, (what, g, b, _) in enumerate(FIRST):
                load(n, n % 3, what, g, b)
            with sp.Fori(1, TURNS) as g:
                for j, (what, gg, b, _) in enumerate(TURN(g)):
                    load(6 * g - 2 + j, (j + 1) % 3, what, gg, b)
            for j, (what, g, b, _) in enumerate(LAST):
                load(6 * TURNS - 2 + j, (j + 1) % 3, what, g, b)

        @block.gpsimd
        def _(pool):
            norm.pool(pool)
            pool.sem_inc(w_split, 3)

            def split(slot, loads, used, chain):
                pool.wait_ge(w_load[slot], 16 * loads)
                if used is not None:
                    hold(pool, passed, done[used[0]], used[1])
                else:
                    pool.sem_inc(passed, 1)
                w = mem.wsplit3[:, slot]
                chain.link(pool.tensor_scalar(w[:, 0, :], mem.stage3[:, slot, :], 1.0, None, ALU.mult))
                pool.tensor_tensor(w[:, 1, :], mem.stage3[:, slot, :], w[:, 0, :].bitcast(F32), ALU.subtract).then_inc(w_split, 1)

            chain = Chain(pool, pool_chain)
            for n, (_, _, _, used) in enumerate(FIRST):
                split(n % 3, n // 3 + 1, used, chain)
            with pool.Fori(1, TURNS) as g:
                chain = Chain(pool, pool_chain, 6 * g - 2, 1)
                for j, (_, _, _, used) in enumerate(TURN(g)):
                    split((j + 1) % 3, 2 * g + (j - 2) // 3 + 1, used, chain)
            chain = Chain(pool, pool_chain, 6 * TURNS - 2, 1)
            for j, (_, _, _, used) in enumerate(LAST):
                split((j + 1) % 3, 2 * TURNS + (j - 2) // 3 + 1, used, chain)

        def down_banks(g, after_gate):
            for k in range(KB):
                bank = B if k % 2 == 0 else A
                yield k, bank, 6 * g - 4 + k // 2 + 1 + (1 if bank == A and after_gate else 0)

        @block.tensor
        def _(pe):
            norm.tensor(pe)

            def hidden(n, slot, bank, count, first=False):
                pe.wait_ge(w_split, n + 4)
                pe.wait_ge(free[bank], count)
                ps3, w = BANKS[bank], mem.wsplit3[:, slot]
                for k in range(KB):
                    if first:
                        pe.wait_ge(norm.lo_done, k + 1)
                    for a, (part, xpart) in enumerate(PASSES):
                        for c in range(3):
                            last = pe.matmul(ps3[:, c, 0:CW], w[:, part, k * P:(k + 1) * P], mem.xs[:, xpart, k, c * CW:(c + 1) * CW],
                                             start=(k == 0 and a == 0), stop=(k == KB - 1 and a == 2))
                last.then_inc(done[bank], 1)

            def down_tiles(n, slots, g, after_gate):
                pe.wait_ge(w_split, n + 5)
                for k, bank, count in down_banks(g, after_gate):
                    pe.wait_ge(free[bank], count)
                    for b in range(2):
                        if k == 0:
                            pe.wait_ge(hid_ready, 2 * g + b)
                        for a, (part, xpart) in enumerate(PASSES):
                            for c in range(3):
                                last = pe.matmul(BANKS[bank][:, c, 0:CW], mem.wsplit3[:, slots[b], part, k * P:(k + 1) * P],
                                                 mem.hid[:, b, xpart, c * CW:(c + 1) * CW], start=(b == 0 and a == 0), stop=(b == 1 and a == 2))
                    last.then_inc(done[bank], 1)

            hidden(0, 0, A, 1, True)
            hidden(1, 1, B, 1)
            hidden(2, 2, A, 2)
            hidden(3, 0, B, 2)
            with pe.Fori(1, TURNS) as g:
                n = 6 * g - 2
                hidden(n, 1, A, 6 * g - 3)
                down_tiles(n + 1, (2, 0), g, True)
                hidden(n + 3, 1, B, 6 * g + 1)
                hidden(n + 4, 2, A, 6 * g + 2)
                hidden(n + 5, 0, B, 6 * g + 2)
            down_tiles(6 * TURNS - 2, (1, 2), TURNS, False)

        @block.scalar
        def _(act):
            act.sem_inc(free[A], 1)
            norm.scalar(act)
            norm.scalar_split(act)

            def one(g, b, first):
                m = 2 * g + b
                act.wait_ge(done[A], 6 * g - 3 if b == 0 and not first else 6 * g + b + 1)
                act.wait_ge(hf_ready, m + 1)
                if first and b == 0:
                    act.wait_ge(norm.lo_done, KB)
                act.activation(by3(mem.sg), mem.ps[:, 0:3, 0:CW], ACT.Silu).then_inc(silu_ready, 1)
                act.wait_ge(silu_ready, m + 1)
                act.sem_inc(free[A], 1)
                act.wait_ge(hf_ready, m + 2)
                if not first:
                    act.wait_ge(done[A], 6 * g + 1)
                act.copy(mem.hid[:, b, 0, :], mem.hf).then_inc(hh_ready, 1)

            one(0, 0, True)
            one(0, 1, True)
            with act.Fori(1, TURNS) as g:
                one(g, 0, False)
                one(g, 1, False)

        @block.vector
        def _(dve):
            dve.sem_inc(free[B], 1)
            dve.sem_inc(hf_ready, 1)
            dve.sem_inc(hid_ready, 1)
            norm.vector(dve)
            norm.vector_split(dve)

            def one(g, b):
                m = 2 * g + b
                dve.wait_ge(silu_ready, m + 1)
                dve.wait_ge(done[B], 6 * g + b + 1)
                dve.wait_ge(hid_ready, m + 1)
                dve.tensor_tensor(by3(mem.hf), mem.ps[:, 3:6, 0:CW], by3(mem.sg), ALU.mult).then_inc(hf_ready, 1)
                dve.wait_ge(hf_ready, m + 2)
                dve.sem_inc(free[B], 1)
                dve.wait_ge(hh_ready, m + 1)
                dve.tensor_tensor(mem.hid[:, b, 1, :], mem.hf, mem.hid[:, b, 0, :].bitcast(F32), ALU.subtract).then_inc(hid_ready, 1)

            def add(g, after_gate):
                for k, bank, count in down_banks(g, after_gate):
                    dve.wait_ge(done[bank], count)
                    dve.tensor_tensor(by3(mem.H[:, k, :]), BANKS[bank][:, :, 0:CW], by3(mem.H[:, k, :]), ALU.add).then_inc(free[bank], 1)

            one(0, 0)
            one(0, 1)
            with dve.Fori(1, TURNS) as g:
                add(g, True)
                one(g, 0)
                one(g, 1)
            add(TURNS, False)


def attention_phase(nc, t, mem, o):
    ITEMS = [("band", i, h) for i in range(TP // P) for h in range(2)]
    AT = (7, 13)
    for e in range(2):
        ITEMS.insert(AT[e], ("streams", e, None))
    NI = len(ITEMS)
    CACHED = {AT[e] - 4 + b: 4 * e + b for e in range(2) for b in range(4)}
    with ExitStack() as ctx:
        sem = phase_semaphores(nc, ctx, "attention")
        s = Memory()
        weight_sems(sem, s)
        pair_done, consts, cchain = sem("pair_done"), sem("consts"), sem("cchain")
        dve_chain, qs_ready = sem("dve_chain"), sem("qs_ready")
        bias_in, bs_in, ck_in, cv_in, kv_out = sem("bias_in"), sem("bs_in"), [sem("ck_in0"), sem("ck_in1")], sem("cv_in"), sem("kv_out")
        qkv_done, q_ready, k_ready, v_ready = sem("qkv_done"), sem("q_ready"), sem("k_ready"), sem("v_ready")
        vt_done, vtm_ready, kt_done, kout_ready = sem("vt_done"), sem("vtm_ready"), sem("kt_done"), sem("kout_ready")
        sc_done, sm_ready, ex_ready, nm_ready, pt_done, pt_ready, pv_done, on_ready, ot_done, ot_ready = (sem(x) for x in
            ("sc_done", "sm_ready", "ex_ready", "nm_ready", "pt_done", "pt_ready", "pv_done", "on_ready", "ot_done", "ot_ready"))
        kc_done, kc_ready, spr_ready = sem("kc_done"), sem("kc_ready"), sem("spr_ready")
        norm = Norm(mem, sem, "mix1", mem.qz, mem.kT[:, :])
        oh_ready, ol_ready, proj_done, proj_free = sem("oh_ready"), sem("ol_ready"), sem("proj_done"), sem("proj_free")
        block = ctx.enter_context(nc.Block())
        ps = mem.ps
        flat = mem.ps[:, :, :].rearrange("p b c -> p (b c)")
        halves = ((0, 64), (64, 128))
        wqkv = t["attn_w_qkv"][0].rearrange("(k p) m -> p k m", p=P)
        def keys_of(n):
            what, i, _ = ITEMS[n]
            return (max(0, i - 4), min(i, 4) + 1, (min(i, 4) + 1) * P) if what == "band" else (None, 5, SPAN)

        ck = lambda b, p: t["cache_k"][0][b].rearrange("(a k) h d -> k a (h d)", k=P)[:, :, bass.ds(p * P, P)]
        cv = lambda b, p: t["cache_v"][0][b].rearrange("(a k) h d -> k a (h d)", k=P)[:, :, bass.ds(p * P, P)]

        @block.sync
        def _(sp):
            with sp.Fori(0, PAIRS) as p:
                cols = bass.ds(p * P, P)
                for u in range(3):
                    hold(sp, s.sp_passed, s.w_split, 4 * p + u + 1)
                    sp.dma_start(mem.stage[:, u % 2, :].rearrange("p (k m) -> p k m", k=KB), wqkv[:, :, bass.ds(p * P + u * D, P)]
                                 ).then_inc(s.w_load[u % 2], 16)
                hold(sp, s.sp_passed, pair_done, p + 1)
                for h in range(2):
                    sp.dma_start(mem.bt[:, h, :], mem.tab_dram[bass.ds(2 * p + h, 1), :, :].rearrange("a q k -> (a q) k")).then_inc(bias_in, 16)
                hold(sp, s.sp_passed, bias_in, 32 * p + 32)
                for b in range(4):
                    for h in range(2):
                        lo = 32 * b + 16 * h
                        sp.dma_start(mem.bs[lo:lo + 16, :], mem.bt[0:16, h, 0:SPAN]).then_inc(bs_in, 16)
                hold(sp, s.sp_passed, s.w_split, 4 * p + 4)
                sp.dma_start(mem.stage[:, 1, :], t["attn_w_out"][0][cols, :]).then_inc(s.w_load[1], 16)
                for b in range(2):
                    hold(sp, s.sp_passed, kc_ready, NS * p + b + 1)
                    sp.dma_start(mem.ck[:, b % 2, :, :], ck(b, p)).then_inc(ck_in[b % 2], 16)
                for b in range(4):
                    sp.dma_start(mem.cv[:, b, :, :], cv(b, p)).then_inc(cv_in, 16)
                hold(sp, s.sp_passed, kout_ready, p + 1)
                hold(sp, s.sp_passed, vtm_ready, p + 1)
                for src, dp, ds_ in ((mem.kout[:, :, :], "k_p", "k_s"), (mem.vtm[:, 4:9, :], "v_p", "v_s")):
                    sp.dma_start(o[dp][0, 0].rearrange("(a k) h d -> k a (h d)", k=P)[:, :, cols], src[:, 0:4, :]).then_inc(kv_out, 16)
                    sp.dma_start(o[ds_][0].rearrange("b t h d -> (b t) (h d)")[:, cols], src[:, 4, :]).then_inc(kv_out, 16)
                for b in range(2, NS):
                    hold(sp, s.sp_passed, kc_ready, NS * p + b + 1)
                    sp.dma_start(mem.ck[:, b % 2, :, :], ck(b, p)).then_inc(ck_in[b % 2], 16)
                hold(sp, s.sp_passed, pv_done, NI * p + AT[0] + 1)
                for b in range(4):
                    sp.dma_start(mem.cv[:, b, :, :], cv(b + 4, p)).then_inc(cv_in, 16)
                hold(sp, s.sp_passed, kv_out, 64 * p + 64)

        @block.gpsimd
        def _(pool):
            norm.pool(pool)
            c = Chain(pool, cchain)
            c.link(pool.memset(mem.smask[:, :, :], 1.0))
            for e in range(2):
                v = mem.smask[:, e, :].rearrange("p (b t) -> p b t", b=NS)
                c.link(pool.affine_select(out=v, in_=v, compare_op=ALU.is_ge, fill=0.0, base=128 * e, pattern=[[-32, NS], [0, TS]], channel_multiplier=1))
                c.link(pool.affine_select(out=v, in_=v, compare_op=ALU.is_ge, fill=0.0, base=31 - 128 * e, pattern=[[32, NS], [0, TS]], channel_multiplier=-1))
            pool.sem_inc(consts, 1)
            split_tiles(pool, mem, s, 4 * PAIRS)

        @block.tensor
        def _(pe):
            norm.tensor(pe)
            pe.sem_inc(s.tile_done, 2)
            with pe.Fori(0, PAIRS) as p:
                pe.wait_ge(pair_done, p + 1)
                for u in range(3):
                    pe.wait_ge(s.w_split, 4 * p + u + 3)
                    if u == 2:
                        pe.wait_ge(q_ready, 2 * p + 2)
                    product(pe, mem, ps[:, 3 * (u % 2):3 * (u % 2) + 3, :], u % 2, mem.xs, norm.lo_done if u == 0 else None).then_inc(qkv_done, 1)
                    pe.wait_ge(qkv_done, 3 * p + u + 1)
                    pe.sem_inc(s.tile_done, 1)
                pe.wait_ge(k_ready, p + 1)
                for i in range(5):
                    last = pe.transpose(flat[:, 3 * 512 + i * P:3 * 512 + (i + 1) * P], mem.kT[:, (4 + i) * P:(5 + i) * P], mem.ident[:, :])
                last.then_inc(kt_done, 1)
                pe.wait_ge(v_ready, p + 1)
                for i in range(9):
                    last = pe.transpose(flat[:, 5 * 512 + i * P:5 * 512 + (i + 1) * P], mem.ofm[:, i * P:(i + 1) * P], mem.ident[:, :])
                last.then_inc(vt_done, 1)
                pe.wait_ge(vtm_ready, p + 1)
                pe.wait_ge(kout_ready, p + 1)

                in_bank7 = []

                def free7():
                    if in_bank7:
                        what, i = in_bank7[-1]
                        pe.wait_ge(*((ot_ready, 8 * p + i + 1) if what == "back" else (kc_ready, NS * p + i + 3)))

                def cached(b):
                    pe.wait_ge(ck_in[b % 2], 16 * (4 * p + b // 2) + 16)
                    free7()
                    for a in range(4):
                        last = pe.transpose(ps[:, 7, a * P:(a + 1) * P], mem.ck[:, b % 2, a, :], mem.ident[:, :])
                    last.then_inc(kc_done, 1)
                    in_bank7.append(("cached", b))

                def scores(n):
                    what, i, h = ITEMS[n]
                    k0, nk, w = keys_of(n)
                    if n >= 2:
                        pe.wait_ge(sm_ready, NI * p + n - 1)
                    at = 1024 * (n % 2)
                    if what == "band":
                        for lo in range(0, w, 512):
                            hi = min(w, lo + 512)
                            last = pe.matmul(flat[:, at + lo:at + hi], mem.qz[:, h, i * P:(i + 1) * P], mem.kT[:, k0 * P + lo:k0 * P + hi], start=True, stop=True)
                    else:
                        pe.wait_ge(qs_ready, p + 1)
                        for b in range(4):
                            m = 4 * i + b
                            pe.wait_ge(kc_ready, NS * p + m + 3)
                            rows, q = slice(32 * b, 32 * b + 32), mem.qs[:, m, :]
                            pe.matmul(flat[rows, at:at + CACHE], q, mem.kc[:, b, :], start=True, stop=True)
                            last = pe.matmul(flat[rows, at + CACHE:at + SPAN], q, mem.kT[:, TP + TS * m:TP + TS * m + TS], start=True, stop=True)
                    last.then_inc(sc_done, 1)

                def turn(n):
                    what, e, _ = ITEMS[n]
                    pe.wait_ge(ex_ready, NI * p + n + 1)
                    if what == "streams":
                        pe.wait_ge(spr_ready, 2 * p + e + 1)
                    if n >= 1:
                        pe.wait_ge(pt_ready, NI * p + n)
                    for j in range(keys_of(n)[1]):
                        last = pe.transpose(flat[:, 2048 + j * P:2048 + (j + 1) * P], mem.pr[:, n % 2, j * P:(j + 1) * P], mem.ident[:, :])
                    last.then_inc(pt_done, 1)

                def values(n):
                    what, i, h = ITEMS[n]
                    k0, nk, _ = keys_of(n)
                    pe.wait_ge(pt_ready, NI * p + n + 1)
                    if n >= 1:
                        pe.wait_ge(on_ready, NI * p + n)
                    if what == "band":
                        for j in range(nk):
                            last = pe.matmul(ps[:, 6, 0:64], mem.pt[:, n % 2, j * P:(j + 1) * P], mem.vtm[:, k0 + j, h * 64:(h + 1) * 64],
                                             start=(j == 0), stop=(j == nk - 1))
                    else:
                        pe.wait_ge(cv_in, 128 * p + 64 * (i + 1))
                        for b in range(4):
                            out = ps[:, 6, 32 * b:32 * b + 32]
                            for j in range(4):
                                pe.matmul(out, mem.cv[:, b, j, :], mem.pt[:, n % 2, j * P + 32 * b:j * P + 32 * b + 32], start=(j == 0), stop=False)
                            last = pe.matmul(out, mem.vtm[:, 8, :], mem.pt[:, n % 2, 512 + 32 * b:512 + 32 * b + 32], start=False, stop=True)
                    last.then_inc(pv_done, 1)

                def back(n):
                    i = ITEMS[n][1]
                    pe.wait_ge(on_ready, NI * p + n + 1)
                    free7()
                    pe.transpose(ps[:, 7, 0:P], mem.otm[:, i % 2, :], mem.ident[:, :]).then_inc(ot_done, 1)
                    in_bank7.append(("back", i))

                for n in range(NI + 3):
                    if n < NI:
                        scores(n)
                    if n in CACHED:
                        cached(CACHED[n])
                    if 2 <= n < NI + 2:
                        values(n - 2)
                    if 1 <= n <= NI:
                        turn(n - 1)
                    if n >= 3 and ITEMS[n - 3][2] == 1:
                        back(n - 3)
                pe.wait_ge(ot_ready, 8 * p + 8)
                pe.wait_ge(s.w_split, 4 * p + 6)
                pe.wait_ge(ol_ready, p + 1)
                for k in range(KB):
                    pe.wait_ge(proj_free, KB * p + k + 1)
                    outer(pe, mem, ps[:, 3 * (k % 2):3 * (k % 2) + 3, :], [(1, mem.osp)], k).then_inc(proj_done, 1)
                pe.wait_ge(proj_done, KB * p + KB)
                pe.sem_inc(s.tile_done, 1)

        @block.scalar
        def _(act):
            act.sem_inc(kc_ready, 2)
            norm.scalar(act)
            norm.scalar_split(act)
            act.wait_ge(consts, 2)
            with act.Fori(0, PAIRS) as p:
                act.wait_ge(qkv_done, 3 * p + 1)
                for h, (lo, hi) in enumerate(halves):
                    act.mul(by3(mem.qz[lo:hi, h, :]), ps[lo:hi, 0:3, 0:CW], HD ** -0.5).then_inc(q_ready, 1)
                act.wait_ge(qkv_done, 3 * p + 3)
                act.copy(by3(mem.ofm[:, :]), ps[:, 0:3, 0:CW]).then_inc(v_ready, 1)
                act.wait_ge(q_ready, 2 * p + 2)
                act.copy(mem.qs[:, :, :].rearrange("p b (h t) -> p b h t", h=2),
                         mem.qz[:, :, TP:T].rearrange("p h (b t) -> p b h t", b=NS)).then_inc(qs_ready, 1)
                act.wait_ge(vt_done, p + 1)
                act.copy(mem.vtm[:, :, :].rearrange("p i c -> p (i c)"), flat[:, 2560:2560 + 9 * P]).then_inc(vtm_ready, 1)

                def expo(n):
                    w = keys_of(n)[2]
                    act.wait_ge(nm_ready, NI * p + n + 1)
                    act.activation(mem.pr[:, n % 2, 0:w], mem.pr[:, n % 2, 0:w], ACT.Exp, bias=mem.nm[:, n:n + 1], accum_out=mem.rsum[:, n:n + 1]).then_inc(ex_ready, 1)

                def copy_pt(n):
                    w = keys_of(n)[1] * P
                    act.wait_ge(pt_done, NI * p + n + 1)
                    if n >= 2:
                        act.wait_ge(pv_done, NI * p + n - 1)
                    act.copy(mem.pt[:, n % 2, 0:w], flat[:, 2048:2048 + w]).then_inc(pt_ready, 1)

                def copy_cached(b):
                    act.wait_ge(kc_done, NS * p + b + 1)
                    if b == 0:
                        act.wait_ge(kv_out, 64 * p + 64)
                    if b == 4:
                        act.wait_ge(sc_done, NI * p + AT[0] + 1)
                    act.copy(mem.kc[:, b % 4, :], ps[:, 7, :]).then_inc(kc_ready, 1)

                for n in range(NI + 1):
                    if n >= 2:
                        copy_pt(n - 2)
                    if n in CACHED:
                        copy_cached(CACHED[n])
                    if n < NI:
                        expo(n)
                copy_pt(NI - 1)
                act.wait_ge(on_ready, NI * p + NI)
                act.wait_ge(ot_ready, 8 * p + 8)
                act.copy(mem.osp[:, 0, :], mem.ofm[:, :]).then_inc(oh_ready, 1)

        @block.vector
        def _(dve):
            dve.sem_inc(pair_done, 1)
            dve.sem_inc(proj_free, 2)
            norm.vector(dve)
            norm.vector_split(dve)
            dve.wait_ge(norm.lo_done, KB)
            dve.memset(mem.qz[:, :, :], 0.0).then_inc(consts, 1)
            dve.wait_ge(consts, 2)
            with dve.Fori(0, PAIRS) as p:
                chain = Chain(dve, dve_chain, p, ATTENTION_LINKS)
                dve.wait_ge(qkv_done, 3 * p + 2)
                dve.tensor_copy(by3(mem.kT[:, :]), ps[:, 3:6, 0:CW]).then_inc(k_ready, 1)
                dve.wait_ge(kt_done, p + 1)
                dve.tensor_copy(mem.kout[:, :, :].rearrange("p i c -> p (i c)"), flat[:, 1536:1536 + 640]).then_inc(kout_ready, 1)
                dve.wait_ge(bias_in, 32 * p + 32)
                dve.wait_ge(bs_in, 128 * p + 128)
                for h in range(2):
                    chain.link(dve.memset(mem.bt[0:64, h, BAND - 64:BAND], NEG))
                    chain.link(dve.memset(mem.bt[64:128, h, 0:64], NEG))

                def biased(n):
                    what, _, h = ITEMS[n]
                    w, at = keys_of(n)[2], 1024 * (n % 2)
                    bias = mem.bt[:, h, BAND - w:BAND] if what == "band" else mem.bs[:, :]
                    dve.wait_ge(sc_done, NI * p + n + 1)
                    if n >= 2:
                        dve.wait_ge(pt_done, NI * p + n - 1)
                    dve.sem_inc(s.dve_passed, 1)
                    dve.tensor_tensor_reduce(mem.pr[:, n % 2, 0:w], flat[:, at:at + w], bias, 1.0, -3e38,
                                             ALU.add, ALU.max, mem.mx[:, n:n + 1]).then_inc(sm_ready, 1)
                    dve.wait_ge(sm_ready, NI * p + n + 1)
                    dve.tensor_scalar(mem.nm[:, n:n + 1], mem.mx[:, n:n + 1], -1.0, None, ALU.mult).then_inc(nm_ready, 1)

                def divided(n):
                    e = ITEMS[n][1]
                    dve.wait_ge(ex_ready, NI * p + n + 1)
                    rinv, pr = mem.rinv[:, n:n + 1], mem.pr[:, n % 2, :]
                    chain.link(dve.reciprocal(rinv, mem.rsum[:, n:n + 1]))
                    dve.tensor_scalar(pr[:, 0:CACHE], pr[:, 0:CACHE], rinv, None, ALU.mult)
                    mask = mem.smask[:, e, :].rearrange("p (b t) -> p b t", b=NS)
                    chain.link(dve.scalar_tensor_tensor(pr[:, SPAN:BAND].rearrange("p (b t) -> p b t", b=NS - 1), spread(pr[:, CACHE:SPAN], NS - 1),
                                                        rinv, mask[:, 1:NS, :], ALU.mult, ALU.mult))
                    dve.scalar_tensor_tensor(pr[:, CACHE:SPAN], pr[:, CACHE:SPAN], rinv, mask[:, 0, :], ALU.mult, ALU.mult).then_inc(spr_ready, 1)

                def scaled(n):
                    what, i, h = ITEMS[n]
                    if what == "streams":
                        dve.wait_ge(pv_done, NI * p + n + 1)
                        for h, (lo, hi) in enumerate(halves):
                            ins = dve.tensor_copy(mem.ofm[lo:hi, TP + 64 * i:TP + 64 * i + 64].rearrange("p (b t) -> p b t", b=4),
                                                  ps[lo:hi, 6, 0:P].rearrange("p (b h t) -> p b h t", b=4, h=2)[:, :, h, :])
                        ins.then_inc(on_ready, 1)
                        return
                    dve.wait_ge(ex_ready, NI * p + n + 1)
                    chain.link(dve.reciprocal(mem.rinv[:, n:n + 1], mem.rsum[:, n:n + 1]))
                    dve.wait_ge(pv_done, NI * p + n + 1)
                    if i >= 2 and h == 0:
                        dve.wait_ge(ot_done, 8 * p + i - 1)
                    dve.tensor_scalar(mem.otm[:, i % 2, h * 64:(h + 1) * 64], ps[:, 6, 0:64], mem.rinv[:, n:n + 1], None, ALU.mult).then_inc(on_ready, 1)

                def home(n):
                    i = ITEMS[n][1]
                    dve.wait_ge(ot_done, 8 * p + i + 1)
                    dve.tensor_copy(mem.ofm[:, i * P:(i + 1) * P], ps[:, 7, 0:P]).then_inc(ot_ready, 1)

                for n in range(NI + 3):
                    if n < NI:
                        biased(n)
                    if 1 <= n <= NI and ITEMS[n - 1][0] == "streams":
                        divided(n - 1)
                    if 2 <= n < NI + 2:
                        scaled(n - 2)
                    if n >= 3 and ITEMS[n - 3][2] == 1:
                        home(n - 3)
                dve.wait_ge(oh_ready, p + 1)
                dve.tensor_tensor(mem.osp[:, 1, :], mem.ofm[:, :], mem.osp[:, 0, :].bitcast(F32), ALU.subtract).then_inc(ol_ready, 1)
                for k in range(KB):
                    dve.wait_ge(proj_done, KB * p + k + 1)
                    dve.tensor_tensor(by3(mem.H[:, k, :]), ps[:, 3 * (k % 2):3 * (k % 2) + 3, 0:CW], by3(mem.H[:, k, :]), ALU.add).then_inc(proj_free, 1)
                dve.wait_ge(proj_free, KB * p + KB + 2)
                dve.wait_ge(kv_out, 64 * p + 64)
                dve.sem_inc(pair_done, 1)
                chain.close("attention, VectorE")


OUTPUTS = [
    ("y_p", (1, TP, D)), ("y_s", (NS, TS, D)), ("wkv_p", (1, 1, 16, HD, HD)), ("shift_p", (1, 1, D)),
    ("k_p", (1, 1, 512, 16, HD)), ("v_p", (1, 1, 512, 16, HD)), ("wkv_s", (1, NS, 16, HD, HD)),
    ("shift_s", (1, NS, D)), ("k_s", (1, NS, TS, 16, HD)), ("v_s", (1, NS, TS, 16, HD)),
]
INPUTS = [
    "x_prompt", "x_sample", "state_wkv", "state_shift", "cache_k", "cache_v", "norm_mix", "norm_ffn", "norm_final",
    "rwkv_mu", "rwkv_w_rkv", "rwkv_w_out", "rwkv_decay_w0", "rwkv_decay_w1", "rwkv_decay_w2", "rwkv_iclr_a0",
    "rwkv_iclr_a1", "rwkv_iclr_a2", "rwkv_gate_g1", "rwkv_gate_g2", "rwkv_k_k", "rwkv_k_a", "rwkv_r_k",
    "rwkv_lnx_w", "rwkv_lnx_b", "attn_w_qkv", "attn_w_out", "attn_rel_bias", "ffn_w_gu", "ffn_w_down",
]


def build(nc, t, o):
    mem = Memory()
    with ExitStack() as ctx:
        def sb(stack, name, shape, dt=F32):
            return stack.enter_context(nc.sbuf_tensor(name, shape, dt))

        mem.ident = sb(ctx, "ident", [P, P])
        mem.ones = sb(ctx, "ones", [P, P])
        mem.headones = sb(ctx, "headones", [P, P])
        mem.vec = sb(ctx, "vec", [P, KB, NROW])
        mem.omu = sb(ctx, "omu", [P, KB, 6])
        mem.ps = ctx.enter_context(nc.psum_tensor("ps", [P, 8, 512], F32))
        mem.h_dram = nc.dram_tensor("h_scratch", (P, KB * T), F32, kind="Internal").ap()
        mem.gated_dram = nc.dram_tensor("gated_scratch", (D, T), F32, kind="Internal").ap()
        mem.rkv_dram = nc.dram_tensor("rkv_scratch", (3, D, T), F32, kind="Internal").ap()
        mem.ext_dram = nc.dram_tensor("bias_scratch", (16, 768), F32, kind="Internal").ap()
        mem.tab_dram = nc.dram_tensor("bias_table", (16, P, BAND), F32, kind="Internal").ap()

        setup_and_rwkv(nc, t, mem, o, sb)
        with ExitStack() as later:
            mem.H = sb(later, "H", [P, KB, T])
            mem.xs = sb(later, "xs", [P, 2, KB, T], F32R)

            def ffn(layer):
                with ExitStack() as stack:
                    mem.stage3 = sb(stack, f"stage3_{layer}", [P, 3, 1024])
                    mem.wsplit3 = sb(stack, f"wsplit3_{layer}", [P, 3, 2, 1024], F32R)
                    mem.hid = sb(stack, f"hid{layer}", [P, 2, 2, T], F32R)
                    mem.tt = sb(stack, f"tt{layer}", [P, 2, T])
                    mem.sg, mem.hf = mem.tt[:, 0, :], mem.tt[:, 1, :]
                    norm_memory(stack, mem, sb, f"ffn{layer}")
                    ffn_phase(nc, t, mem, layer)

            with ExitStack() as stack:
                ring(stack, mem, sb, "project")
                mem.tt = sb(stack, "gated", [P, 2, T])
                project_phase(nc, t, mem)
            ffn(0)
            with ExitStack() as att:
                ring(att, mem, sb, "attention")
                attention_memory(att, mem, sb)
                attention_phase(nc, t, mem, o)
            ffn(1)
            with ExitStack() as stack:
                norm_memory(stack, mem, sb, "final")
                mem.yrow = sb(stack, "yrow", [P, 2, D])
                mem.sq = sb(stack, "sq_final", [P, 2, T])
                norm_phase(nc, mem, o, "final", "out")


def ring(stack, mem, sb, name):
    mem.stage = sb(stack, f"stage_{name}", [P, 2, 1024])
    mem.wsplit = sb(stack, f"wsplit_{name}", [P, 2, 2, 1024], F32R)


def norm_memory(stack, mem, sb, name):
    mem.total = sb(stack, f"total_{name}", [P, T])
    mem.sel9 = sb(stack, f"sel9_{name}", [P, T])
    mem.rms = sb(stack, f"rms_{name}", [P, 9])
    mem.rmst = sb(stack, f"rmst_{name}", [P, P])


def setup_and_rwkv(nc, t, mem, o, sb):
    with ExitStack() as rwkv:
        mem.lora_wa = sb(rwkv, "lora_wa", [P, T])
        mem.lora_g = sb(rwkv, "lora_g", [P, T])
        mem.lora_g2 = sb(rwkv, "lora_g2", [P, T])
        with ExitStack() as before:
            mem.xnp = sb(before, "xnp", [P, KB, TPAD])
            with ExitStack() as first:
                mem.H = sb(first, "H0", [P, KB, T])
                mem.xrow = sb(first, "xrow", [P, 2, D])
                mem.rows = sb(first, "rows", [NROW, D])
                mem.sq = sb(first, "sq", [P, 2, T])
                norm_memory(first, mem, sb, "mix0")
                mem.shiftcol = sb(first, "shiftcol", [P, KB, 1 + NS])
                mem.shiftrow = sb(first, "shiftrow", [1 + NS, D])
                setup_phase(nc, t, mem)
                norm_phase(nc, mem, o, "mix0", "padded")
            with ExitStack() as mix:
                ring(mix, mem, sb, "mix")
                mem.mixed = sb(mix, "mixed", [P, 2, KB, T], F32R)
                mem.mt1 = sb(mix, "mt1", [P, 2, TPAD])
                mem.mt2 = sb(mix, "mt2", [P, 2, TPAD])
                mem.rkvout = (mem.lora_g, mem.lora_g2)
                mix_phase(nc, t, mem)
        with ExitStack() as scan:
            mem.arena = sb(scan, "arena", [P, (nc.sbuf_bytes_remaining - 64) // 4])
            recurrence_phase(nc, t, mem, o)


def attention_memory(att, mem, sb):
    mem.otm = sb(att, "otm", [P, 2, P])
    mem.qz = sb(att, "qz", [P, 2, T])
    mem.kT = sb(att, "kT", [P, T])
    mem.vtm = sb(att, "vtm", [P, 9, P])
    mem.ofm = sb(att, "ofm", [P, T])
    mem.sel9 = mem.ofm
    mem.rms = sb(att, "rms_a", [P, 9])
    mem.rmst = mem.otm[:, 0, :]
    mem.osp = sb(att, "osp", [P, 2, T], F32R)
    mem.bt = sb(att, "bt", [P, 2, BAND])
    mem.bs = sb(att, "bs", [P, SPAN])
    mem.pr = sb(att, "pr", [P, 2, BAND])
    mem.pt = sb(att, "pt", [P, 2, BAND])
    mem.qs = sb(att, "qs", [P, NS, 32])
    mem.kc = sb(att, "kc", [P, 4, CACHE])
    mem.smask = sb(att, "smask", [P, 2, P])
    mem.mx, mem.nm, mem.rsum, mem.rinv = (sb(att, x, [P, 18]) for x in ("mx", "nm", "rsum", "rinv"))
    mem.cv = sb(att, "cv", [P, 4, 4, P])
    mem.ck = sb(att, "ck", [P, 2, 4, P])
    mem.kout = mem.kc[:, :, :].rearrange("p a c -> p (a c)")[:, 0:640].rearrange("p (i c) -> p i c", i=5)


def kernel(**inputs):
    import concourse.bacc as bacc
    from concourse.bass_utils import run_bass_kernel_spmd

    nc = bacc.Bacc("TRN2", target_bir_lowering=False, num_devices=1)
    arrays = {f"in_{n}": np.ascontiguousarray(inputs[n]) for n in INPUTS}
    t = {n: nc.dram_tensor(f"in_{n}", arrays[f"in_{n}"].shape, F32, kind="ExternalInput").ap() for n in INPUTS}
    o = {n: nc.dram_tensor(f"out_{n}", shape, F32, kind="ExternalOutput").ap() for n, shape in OUTPUTS}
    build(nc, t, o)
    got = run_bass_kernel_spmd(nc, [arrays], core_ids=[0]).results[0]
    return tuple(got[f"out_{n}"] for n, _ in OUTPUTS)
```
